# Optimizing a Trainium2 kernel written in Bass

```python
import math
import jax, jax.numpy as jnp
from jax import lax
import numpy as np

D_MODEL = 1024
BATCH = 1
SEQ = 256
DEPTH = 1

HEAD_DIM = 64
SWA_HEADS = 8
SWA_KV_HEADS = 2
SWA_WINDOW = 128
SWA_BLOCK = 128
RNN_WIDTH = D_MODEL
RNN_BLOCKS = 16
RNN_BLOCK_WIDTH = RNN_WIDTH // RNN_BLOCKS
RNN_CONV = 4
RGLRU_C = 8.0
MOBA_HEADS = 8
MOBA_BLOCK = 256
MOBA_TOPK = 3
NUM_BUCKETS = 32
MAX_DISTANCE = 2048
D_FF = 2816
FFN_CONV = 3

RMS_EPS = 1e-6
NEG_INF = -1e30
N_BRANCH = 3
SWA_Q = SWA_HEADS * HEAD_DIM
SWA_KV = SWA_KV_HEADS * HEAD_DIM
MOBA_W = MOBA_HEADS * HEAD_DIM
IN_WIDTHS = (SWA_Q, SWA_KV, SWA_KV, RNN_WIDTH, RNN_WIDTH, MOBA_W, MOBA_W, MOBA_W, N_BRANCH * D_MODEL)
IN_OFFSETS = tuple(sum(IN_WIDTHS[:i + 1]) for i in range(len(IN_WIDTHS) - 1))
D_IN = sum(IN_WIDTHS)
D_MIX = SWA_Q + RNN_WIDTH + MOBA_W


def rms_norm(x, gain):
    xf = x.astype(jnp.float32)
    y = xf * lax.rsqrt(jnp.mean(xf * xf, axis=-1, keepdims=True) + RMS_EPS)
    return (y * gain.astype(jnp.float32)).astype(x.dtype)

def t5_bucket(dist):
    dist = jnp.maximum(dist, 0)
    max_exact = NUM_BUCKETS // 2
    log_ratio = jnp.log(jnp.maximum(dist, 1).astype(jnp.float32) / max_exact) / math.log(MAX_DISTANCE / max_exact)
    large = max_exact + (log_ratio * (NUM_BUCKETS - max_exact)).astype(jnp.int32)
    large = jnp.minimum(large, NUM_BUCKETS - 1)
    return jnp.where(dist < max_exact, dist, large)

def causal_dwconv(x, w, b):
    k_width = w.shape[0]
    s = x.shape[1]
    xp = jnp.pad(x, ((0, 0), (k_width - 1, 0), (0, 0)))
    return sum(xp[:, k:k + s] * w[k] for k in range(k_width)) + b

def swa_attention(q, k, v, sinks, bias_a):
    b_sz, s_len = q.shape[:2]
    L = SWA_BLOCK
    nblk = s_len // L
    grp = SWA_HEADS // SWA_KV_HEADS
    qb = q.reshape(b_sz, nblk, L, SWA_KV_HEADS, grp, HEAD_DIM)

    def band(t):
        tp = jnp.pad(t, ((0, 0), (L, 0), (0, 0), (0, 0))).reshape(b_sz, nblk + 1, L, SWA_KV_HEADS, HEAD_DIM)
        return jnp.concatenate([tp[:, :-1], tp[:, 1:]], axis=2)

    kb, vb = band(k), band(v)
    s = jnp.einsum('bnqkgd,bnskd->bnkgqs', qb, kb).astype(jnp.float32) * (HEAD_DIM ** -0.5)
    qi = jnp.arange(L)
    sj = jnp.arange(2 * L)
    diff = qi[:, None] + L - sj[None, :]
    bias = bias_a[t5_bucket(diff)].astype(jnp.float32).transpose(2, 0, 1).reshape(SWA_KV_HEADS, grp, L, 2 * L)
    key_pos = jnp.arange(nblk)[:, None] * L - L + sj[None, :]
    valid = ((diff >= 0) & (diff < SWA_WINDOW))[None] & (key_pos >= 0)[:, None, :]
    s = jnp.where(valid[None, :, None, None], s + bias, NEG_INF)
    sink = sinks.astype(jnp.float32).reshape(SWA_KV_HEADS, grp)[:, :, None, None]
    m = jnp.maximum(jnp.max(s, axis=-1, keepdims=True), sink)
    p = jnp.exp(s - m)
    p = p / (jnp.sum(p, axis=-1, keepdims=True) + jnp.exp(sink - m))
    o = jnp.einsum('bnkgqs,bnskd->bnqkgd', p.astype(v.dtype), vb)
    return o.reshape(b_sz, s_len, SWA_Q)

def rg_lru(x, ga_w, ga_b, gx_w, gx_b, lam):
    b_sz, s_len, width = x.shape
    xb = x.reshape(b_sz, s_len, RNN_BLOCKS, RNN_BLOCK_WIDTH)
    r = jax.nn.sigmoid(jnp.einsum('bsnc,ncd->bsnd', xb, ga_w).reshape(b_sz, s_len, width) + ga_b)
    i = jax.nn.sigmoid(jnp.einsum('bsnc,ncd->bsnd', xb, gx_w).reshape(b_sz, s_len, width) + gx_b)
    log_a = -RGLRU_C * r.astype(jnp.float32) * jax.nn.softplus(-lam.astype(jnp.float32))
    a = jnp.exp(log_a)
    mult = jnp.sqrt(-jnp.expm1(2.0 * log_a))
    mult = jnp.where((jnp.arange(s_len) == 0)[None, :, None], 1.0, mult)
    u = mult * (i * x).astype(jnp.float32)

    def combine(left, right):
        a_l, b_l = left
        a_r, b_r = right
        return (a_l * a_r, a_r * b_l + b_r)

    _, h = lax.associative_scan(combine, (a, u), axis=1)
    return h.astype(x.dtype)

def moba_attention(q, k, v, bias_c):
    b_sz, s_len = q.shape[:2]
    MB = MOBA_BLOCK
    nb = -(-s_len // MB)
    s_pad = nb * MB
    pad = ((0, 0), (0, s_pad - s_len), (0, 0), (0, 0))
    q, k, v = jnp.pad(q, pad), jnp.pad(k, pad), jnp.pad(v, pad)
    topk = min(MOBA_TOPK, nb)
    kb = k.reshape(b_sz, nb, MB, MOBA_HEADS, HEAD_DIM)
    vb = v.reshape(b_sz, nb, MB, MOBA_HEADS, HEAD_DIM)
    k_mean = jnp.mean(kb.astype(jnp.float32), axis=2).astype(k.dtype)
    k_bh = kb.transpose(0, 3, 1, 2, 4)
    v_bh = vb.transpose(0, 3, 1, 2, 4)
    q_chunks = q.reshape(b_sz, nb, MB, MOBA_HEADS, HEAD_DIM).transpose(1, 0, 2, 3, 4)
    k_own = kb.transpose(1, 0, 2, 3, 4)
    v_own = vb.transpose(1, 0, 2, 3, 4)
    pos = jnp.arange(MB)
    own_diff = pos[:, None] - pos[None, :]
    own_mask = own_diff >= 0
    own_bias = bias_c[t5_bucket(own_diff)].astype(jnp.float32).transpose(0, 2, 1)
    b_ix = jnp.arange(b_sz)[:, None, None, None]
    h_ix = jnp.arange(MOBA_HEADS)[None, None, :, None]
    blk_ids = jnp.arange(nb)
    scale = HEAD_DIM ** -0.5

    def one_block(args):
        n, q_c, k_c, v_c = args
        gate = jnp.einsum('bqhd,bmhd->bqhm', q_c, k_mean).astype(jnp.float32)
        gate = jnp.where(blk_ids < n, gate, NEG_INF)
        _, sel = lax.top_k(gate, topk)
        sel_valid = sel < n
        k_sel = k_bh[b_ix, h_ix, sel]
        v_sel = v_bh[b_ix, h_ix, sel]
        s_sel = jnp.einsum('bqhd,bqhtsd->bqhts', q_c, k_sel).astype(jnp.float32) * scale
        dist = (n * MB + pos)[None, :, None, None, None] - (sel[..., None] * MB + pos)
        s_sel = s_sel + bias_c[t5_bucket(dist), h_ix[..., None]].astype(jnp.float32)
        s_sel = jnp.where(sel_valid[..., None], s_sel, NEG_INF).reshape(b_sz, MB, MOBA_HEADS, topk * MB)
        s_own = jnp.einsum('bqhd,bshd->bqhs', q_c, k_c).astype(jnp.float32) * scale + own_bias
        s_own = jnp.where(own_mask[:, None, :], s_own, NEG_INF)
        p = jax.nn.softmax(jnp.concatenate([s_sel, s_own], axis=-1), axis=-1).astype(v.dtype)
        p_sel = p[..., :topk * MB].reshape(b_sz, MB, MOBA_HEADS, topk, MB)
        p_own = p[..., topk * MB:]
        return jnp.einsum('bqhts,bqhtsd->bqhd', p_sel, v_sel) + jnp.einsum('bqhs,bshd->bqhd', p_own, v_c)

    o = lax.map(one_block, (blk_ids, q_chunks, k_own, v_own))
    return o.transpose(1, 0, 2, 3, 4).reshape(b_sz, s_pad, MOBA_W)[:, :s_len]

def first_inputs(seed: int = 0) -> dict:
    key = jax.random.key(seed)
    ks = jax.random.split(key, 32)
    f32 = jnp.float32

    def nrm(k, shape, fan_in, scale=1.0):
        return jax.random.normal(k, shape, f32) * (scale * fan_in ** -0.5)

    def gain(k, shape):
        return 1.0 + 0.05 * jax.random.normal(k, shape, f32)

    def small(k, shape, scale=0.02):
        return scale * jax.random.normal(k, shape, f32)

    a_init = jax.random.uniform(ks[16], (DEPTH, RNN_WIDTH), f32, 0.9, 0.999)
    w_branch = jnp.concatenate([
        nrm(ks[20], (DEPTH, SWA_Q, D_MODEL), SWA_Q),
        nrm(ks[21], (DEPTH, RNN_WIDTH, D_MODEL), RNN_WIDTH),
        nrm(ks[22], (DEPTH, MOBA_W, D_MODEL), MOBA_W)], axis=1)
    return {
        'x': jax.random.normal(ks[0], (BATCH, SEQ, D_MODEL), f32),
        'c': jax.random.normal(ks[1], (BATCH, D_MODEL), f32),
        'w_mod': nrm(ks[2], (DEPTH, D_MODEL, 6 * D_MODEL), D_MODEL, 0.5),
        'b_mod': small(ks[3], (DEPTH, 6 * D_MODEL)),
        'norm_mix': gain(ks[4], (DEPTH, D_MODEL)),
        'norm_ffn': gain(ks[5], (DEPTH, D_MODEL)),
        'w_in': nrm(ks[6], (DEPTH, D_MODEL, D_IN), D_MODEL),
        'qnorm_a': gain(ks[7], (DEPTH, HEAD_DIM)),
        'knorm_a': gain(ks[8], (DEPTH, HEAD_DIM)),
        'sinks': small(ks[9], (DEPTH, SWA_HEADS), 0.5),
        'rnn_conv_w': nrm(ks[10], (DEPTH, RNN_CONV, RNN_WIDTH), RNN_CONV),
        'rnn_conv_b': small(ks[11], (DEPTH, RNN_WIDTH)),
        'rnn_gate_a_w': nrm(ks[12], (DEPTH, RNN_BLOCKS, RNN_BLOCK_WIDTH, RNN_BLOCK_WIDTH), RNN_BLOCK_WIDTH),
        'rnn_gate_a_b': small(ks[13], (DEPTH, RNN_WIDTH)),
        'rnn_gate_x_w': nrm(ks[14], (DEPTH, RNN_BLOCKS, RNN_BLOCK_WIDTH, RNN_BLOCK_WIDTH), RNN_BLOCK_WIDTH),
        'rnn_gate_x_b': small(ks[15], (DEPTH, RNN_WIDTH)),
        'rnn_lambda': jnp.log(a_init) - jnp.log1p(-a_init),
        'qnorm_c': gain(ks[17], (DEPTH, HEAD_DIM)),
        'knorm_c': gain(ks[18], (DEPTH, HEAD_DIM)),
        'rel_bias': small(ks[19], (NUM_BUCKETS, SWA_HEADS + MOBA_HEADS), 0.5),
        'w_branch': w_branch,
        'w_out': nrm(ks[23], (DEPTH, D_MODEL, D_MODEL), D_MODEL),
        'w_up': nrm(ks[24], (DEPTH, D_MODEL, 2 * D_FF), D_MODEL),
        'ffn_conv_w': nrm(ks[25], (DEPTH, FFN_CONV, 2 * D_FF), FFN_CONV),
        'ffn_conv_b': small(ks[26], (DEPTH, 2 * D_FF)),
        'w_down': nrm(ks[27], (DEPTH, D_FF, D_MODEL), D_FF),
    }

def first_block(x, c, w_mod, b_mod, norm_mix, norm_ffn, w_in, qnorm_a, knorm_a, sinks,
              rnn_conv_w, rnn_conv_b, rnn_gate_a_w, rnn_gate_a_b, rnn_gate_x_w, rnn_gate_x_b,
              rnn_lambda, qnorm_c, knorm_c, rel_bias, w_branch, w_out, w_up, ffn_conv_w,
              ffn_conv_b, w_down):
    b_sz, s_len, _ = x.shape
    c_act = jax.nn.silu(c)
    bias_a = rel_bias[:, :SWA_HEADS]
    bias_c = rel_bias[:, SWA_HEADS:]
    for l in range(DEPTH):
        mod = (c_act @ w_mod[l] + b_mod[l])[:, None, :]
        shift_m, scale_m, gate_m, shift_f, scale_f, gate_f = jnp.split(mod, 6, axis=-1)

        h = rms_norm(x, norm_mix[l]) * (1.0 + scale_m) + shift_m
        z = h @ w_in[l]
        qa, ka, va, xr, yr, qc, kc, vc, g_logits = jnp.split(z, IN_OFFSETS, axis=-1)

        qa = rms_norm(qa.reshape(b_sz, s_len, SWA_HEADS, HEAD_DIM), qnorm_a[l])
        ka = rms_norm(ka.reshape(b_sz, s_len, SWA_KV_HEADS, HEAD_DIM), knorm_a[l])
        va = va.reshape(b_sz, s_len, SWA_KV_HEADS, HEAD_DIM)
        o_a = swa_attention(qa, ka, va, sinks[l], bias_a)

        xr = causal_dwconv(xr, rnn_conv_w[l], rnn_conv_b[l])
        hr = rg_lru(xr, rnn_gate_a_w[l], rnn_gate_a_b[l], rnn_gate_x_w[l], rnn_gate_x_b[l], rnn_lambda[l])
        o_b = hr * jax.nn.gelu(yr)

        qc = rms_norm(qc.reshape(b_sz, s_len, MOBA_HEADS, HEAD_DIM), qnorm_c[l])
        kc = rms_norm(kc.reshape(b_sz, s_len, MOBA_HEADS, HEAD_DIM), knorm_c[l])
        vc = vc.reshape(b_sz, s_len, MOBA_HEADS, HEAD_DIM)
        o_c = moba_attention(qc, kc, vc, bias_c)

        wb = w_branch[l]
        p_a = o_a @ wb[:SWA_Q]
        p_b = o_b @ wb[SWA_Q:SWA_Q + RNN_WIDTH]
        p_c = o_c @ wb[SWA_Q + RNN_WIDTH:]
        g = jax.nn.sigmoid(g_logits.reshape(b_sz, s_len, N_BRANCH, D_MODEL))
        merged = g[:, :, 0] * p_a + g[:, :, 1] * p_b + g[:, :, 2] * p_c
        x = x + gate_m * (merged @ w_out[l])

        h = rms_norm(x, norm_ffn[l]) * (1.0 + scale_f) + shift_f
        u = causal_dwconv(h @ w_up[l], ffn_conv_w[l], ffn_conv_b[l])
        u_gate, u_val = jnp.split(u, 2, axis=-1)
        x = x + gate_f * ((jax.nn.silu(u_gate) * u_val) @ w_down[l])
    return x


DEPTH_2 = 2

MEM_LEN = 256
CONV_D = D_MODEL
CONV_K = 31
N_HEADS = 8
V_DIM = 2 * HEAD_DIM
QK_D = N_HEADS * 2 * HEAD_DIM
ATTN_D = N_HEADS * V_DIM
Q_BLOCK = 128
N_BUCKETS = 32
MAX_DISTANCE_2 = 128
POOL_WINDOWS = (2, 4, 8, 16)
POOL_GROUPS = len(POOL_WINDOWS)
POOL_D = D_MODEL
POOL_GD = POOL_D // POOL_GROUPS
X_HEADS = 4
X_HEAD_DIM = D_MODEL // X_HEADS
X_D = X_HEADS * X_HEAD_DIM
SPLITS = (2 * CONV_D,
          2 * CONV_D + QK_D,
          2 * CONV_D + 2 * QK_D,
          2 * CONV_D + 2 * QK_D + ATTN_D,
          2 * CONV_D + 2 * QK_D + ATTN_D + POOL_D)
IN_COLS = SPLITS[-1] + N_BRANCH * D_MODEL
LN_EPS = 1e-5
NEG_INF_2 = -1e30


def rms_norm_2(x, g):
    xf = x.astype(jnp.float32)
    y = xf * lax.rsqrt(jnp.mean(xf * xf, axis=-1, keepdims=True) + RMS_EPS)
    return (y * g.astype(jnp.float32)).astype(x.dtype)

def layer_norm(x, g, b):
    xf = x.astype(jnp.float32)
    mu = jnp.mean(xf, axis=-1, keepdims=True)
    xc = xf - mu
    y = xc * lax.rsqrt(jnp.mean(xc * xc, axis=-1, keepdims=True) + LN_EPS)
    return (y * g.astype(jnp.float32) + b.astype(jnp.float32)).astype(x.dtype)

def swiglu(h, w1, w3, w2):
    return (jax.nn.silu(h @ w1) * (h @ w3)) @ w2

def t5_bucket_2(n):
    n = jnp.maximum(n, 0)
    max_exact = N_BUCKETS // 2
    nf = jnp.maximum(n, 1).astype(jnp.float32)
    large = max_exact + (jnp.log(nf / max_exact) / math.log(MAX_DISTANCE_2 / max_exact)
                         * (N_BUCKETS - max_exact)).astype(jnp.int32)
    large = jnp.minimum(large, N_BUCKETS - 1)
    return jnp.where(n < max_exact, n, large)

def conv_branch(u, w_dw, b_dw, ln_g, ln_b, w_pw):
    a, gt = jnp.split(u, 2, axis=-1)
    z = a * jax.nn.sigmoid(gt)
    z = lax.conv_general_dilated(z, w_dw[:, None, :], window_strides=(1,),
                                 padding=((CONV_K - 1, 0),),
                                 dimension_numbers=('NWC', 'WIO', 'NWC'),
                                 feature_group_count=CONV_D) + b_dw
    z = jax.nn.silu(layer_norm(z, ln_g, ln_b))
    return z @ w_pw

def diff_attention(q, k, v, lam, lam_init, subln_g, rel_bias):
    B, S = q.shape[0], q.shape[1]
    lamf = lam.astype(jnp.float32)
    lam_full = (jnp.exp(jnp.sum(lamf[0] * lamf[1])) - jnp.exp(jnp.sum(lamf[2] * lamf[3])) + lam_init)
    scale = HEAD_DIM ** -0.5
    n_blocks = S // Q_BLOCK
    k_pos = jnp.arange(S)
    qb = q.reshape(B, n_blocks, Q_BLOCK, N_HEADS, 2, HEAD_DIM).transpose(1, 0, 2, 3, 4, 5)

    def block(args):
        i, qi = args
        q_pos = i * Q_BLOCK + jnp.arange(Q_BLOCK)
        rel = q_pos[:, None] - k_pos[None, :]
        bias = rel_bias.astype(jnp.float32)[t5_bucket_2(rel)]
        logits = jnp.einsum('bqhmd,bkhmd->bhmqk', qi, k).astype(jnp.float32) * scale
        logits = logits + bias.transpose(2, 0, 1)[None, :, None]
        logits = jnp.where((rel >= 0)[None, None, None], logits, NEG_INF_2)
        p = jax.nn.softmax(logits, axis=-1)
        p = p[:, :, 0] - lam_full * p[:, :, 1]
        return jnp.einsum('bhqk,bkhv->bqhv', p.astype(v.dtype), v)

    out = lax.map(block, (jnp.arange(n_blocks), qb))
    out = out.transpose(1, 0, 2, 3, 4).reshape(B, S, N_HEADS, V_DIM)
    out = rms_norm_2(out, subln_g) * (1.0 - lam_init)
    return out.reshape(B, S, ATTN_D)

def pool_branch(u, w_grp, scale, w_o):
    B, S = u.shape[0], u.shape[1]
    uf = u.astype(jnp.float32).reshape(B, S, POOL_GROUPS, POOL_GD)
    cz = jnp.pad(jnp.cumsum(uf, axis=1), ((0, 0), (1, 0), (0, 0), (0, 0)))
    t = jnp.arange(S)
    outs = []
    for g, w in enumerate(POOL_WINDOWS):
        c = cz[:, :, g]
        prev = jnp.pad(c, ((0, 0), (w - 1, 0), (0, 0)))[:, :S]
        cnt = jnp.minimum(t + 1, w).astype(jnp.float32)[None, :, None]
        outs.append((c[:, 1:] - prev) / cnt)
    pooled = (jnp.stack(outs, axis=2) - uf).astype(u.dtype)
    y = jnp.einsum('bsgc,gcd->bsgd', pooled, w_grp).reshape(B, S, POOL_D) * scale
    return y @ w_o

def cross_attention(h, mem_n, wq, wkv, wo):
    B, S = h.shape[0], h.shape[1]
    M = mem_n.shape[1]
    q = (h @ wq).reshape(B, S, X_HEADS, X_HEAD_DIM)
    k, v = jnp.split(mem_n @ wkv, 2, axis=-1)
    k = k.reshape(B, M, X_HEADS, X_HEAD_DIM)
    v = v.reshape(B, M, X_HEADS, X_HEAD_DIM)
    logits = jnp.einsum('bshd,bmhd->bhsm', q, k).astype(jnp.float32) * (X_HEAD_DIM ** -0.5)
    p = jax.nn.softmax(logits, axis=-1)
    o = jnp.einsum('bhsm,bmhd->bshd', p.astype(v.dtype), v).reshape(B, S, X_D)
    return o @ wo

def mixer_block(h, w_in, conv_dw, conv_dw_b, conv_ln_g, conv_ln_b, conv_pw,
                lam, lam_init, subln_g, attn_o, rel_bias, pool_w, pool_scale, pool_o, w_out):
    B, S = h.shape[0], h.shape[1]
    u = h @ w_in
    u_conv, q, k, v, u_pool, gates = jnp.split(u, SPLITS, axis=-1)
    y_conv = conv_branch(u_conv, conv_dw, conv_dw_b, conv_ln_g, conv_ln_b, conv_pw)
    q = q.reshape(B, S, N_HEADS, 2, HEAD_DIM)
    k = k.reshape(B, S, N_HEADS, 2, HEAD_DIM)
    v = v.reshape(B, S, N_HEADS, V_DIM)
    y_attn = diff_attention(q, k, v, lam, lam_init, subln_g, rel_bias) @ attn_o
    y_pool = pool_branch(u_pool, pool_w, pool_scale, pool_o)
    g = jax.nn.sigmoid(gates.reshape(B, S, N_BRANCH, D_MODEL))
    merged = g[:, :, 0] * y_conv + g[:, :, 1] * y_attn + g[:, :, 2] * y_pool
    return merged @ w_out

def second_inputs(seed: int = 0) -> dict:
    key = jax.random.key(seed)
    ks = jax.random.split(key, 24)
    f32 = jnp.float32

    def nrm(k, shape, scale):
        return jax.random.normal(k, shape, f32) * scale

    L = DEPTH_2
    return {
        "x": nrm(ks[0], (BATCH, SEQ, D_MODEL), 1.0),
        "mem": nrm(ks[1], (BATCH, MEM_LEN, D_MODEL), 1.0),
        "norm_g": 1.0 + nrm(ks[2], (L, 8, D_MODEL), 0.05),
        "ffn_w1": nrm(ks[3], (L, 2, D_MODEL, D_FF), D_MODEL ** -0.5),
        "ffn_w3": nrm(ks[4], (L, 2, D_MODEL, D_FF), D_MODEL ** -0.5),
        "ffn_w2": nrm(ks[5], (L, 2, D_FF, D_MODEL), D_FF ** -0.5),
        "w_in": nrm(ks[6], (L, D_MODEL, IN_COLS), D_MODEL ** -0.5),
        "conv_dw": nrm(ks[7], (L, CONV_K, CONV_D), CONV_K ** -0.5),
        "conv_dw_b": nrm(ks[8], (L, CONV_D), 0.02),
        "conv_ln_g": 1.0 + nrm(ks[9], (L, CONV_D), 0.05),
        "conv_ln_b": nrm(ks[10], (L, CONV_D), 0.02),
        "conv_pw": nrm(ks[11], (L, CONV_D, D_MODEL), CONV_D ** -0.5),
        "attn_lam": nrm(ks[12], (L, 4, HEAD_DIM), 0.1),
        "attn_subln": 1.0 + nrm(ks[13], (L, V_DIM), 0.05),
        "attn_o": nrm(ks[14], (L, ATTN_D, D_MODEL), ATTN_D ** -0.5),
        "rel_bias": nrm(ks[15], (N_BUCKETS, N_HEADS), 0.5),
        "pool_w": nrm(ks[16], (L, POOL_GROUPS, POOL_GD, POOL_GD), POOL_GD ** -0.5),
        "pool_scale": 1.0 + nrm(ks[17], (L, POOL_D), 0.1),
        "pool_o": nrm(ks[18], (L, POOL_D, D_MODEL), POOL_D ** -0.5),
        "w_out": nrm(ks[19], (L, D_MODEL, D_MODEL), D_MODEL ** -0.5),
        "mem_norm": 1.0 + nrm(ks[20], (L, D_MODEL), 0.05),
        "xattn_q": nrm(ks[21], (L, D_MODEL, X_D), D_MODEL ** -0.5),
        "xattn_kv": nrm(ks[22], (L, D_MODEL, 2 * X_D), D_MODEL ** -0.5),
        "xattn_o": nrm(ks[23], (L, X_D, D_MODEL), X_D ** -0.5),
    }

def second_block(x, mem, norm_g, ffn_w1, ffn_w3, ffn_w2, w_in, conv_dw, conv_dw_b, conv_ln_g, conv_ln_b,
              conv_pw, attn_lam, attn_subln, attn_o, rel_bias, pool_w, pool_scale, pool_o, w_out,
              mem_norm, xattn_q, xattn_kv, xattn_o):
    for l in range(DEPTH_2):
        ng = norm_g[l]
        lam_init = 0.8 - 0.6 * math.exp(-0.3 * l)
        h = rms_norm_2(x, ng[0])
        x = x + 0.5 * rms_norm_2(swiglu(h, ffn_w1[l, 0], ffn_w3[l, 0], ffn_w2[l, 0]), ng[1])
        h = rms_norm_2(x, ng[2])
        y = mixer_block(h, w_in[l], conv_dw[l], conv_dw_b[l], conv_ln_g[l], conv_ln_b[l], conv_pw[l],
                        attn_lam[l], lam_init, attn_subln[l], attn_o[l], rel_bias,
                        pool_w[l], pool_scale[l], pool_o[l], w_out[l])
        x = x + rms_norm_2(y, ng[3])
        h = rms_norm_2(x, ng[4])
        y = cross_attention(h, rms_norm_2(mem, mem_norm[l]), xattn_q[l], xattn_kv[l], xattn_o[l])
        x = x + rms_norm_2(y, ng[5])
        h = rms_norm_2(x, ng[6])
        x = x + 0.5 * rms_norm_2(swiglu(h, ffn_w1[l, 1], ffn_w3[l, 1], ffn_w2[l, 1]), ng[7])
    return x


def setup_inputs(seed=0):
    out = dict(first_inputs(seed))
    for name, value in second_inputs(seed + 1).items():
        if name != "x":
            out[name + "_2"] = value
    return out


def reference(
    x, c, w_mod, b_mod, norm_mix, norm_ffn, w_in, qnorm_a, knorm_a, sinks, rnn_conv_w,
    rnn_conv_b, rnn_gate_a_w, rnn_gate_a_b, rnn_gate_x_w, rnn_gate_x_b, rnn_lambda, qnorm_c,
    knorm_c, rel_bias, w_branch, w_out, w_up, ffn_conv_w, ffn_conv_b, w_down, mem_2, norm_g_2,
    ffn_w1_2, ffn_w3_2, ffn_w2_2, w_in_2, conv_dw_2, conv_dw_b_2, conv_ln_g_2, conv_ln_b_2,
    conv_pw_2, attn_lam_2, attn_subln_2, attn_o_2, rel_bias_2, pool_w_2, pool_scale_2, pool_o_2,
    w_out_2, mem_norm_2, xattn_q_2, xattn_kv_2, xattn_o_2,
):
    x = first_block(
        x, c, w_mod, b_mod, norm_mix, norm_ffn, w_in, qnorm_a, knorm_a, sinks, rnn_conv_w,
        rnn_conv_b, rnn_gate_a_w, rnn_gate_a_b, rnn_gate_x_w, rnn_gate_x_b, rnn_lambda, qnorm_c,
        knorm_c, rel_bias, w_branch, w_out, w_up, ffn_conv_w, ffn_conv_b, w_down,
    )
    return second_block(
        x, mem_2, norm_g_2, ffn_w1_2, ffn_w3_2, ffn_w2_2, w_in_2, conv_dw_2, conv_dw_b_2,
        conv_ln_g_2, conv_ln_b_2, conv_pw_2, attn_lam_2, attn_subln_2, attn_o_2, rel_bias_2,
        pool_w_2, pool_scale_2, pool_o_2, w_out_2, mem_norm_2, xattn_q_2, xattn_kv_2, xattn_o_2,
    )


_drawn_inputs = setup_inputs


def setup_inputs(seed=0):
    import zlib

    import numpy as np

    out = dict(_drawn_inputs(seed))
    spreads = {}
    factors = {'norm_mix': 5.022,
     'norm_ffn': 2.702,
     'qnorm_a': 8.0,
     'knorm_a': 8.0,
     'sinks': 8.0,
     'rnn_conv_b': 7.56,
     'rnn_gate_a_b': 8.0,
     'rnn_gate_x_b': 8.0,
     'qnorm_c': 8.0,
     'knorm_c': 8.0,
     'ffn_conv_b': 6.599,
     'conv_dw_b_2': 2.894,
     'conv_ln_b_2': 6.385,
     'attn_lam_2': 5.036}
    for name, (base, spread) in spreads.items():
        noise = np.random.default_rng([zlib.crc32(name.encode()), seed]).standard_normal(out[name].shape)
        drawn = base * np.exp(spread * noise) if base else spread * noise
        out[name] = __import__('jax').numpy.asarray(drawn.astype(out[name].dtype))
    for name, factor in factors.items():
        out[name] = (out[name] * factor).astype(out[name].dtype)
    return out
```

```python
import math
from contextlib import ExitStack

import concourse.bass as bass
from concourse import mybir

F32 = mybir.dt.float32
F32R = mybir.dt.float32r
ALU = mybir.AluOpType
ACT = mybir.ActivationFunctionType
AX_X = mybir.AxisListType.X

P = 128
T = 256
TT = T // P
D = 1024
NF = D // P
DFF = 2816
HD = 64
LINE = 384
RMS_EPS = 1e-6
LN_EPS = 1e-5
RGLRU_C = 8.0
CONV_K = 31
RNN_K = 4
FFN_K = 3
POOL_PAD = 15
LAYERS = 2
UNIT_KT = 4
COLS = 256
RAW = 6
SPLIT = 4
AHEAD = SPLIT - 1
CONV_PARTS = 3
NEG = -1e30

W_IN_1 = dict(qa=(0, 512), ka=(512, 128), va=(640, 128), xr=(768, 1024), yr=(1792, 1024), qc=(2816, 512),
              kc=(3328, 512), vc=(3840, 512), g=(4352, 3072))
W_IN_2 = dict(a=0, gt=1024, q=2048, k=3072, v=4096, pool=5120, gates=6144)

COL = {}
ROW_TILES = []


def _layout():
    def tile(parts):
        base = sum(n for n, _ in ROW_TILES)
        at = 0
        where = []
        for name, n in parts:
            COL[name] = COL.get(name, (base + at, 0))[0], COL.get(name, (0, 0))[1] + n
            where.append((name, at, n))
            at += n
        ROW_TILES.append((at, where))
    tile([("norm_mix", 8), ("norm_ffn", 8), ("b_mod", 48), ("rnn_conv_w", 32), ("rnn_conv_b", 8),
          ("gate_a_b", 8), ("gate_x_b", 8), ("lambda", 8)])
    tile([("ffn_conv_w", 128)])
    tile([("ffn_conv_w", 4), ("ffn_conv_b", 44), ("qk_gain", 4)])
    for l in range(LAYERS):
        tile([(f"norm{l}", 64), (f"dw_b{l}", 8), (f"ln_g{l}", 8), (f"ln_b{l}", 8), (f"pscale{l}", 8),
              (f"memn{l}", 8), (f"subln{l}", 1)])
        tile([(f"dw{l}", 128)])
        tile([(f"dw{l}", 120)])


_layout()
NCOLS = sum(n for n, _ in ROW_TILES)


def lam_init(layer):
    return 0.8 - 0.6 * math.exp(-0.3 * layer)


def plan(stop=None):
    S = []
    units = []
    readers = {}
    stat = [0]
    xv = [0]
    pairs = []

    def add(kind, **k):
        S.append((kind, k))

    def gemm(w, col, kts, x, evac, ft0=0, form="F", cols=COLS, side=(), src=None, **k):
        p = dict(k, id=len(pairs), x=x, last_unit=len(units) + -(-kts // UNIT_KT) - 1, cols=cols)
        pairs.append(p)
        n = -(-kts // UNIT_KT)
        for j in range(n):
            nk = min(UNIT_KT, kts - j * UNIT_KT)
            u = dict(k, n=len(units), w=w, col=col, kt0=j * UNIT_KT, nkt=nk, x=x, ft0=ft0, form=form, cols=cols,
                     pair=p["id"], first=j == 0, last=j == n - 1, src=src)
            units.append(u)
            readers[x[0]] = u["n"]
            add("unit", **u)
        add(evac, **p)
        return p

    def new_stat():
        stat[0] += 1
        return stat[0]

    def order():
        seen, last, splits, raw = {}, None, [], []
        for kind, k in S:
            for field in ("s", "mod_s"):
                if k.get(field) is not None and k[field] not in seen:
                    seen[k[field]] = last
                    last = k[field]
        for kind, k in S:
            if kind == "unit":
                k["m"] = len(splits)
                splits.append(k)
        for kind, k in S:
            if kind == "mod":
                k["raw"] = len(raw)
                raw.append(k)
            elif kind == "presplit" or (kind == "unit" and k["m"] + AHEAD < len(splits)):
                u = splits[k["m"] if kind == "presplit" else k["m"] + AHEAD]
                u["raw"] = len(raw)
                raw.append(u)
        return S, splits, raw, seen

    def split(buf, gen, src, fts=NF, ft0=0, **k):
        for f in range(fts):
            add("split", buf=buf, gen=gen, src=src, f=f, ft0=ft0, after=readers.get(buf), v=xv[0], **k)

    def weave(main, side, per=1):
        out, side = [], list(side)
        for s in main:
            out.append(s)
            if s[0] == "unit":
                for _ in range(per):
                    if side:
                        out.append(side.pop(0))
        return out + side

    def collect(fn):
        mark = len(S)
        fn()
        got = S[mark:]
        del S[mark:]
        return got

    def x_stats(key, src="x"):
        s = new_stat()
        add("square", key=key, src=src, v=xv[0])
        add("stat", key=key, s=s)
        add("rstd", key=key, s=s, out="RX", scale=1.0 / D, eps="eps_rms")

    def attention(cfg, n):
        steps = []
        for i in range(n):
            steps.append(("scores", dict(cfg=cfg, i=i)))
            if i and cfg[:4] == "diff":
                steps.append(("subln", dict(cfg=cfg, i=i - 1, s=new_stat())))
            steps += [("softmax", dict(cfg=cfg, i=i)), ("turn", dict(cfg=cfg, i=i)), ("pv", dict(cfg=cfg, i=i))]
        if cfg[:4] == "diff":
            steps.append(("subln", dict(cfg=cfg, i=n - 1, s=new_stat())))
        return steps

    def done(tag):
        return stop == tag

    def residual(key, form, **k):
        xv[0] += 1
        add("residual", key=key, form=form, v=xv[0], **k)

    add("setup")

    def modulation(first, count):
        got = []
        stat_id = new_stat()
        for n in range(first, first + count):
            u = dict(n=len(units), w="w_mod", col=n * P, mod=n, first=first, mod_s=stat_id, src="mod")
            units.append(u)
            got.append(("mod", u))
        return got + [("mod_sum", dict(first=first, count=count, s=stat_id))]

    initial = modulation(0, 2 * NF)
    S += initial[:RAW]
    add("params", part=0)
    add("turn_x")
    S += initial[RAW:]
    add("bias")
    for m in range(AHEAD):
        add("presplit", m=m)
    x_stats("b1x")
    add("adapt", key="b1h", rstd="b1x", shift=0, scale=1, norm="norm_mix", after=None, v=0)

    def z1(name, j, evac, form="F", cols=COLS, **k):
        gemm("w_in", W_IN_1[name][0] + j * COLS, NF, ("H", "b1h"), evac, form=form, cols=cols, **k)

    waiting, normed = [], []

    def qk_units(name, n, dst, gain):
        for j in range(n):
            s = new_stat()
            normed.append(s)
            b = len(normed) % 2
            k = dict(dst=dst, ft=2 * j, b=b, before=normed[-3] if len(normed) > 2 else None)
            if name == "qc" and j == 1:
                add("params", part=1)
            if name == "ka":
                gemm("w_in", W_IN_1["ka"][0], NF, ("H", "b1h"), "evac_qk", src="dup", **k)
            else:
                z1(name, j, "evac_qk", **k)
            waiting.append(dict(dst=dst, ft=2 * j, gain=gain, s=s, b=b))
            if len(waiting) > 1:
                add("qk_norm", **waiting.pop(0))
    qk_units("qc", 2, "qc", 2)
    qk_units("kc", 2, "kc", 3)
    for j in range(2):
        z1("vc", j, "evac_v1", form="T", dst="vc", c0=j * COLS)
    qk_units("qa", 2, "qa", 0)
    qk_units("ka", 1, "ka", 1)
    gemm("w_in", W_IN_1["va"][0], NF, ("H", "b1h"), "evac_v1", form="T", cols=128, dst="va", c0=0)
    add("qk_norm", **waiting.pop(0))

    def rest():
        add("pads1")
        for j in range(4):
            z1("xr", j, "evac_xr", ft=2 * j)
        for j in range(4):
            z1("yr", j, "evac_yr", ft=2 * j)
    add("hankel", which=1, l=0, after=None)
    side = attention("moba", 4) + [("hankel", dict(which=0, l=0, after=("scores", "moba", 3)))] + attention("swa", 4)
    main = collect(rest)
    S += weave(main, side, 2)

    late = []
    for f in range(NF + 3):
        if f < NF:
            late.append(("rnn_conv", dict(f=f)))
        if 2 <= f < NF + 2:
            late.append(("rnn_in", dict(f=f - 2)))
        if 1 <= f <= NF:
            late.append(("rnn_gate", dict(f=f - 1, s=new_stat())))
        if f >= 3:
            late.append(("rnn_mult", dict(f=f - 3)))
    late.append(("rnn_scan", {}))
    for n in range(2 * NF, 6 * NF, 4):
        late += modulation(n, 4)
    split("G", "oa", "qa", fts=4)
    split("G", "oc", "qc", fts=4, ft0=4)
    mark = len(S)
    for b, (row, kts, ft0, gens) in enumerate([(0, 4, 0, "oa"), (1536, 4, 4, "oc"), (512, 8, 0, "ob")]):
        gate = {"oa": 0, "ob": 1, "oc": 2}[gens]
        if gens == "ob":
            main = S[mark:]
            del S[mark:]
            S += weave(main, late, 3)
            split("G", "ob", "XC", half=True)
        for c in range(4):
            gemm("w_in", W_IN_1["g"][0] + gate * D + c * COLS, NF, ("H", "b1h"), "evac_gate", scaled=False, ft=2 * c)
            gemm("w_branch", c * COLS, kts, ("G", gens), "evac_branch", ft0=ft0, row0=row, ft=2 * c,
                 first_branch=b == 0, mg=("b1", b))
    split("H", "b1m", "MG", mg=("b1", 2), half=True)
    for c in range(4):
        gemm("w_out", c * COLS, NF, ("H", "b1m"), "evac_y", ft=2 * c, sq=None, yk="b1r")
    residual("b1r", "gate_mod", chunk=2)
    x_stats("b1f")
    add("adapt", key="b1g", rstd="b1f", shift=3, scale=4, norm="norm_ffn", after=readers["H"], v=xv[0])
    add("pads_f1")
    for j in range(11):
        gemm("w_up", j * COLS, NF, ("H", "b1g"), "evac_up1", j=j, val=0)
        gemm("w_up", DFF + j * COLS, NF, ("H", "b1g"), "evac_up1", j=j, val=1)
        if j:
            add("hid_split", gen="b1u", j=j - 1)
    add("hid_split", gen="b1u", j=10)
    for c in range(4):
        gemm("w_down", c * COLS, 22, ("HID", "b1u"), "evac_y", ft=2 * c, sq=None, yk="b1s")
    residual("b1s", "gate_mod", chunk=5)
    if stop == "block1":
        add("finish")
        return order()

    def ffn(l, i):
        key = f"l{l}f{i}"
        split("H", key, "x", col=(f"norm{l}", (0, 6)[i] * 8))
        x_stats(key)
        for j in range(11):
            gemm("w1", j * COLS, NF, ("H", key), "evac_ffn_gate", l=l, i=i, j=j)
            gemm("w3", j * COLS, NF, ("H", key), "evac_ffn_val", l=l, i=i, j=j)
            if j:
                add("hid_split", gen=key, j=j - 1)
        add("hid_split", gen=key, j=10)
        s = new_stat()
        for c in range(4):
            gemm("w2", c * COLS, 22, ("HID", key), "evac_y", ft=2 * c, sq=s, yk=key, l=l, i=i)
            if c:
                add("ystat", s=s, c=c - 1)
        add("ystat", s=s, c=3)
        add("rstd", key=key + "y", s=s, out="RY", scale=1.0 / D, eps="eps_rms")
        residual(key, "normed", col=(f"norm{l}", (1, 7)[i] * 8), half=True)

    def z2(l, name, j, evac, form="F", **k):
        gemm("w_in_2", W_IN_2[name] + j * COLS, NF, ("H", f"l{l}m"), evac, form=form, l=l, **k)

    def mixer(l):
        key = f"l{l}m"
        split("H", key, "x", col=(f"norm{l}", 16))
        x_stats(key)
        add("rstd_cols", key=key, s=new_stat())
        for j in range(4):
            z2(l, "v", j, "evac_v2", form="T", dst="v", c0=j * COLS)
        for j in range(4):
            z2(l, "k", j, "evac_scaled", dst="k", ft=2 * j, by=1.0)
        for j in range(4):
            z2(l, "q", j, "evac_scaled", dst="q", ft=2 * j, by=HD ** -0.5)
        add("hankel", which=2, l=l, after=("unit", readers["HID"]))
        add("pads2", l=l, hid_unit=readers["HID"])

        def rest():
            for j in range(4):
                z2(l, "gt", j, "evac_gate", scaled=True, ft=2 * j)
                z2(l, "a", j, "evac_glu", ft=2 * j)
            for j in range(4):
                z2(l, "pool", j, "evac_pool", ft=2 * j)
                add("window", g=j, l=l)
            split("G", key + "p", "pooled")
            for g in range(4):
                gemm("pool_w", 0, 2, ("G", key + "p"), "evac_pool_w", ft0=2 * g, l=l, g=g)
            for c in range(4):
                z2(l, "gates", 8 + c, "evac_gate", scaled=True, ft=2 * c)
                gemm("pool_o", c * COLS, NF, ("G", key + "q"), "evac_branch", l=l, ft=2 * c, first_branch=True,
                     mg=(key, 0))
            add("cln_mean", l=l, s=new_stat())
            add("cln_var", l=l, s=new_stat())
            add("cln_out", l=l)
            split("G", key + "c", "TMP", half=True)
            for c in range(4):
                z2(l, "gates", c, "evac_gate", scaled=True, ft=2 * c)
                gemm("conv_pw", c * COLS, NF, ("G", key + "c"), "evac_branch", l=l, ft=2 * c, first_branch=False,
                     mg=(key, 1))
        att = attention(f"diff{l}", 8)
        main = collect(rest)
        after_glu = 1 + max(i for i, (kind, _) in enumerate(main) if kind == "evac_glu")
        conv = [("conv31", dict(l=l, f=f, part=part)) for f in range(NF) for part in range(CONV_PARTS)]
        n0 = sum(kind == "unit" for kind, _ in main[:after_glu])
        S.extend(weave(main[:after_glu], att[:n0], 1))
        att = att[n0:]
        side = []
        for i in range(max(len(att), len(conv))):
            side += conv[i:i + 1] + att[i:i + 1]
        S.extend(weave(main[after_glu:], side, 2))
        split("G", key + "a", "q")
        for c in range(4):
            z2(l, "gates", 4 + c, "evac_gate", scaled=True, ft=2 * c)
            gemm("attn_o", c * COLS, NF, ("G", key + "a"), "evac_branch", l=l, ft=2 * c, first_branch=False,
                 mg=(key, 2))
        split("H", key + "o", "MG", mg=(key, 2), half=True)
        s = new_stat()
        for c in range(4):
            gemm("w_out_2", c * COLS, NF, ("H", key + "o"), "evac_y", ft=2 * c, sq=s, yk=key, l=l)
            if c:
                add("ystat", s=s, c=c - 1)
        add("ystat", s=s, c=3)
        add("rstd", key=key + "y", s=s, out="RY", scale=1.0 / D, eps="eps_rms")
        residual(key, "normed", col=(f"norm{l}", 24), half=False)

    def cross(l):
        key = f"l{l}c"
        add("mem_load", l=l, v=xv[0])
        split("H", key, "x", col=(f"norm{l}", 32))
        x_stats(key)
        for j in range(4):
            gemm("xattn_q", j * COLS, NF, ("H", key), "evac_scaled", l=l, dst="xq", ft=2 * j, by=(D // 4) ** -0.5)
        add("mem_turn", l=l)
        split("M", key + "m", "memf", col=(f"memn{l}", 0))
        x_stats(key + "m", src="memf")
        add("rstd_cols", key=key + "m", s=new_stat())
        for j in range(4):
            gemm("xattn_kv", j * COLS, NF, ("M", key + "m"), "evac_scaled", l=l, dst="xk", ft=2 * j, by=1.0)
        for j in range(4):
            gemm("xattn_kv", D + j * COLS, NF, ("M", key + "m"), "evac_v2", form="T", l=l, dst="xv", c0=j * COLS)
        S.extend(attention(f"cross{l}", 4))
        split("H", key + "o", "xq")
        s = new_stat()
        for c in range(4):
            gemm("xattn_o", c * COLS, NF, ("H", key + "o"), "evac_y", ft=2 * c, sq=s, yk=key, l=l)
            if c:
                add("ystat", s=s, c=c - 1)
        add("ystat", s=s, c=3)
        add("rstd", key=key + "y", s=s, out="RY", scale=1.0 / D, eps="eps_rms")
        residual(key, "normed", col=(f"norm{l}", 40), half=False)

    for l in range(LAYERS):
        ffn(l, 0)
        if done(f"f{l}0"):
            break
        mixer(l)
        if done(f"m{l}"):
            break
        cross(l)
        if done(f"c{l}"):
            break
        ffn(l, 1)
        if done(f"f{l}1"):
            break
    add("finish")
    return order()


def build(nc, a, out, scratch, marks, final, stop=None):
    steps, splits, raws, stat_before = plan(stop)

    ctx = ExitStack()
    sb = lambda name, shape, dt=F32: ctx.enter_context(nc.sbuf_tensor(name, shape, dt))

    RAWB = sb("raw_weights", [P, RAW, UNIT_KT, COLS])
    WH, WL = sb("weights_hi", [P, SPLIT, UNIT_KT, COLS], F32R), sb("weights_lo", [P, SPLIT, UNIT_KT, COLS], F32R)
    X, Y = sb("x_res", [P, NF, T]), sb("y", [P, NF, T])
    HH, HL = sb("h_hi", [P, NF, T], F32R), sb("h_lo", [P, NF, T], F32R)
    SQ = sb("squares", [P, NF, T])
    RX, RY, RQ = sb("rstd_x", [P, T]), sb("rstd_y", [P, T]), sb("rstd_q", [P, 2, T])
    RT = sb("rstd_tok", [P, TT])
    ASQ = sb("small_squares", [P, 2, 2, T])
    CT = sb("param_cols", [P, NCOLS])
    HALFB = sb("half_gate_bias", [P, 2 * NF])
    MODC = sb("mod_cols", [P, 48])
    CC, SP4, QG = sb("silu_c", [P, NF]), sb("softplus4", [P, NF]), sb("qk_gains", [P, 4])
    ONES, IDENT, FLIP, HEADS = (sb(n, [P, P]) for n in ("ones", "ident", "flip", "headsum"))
    EPS = sb("eps", [P, 4])
    LAM, SINK = sb("neg_lam", [P, LAYERS]), sb("neg_sinks", [P, 8])
    NM, DEN, RD, ES = sb("neg_max", [P, 4]), sb("den", [P, 4]), sb("rden", [P, 4]), sb("sink_exp", [P, 4])

    def overlay(**shapes):
        with ExitStack() as c:
            return {n: c.enter_context(nc.sbuf_tensor(n, *(s if isinstance(s, tuple) else (s,)), F32)
                                       if not isinstance(s, tuple) else nc.sbuf_tensor(n, s[0], s[1]))
                    for n, s in shapes.items()}
    R = F32R
    o_set = overlay(rows=[P, len(ROW_TILES), P], xtok=[P, TT, D], onehot=[33, 3, LINE], relb=[33, 24],
                    lines=[8, 3, LINE], lamb=[P, LAYERS * 4 * HD], lamp=[P, LAYERS * 2, HD], lams=[P, LAYERS * 2],
                    spt=[P, 6, NF], sgc=[P, NF], sinks_in=[P, 8], c_cols=[P, NF])
    o_b1 = overlay(gh=([P, NF, T], R), gl=([P, NF, T], R), qa=[P, 4, T], ka=[P, 2, T], va=[P, TT, 128],
                   qc=[P, 4, T], kc=[P, 4, T], vc=[P, TT, 512], hank1=[P, 8, T], e1=[P, 2, 2, T], pt1=[P, 768],
                   xr=[P, NF, RNN_K - 1 + T], xc=[P, NF, T], s_all=[P, NF, T], rg=[P, 2, T],
                   gt1=[P, 2, 2, T], bt1=[P, 2, T], bd=[P, NF, 2, P])
    o_f1 = overlay(hidh=([P, 22, T], R), hidl=([P, 22, T], R), up=[P, 2, 2, T + FFN_K - 1], uc=[P, 2, 2, T],
                   fe1=[P, 2, T], hf1=[P, 2, 2, T])
    o_f2 = overlay(hidh2=([P, 22, T], R), hidl2=([P, 22, T], R), fa=[P, 2, 2, T], fe=[P, 2, 2, T], fb=[P, 2, T],
                   hf=[P, 2, 2, T])
    o_m = overlay(gh2=([P, NF, T], R), gl2=([P, NF, T], R), q=[P, NF, T], k=[P, NF, T], v=[P, TT, D],
                  hank2=[P, 8, T], e2=[P, 2, 2, T], pt2=[P, 768], zp=[P, NF, CONV_K - 1 + T],
                  pu=[P, NF, POOL_PAD + T], tmp2=[P, NF, T], gt2=[P, 2, 2, T], bt2=[P, 2, T],
                  cnt=[P, 4, T])
    o_c = overlay(mh=([P, NF, T], R), ml=([P, NF, T], R), xq=[P, NF, T], xk=[P, NF, T], xv=[P, TT, D],
                  e3=[P, 2, 2, T], pt3=[P, 2 * 512], memt=[P, TT, D], memf=[P, NF, T])
    o_o = overlay(otok=[P, TT, D])

    o_b1["tmp1"] = o_b1["hank1"]
    wide = POOL_PAD + T
    WIN = [SQ[:].rearrange("p f t -> p (f t)")[:, i * 2 * wide:(i + 1) * 2 * wide].rearrange("p (a t) -> p a t", a=2)
           for i in range(2)]
    RT8 = sb("adapt_gain", [P, NF])
    MGS = {"b1": SQ[:], "m": o_m["pu"][:, :, POOL_PAD:]}
    last_x = max([k["v"] for kind, k in steps if kind == "residual"], default=0)
    n_pairs = 1 + max([k["id"] for kind, k in steps if kind.startswith("evac")], default=-1)
    last_pairs = [p for p in (n_pairs - 2, n_pairs - 1) if p >= 0]

    GP = ctx.enter_context(nc.psum_tensor("gemm_ps", [P, 2, 2, 512], F32))
    PB = ctx.enter_context(nc.psum_tensor("misc_ps", [P, 4, 512], F32))
    GPF = GP[:].rearrange("p a b c -> p (a b c)")
    PBF = PB[:].rearrange("p a b -> p (a b)")
    STAT = PB[:, 3, :]
    TURN = PBF[:, 512:1536]

    names = [f"raw_landed{i}" for i in range(RAW)] + [
        "consts_in", "ident_in", "x_in", "bias_in", "small_in", "count_in", "hankel_in", "line_out", "mem_in", "rows_in", "blocks_in", "y_out",
        "weights_rounded", "weights_rest", "gemm_done", "act_drain", "vec_drain", "act_norm", "vec_norm", "pe_norm",
        "act_attn", "vec_attn", "pe_attn", "act_rnn", "vec_rnn", "pe_rnn", "act_ffn", "vec_ffn", "act_split",
        "vec_split", "act_conv", "vec_conv", "vec_mod", "c_in", "rows_in2", "act_gelu", "vec_gelu", "pe_mod", "act_setup", "vec_setup",
        "pe_setup", "pool_setup"]
    sems = {n: ctx.enter_context(nc.semaphore(n)) for n in names}

    count = {}

    def up(name, reached=None, by=1):
        count[name] = count.get(name, 0) + by
        if reached is not None:
            marks[reached] = (name, count[name])
        return count[name]

    def mark(reached, name):
        marks[reached] = (name, count[name])

    def at(*reached):
        assert reached in marks or not final, reached
        return marks.get(reached, (None, 1))[1]

    def done(reached):
        assert reached in marks or not final, reached
        name, value = marks.get(reached, (names[0], 1))
        return sems[name], value

    XBUF = {"H": (HH, HL), "M": (o_c["mh"], o_c["ml"])}

    def xbuf(buf, gen):
        if buf == "G":
            return (o_b1["gh"], o_b1["gl"]) if gen in ("oa", "ob", "oc") else (o_m["gh2"], o_m["gl2"])
        if buf == "HID":
            return (o_f1["hidh"], o_f1["hidl"]) if gen == "b1u" else (o_f2["hidh2"], o_f2["hidl2"])
        return XBUF[buf]

    BUF = {"x": X, "y": Y, "qa": o_b1["qa"], "ka": o_b1["ka"], "qc": o_b1["qc"], "kc": o_b1["kc"], "va": o_b1["va"],
           "vc": o_b1["vc"], "XC": o_b1["xc"], "q": o_m["q"], "k": o_m["k"], "v": o_m["v"], "xq": o_c["xq"],
           "xk": o_c["xk"], "xv": o_c["xv"], "memf": o_c["memf"], "pooled": o_m["tmp2"], "TMP": o_m["tmp2"],
           }

    def col(name, i=0, n=1):
        return CT[:, COL[name][0] + i:COL[name][0] + i + n]

    def bc(ap, n=2):
        return ap.unsqueeze(1).to_broadcast([P, n, T])

    def slot(pid):
        return GP[:, pid % 2, :, 0:T]

    def att(cfg, i):
        if cfg in ("swa", "moba"):
            q, k, v = (o_b1["qa"], o_b1["ka"], o_b1["va"]) if cfg == "swa" else (o_b1["qc"], o_b1["kc"], o_b1["vc"])
            kt = i // 2 if cfg == "swa" else i
            vcol = (lambda m: (i // 2) * HD) if cfg == "swa" else (lambda m: (2 * i + m) * HD)
            return dict(maps=2, q=[q[64 * m:64 * m + 64, i, :] for m in (0, 1)],
                        k=[k[64 * m:64 * m + 64, kt, :] for m in (0, 1)],
                        v=[[v[:, b, vcol(m):vcol(m) + HD] for b in (0, 1)] for m in (0, 1)],
                        hank=o_b1["hank1"], head=[2 * i, 2 * i + 1], E=o_b1["e1"], PT=o_b1["pt1"], o=q[:, i, :],
                        causal=True, pack="pair", hname=("hank", 0 if cfg == "swa" else 1, 0))
        l = int(cfg[-1])
        if cfg[:4] == "diff":
            q, k, v = o_m["q"], o_m["k"], o_m["v"]
            return dict(maps=2, q=[q[64 * m:64 * m + 64, i, :] for m in (0, 1)],
                        k=[k[64 * m:64 * m + 64, i, :] for m in (0, 1)],
                        v=[[v[:, b, i * P:(i + 1) * P] for b in (0, 1)]], hank=o_m["hank2"], head=[i, i],
                        E=o_m["e2"], PT=o_m["pt2"], o=q[:, i, :], causal=True, pack="diff", hname=("hank", 2, l))
        q, k, v = o_c["xq"], o_c["xk"], o_c["xv"]
        return dict(maps=1, q=[[q[:, 2 * i + f, :] for f in (0, 1)]], k=[[k[:, 2 * i + f, :] for f in (0, 1)]],
                    v=[[v[:, b, (2 * i + f) * P:(2 * i + f + 1) * P] for b in (0, 1)] for f in (0, 1)],
                    hank=None, E=o_c["e3"], PT=o_c["pt3"], o=q[:, 2 * i:2 * i + 2, :], causal=False, pack="cross",
                    hname=None)

    def scores_at(c, qt, m, nk):
        return PB[:, qt, 0:nk] if c["maps"] == 1 else PB[:, m, P * qt:P * qt + nk]

    def source(k):
        if k["src"] == "MG":
            return MGS["b1" if k["mg"][0] == "b1" else "m"][:, k["f"], :]
        return BUF[k["src"]][:, k["f"], :]

    def ready_of(k):
        src, f, gen = k["src"], k["f"], k["gen"]
        return {"x": ("x", k["v"], f // 2), "qa": ("o", "swa", f), "qc": ("o", "moba", f), "XC": ("ob", f),
                "MG": ("mg",) + (k.get("mg") or ()) + (f // 2,), "q": ("o", "diff" + gen[1], f),
                "xq": ("o", "cross" + gen[1], f // 2), "pooled": ("pooled", gen[:2], f // 2),
                "TMP": ("cln", gen[:2], f), "memf": ("memf", gen[:2], f // 4)}[src]

    W_DRAM = {
        "w_mod": lambda u: a["w_mod"][0], "w_in": lambda u: a["w_in"][0],
        "w_branch": lambda u: a["w_branch"][0, u["row0"]:u["row0"] + (512 if u["ft0"] or u["row0"] == 0 else 1024), :],
        "w_out": lambda u: a["w_out"][0], "w_up": lambda u: a["w_up"][0], "w_down": lambda u: a["w_down"][0],
        "w1": lambda u: a["ffn_w1_2"][u["l"], u["i"]], "w3": lambda u: a["ffn_w3_2"][u["l"], u["i"]],
        "w2": lambda u: a["ffn_w2_2"][u["l"], u["i"]], "w_in_2": lambda u: a["w_in_2"][u["l"]],
        "pool_w": lambda u: a["pool_w_2"][u["l"], u["g"]], "pool_o": lambda u: a["pool_o_2"][u["l"]],
        "conv_pw": lambda u: a["conv_pw_2"][u["l"]], "attn_o": lambda u: a["attn_o_2"][u["l"]],
        "w_out_2": lambda u: a["w_out_2"][u["l"]], "xattn_q": lambda u: a["xattn_q_2"][u["l"]],
        "xattn_kv": lambda u: a["xattn_kv_2"][u["l"]], "xattn_o": lambda u: a["xattn_o_2"][u["l"]],
    }

    def mod_raw(r):
        return RAWB[:, r % RAW].rearrange("p k n -> p (k n)").rearrange("p (k n) -> p k n", n=P)

    block = ctx.enter_context(nc.Block())

    @block.sync
    def _(sp):
        c_cols = bass.AP(tensor=a["c"].tensor, offset=a["c"].offset, ap=[[1, P], [P, NF]])
        sp.dma_start(o_set["c_cols"][:], c_cols, allow_slow_non_contiguous=True).then_inc(sems["c_in"], 16)
        up("c_in", ("c_in",), by=16)
        src = {"norm_mix": a["norm_mix"], "norm_ffn": a["norm_ffn"], "b_mod": a["b_mod"],
               "rnn_conv_w": a["rnn_conv_w"], "rnn_conv_b": a["rnn_conv_b"], "gate_a_b": a["rnn_gate_a_b"],
               "gate_x_b": a["rnn_gate_x_b"], "lambda": a["rnn_lambda"], "ffn_conv_w": a["ffn_conv_w"],
               "ffn_conv_b": a["ffn_conv_b"]}
        for l in range(LAYERS):
            src |= {f"norm{l}": a["norm_g_2"][l], f"dw_b{l}": a["conv_dw_b_2"][l], f"ln_g{l}": a["conv_ln_g_2"][l],
                    f"ln_b{l}": a["conv_ln_b_2"][l], f"pscale{l}": a["pool_scale_2"][l],
                    f"memn{l}": a["mem_norm_2"][l], f"subln{l}": a["attn_subln_2"][l], f"dw{l}": a["conv_dw_2"][l]}
        used = {}

        def load_rows(tiles, sem, mark):
            for i in tiles:
                for name, at_, n in ROW_TILES[i][1]:
                    if name == "qk_gain":
                        for j, g in enumerate(("qnorm_a", "knorm_a", "qnorm_c", "knorm_c")):
                            for h in range(2):
                                sp.dma_start(o_set["rows"][at_ + j:at_ + j + 1, i, h * HD:(h + 1) * HD], a[g]).then_inc(sems["rows_in2"], 16)
                                up("rows_in2", by=16)
                        continue
                    ap = src[name]
                    first = used.get(name, 0)
                    used[name] = first + n
                    flat = bass.AP(tensor=ap.tensor, offset=ap.offset + first * P, ap=[[P, n], [1, P]])
                    sp.dma_start(o_set["rows"][at_:at_ + n, i, :], flat).then_inc(sems[sem], 16)
                    up(sem, mark, by=16)

        for u in raws:
            r = u["raw"]
            if r == RAW:
                sp.dma_start(IDENT[:], a["ident"]).then_inc(sems["ident_in"], 16)
                up("ident_in", ("ident",), by=16)
                load_rows((0,), "rows_in", ("rows",))
                sp.dma_start(o_set["xtok"][:], a["x"][0].rearrange("(t p) d -> p t d", p=P)).then_inc(sems["x_in"], 16)
                up("x_in", ("xtok",), by=16)
                sp.dma_start(FLIP[:], a["flip"]).then_inc(sems["consts_in"], 16)
                up("consts_in", by=16)
                sp.dma_start(HEADS[:], a["headsum"]).then_inc(sems["consts_in"], 16)
                up("consts_in", ("consts",), by=16)
            if r == 2 * NF + 2:
                load_rows(range(1, len(ROW_TILES)), "rows_in2", ("rows2",))
            if r >= RAW:
                sp.wait_ge(*done(("free", r - RAW)))
            w = W_DRAM[u["w"]](u).rearrange("(k p) n -> p k n", p=P)
            if u["src"] == "mod":
                sp.dma_start(mod_raw(r), w[:, :, u["col"]:u["col"] + P]).then_inc(sems[f"raw_landed{r % RAW}"], 16)
                up(f"raw_landed{r % RAW}", ("landed", r), by=16)
                continue
            w = w[:, u["kt0"]:u["kt0"] + u["nkt"], :]
            dst = RAWB[:, r % RAW, 0:u["nkt"], :]
            sem = f"raw_landed{r % RAW}"
            if u["src"] == "dup":
                for g in range(4):
                    c = u["col"] + (g // 2) * HD
                    sp.dma_start(dst[:, :, g * HD:(g + 1) * HD], w[:, :, c:c + HD]).then_inc(sems[sem], 16)
                    up(sem, ("landed", r), by=16)
            else:
                sp.dma_start(dst[:, :, 0:u["cols"]], w[:, :, u["col"]:u["col"] + u["cols"]]).then_inc(sems[sem], 16)
                up(sem, ("landed", r), by=16)
        sp.wait_ge(sems["act_setup"], at("otok"))
        sp.dma_start(out[0].rearrange("(t p) d -> p t d", p=P), o_o["otok"][:]).then_inc(sems["y_out"], 16)
        sp.wait_ge(sems["y_out"], up("y_out", by=16))

    @block.tensor
    def _(pe):
        state = dict(att=None)

        def stat_free(s):
            if stat_before.get(s) is not None:
                pe.wait_ge(*done(("stat_read", stat_before[s])))

        def pe_unit(u):
            xh, xl = xbuf(*u["x"])
            m = u["m"] % SPLIT
            pe.wait_ge(sems["weights_rest"], at("rest", u["m"]))
            if u["first"]:
                if u["pair"] >= 2:
                    pe.wait_ge(*done(("evac", u["pair"] - 2)))
                else:
                    pe.wait_ge(sems["vec_setup"], at("x", 0, 3))
            ps = GP[:, u["pair"] % 2, :, :]
            tiles = u["cols"] // P if u["form"] == "F" else TT
            for c in range(tiles):
                for kt in range(u["nkt"]):
                    f = u["ft0"] + u["kt0"] + kt
                    if c == 0:
                        pe.wait_ge(*done(("split", *u["x"], f)))
                    for n, (w, x) in enumerate(((WH, xh), (WH, xl), (WL, xh))):
                        start = u["first"] and kt == 0 and n == 0
                        stop_ = u["last"] and kt == u["nkt"] - 1 and n == 2
                        if u["form"] == "F":
                            mm = pe.matmul(ps[:, c, 0:T], w[:, m, kt, c * P:(c + 1) * P], x[:, f, :],
                                           start=start, stop=stop_)
                        else:
                            mm = pe.matmul(ps[:, c, 0:u["cols"]], x[:, f, c * P:(c + 1) * P],
                                           w[:, m, kt, 0:u["cols"]], start=start, stop=stop_)
            mm.then_inc(sems["gemm_done"], 1)
            up("gemm_done", ("unit", u["n"]))

        def pe_params(k):
            if k["part"] == 0:
                pe.wait_ge(sems["ident_in"], at("ident"))
                pe.wait_ge(sems["rows_in"], at("rows"))
            else:
                pe.wait_ge(sems["rows_in2"], at("rows2"))
                pe.wait_ge(sems["act_setup"], at("lines_read"))
            for i in ((0,) if k["part"] == 0 else range(1, len(ROW_TILES))):
                n = ROW_TILES[i][0]
                t = pe.transpose(PBF[:, i * P:i * P + n], o_set["rows"][0:n, i, :], IDENT[0:n, 0:n])
            t.then_inc(sems["pe_setup"], 1)
            up("pe_setup", ("rows_T", k["part"]))

        def pe_turn_x(k):
            pe.wait_ge(sems["x_in"], at("xtok"))
            for f in range(NF):
                for t in range(TT):
                    mm = pe.transpose(GPF[:, f * T + t * P:f * T + (t + 1) * P], o_set["xtok"][:, t, f * P:(f + 1) * P],
                                      IDENT[:])
            mm.then_inc(sems["pe_setup"], 1)
            up("pe_setup", ("x_T",))

        def pe_mod(u):
            pe.wait_ge(*done(("landed", u["raw"])))
            pe.wait_ge(sems["vec_setup"], at("cc"))
            if u["mod"] == u["first"]:
                stat_free(u["mod_s"])
            i = u["mod"] - u["first"]
            for kt in range(NF):
                mm = pe.matmul(STAT[:, i:i + 1], mod_raw(u["raw"])[:, kt, :], CC[:, kt:kt + 1], start=kt == 0,
                               stop=kt == NF - 1)
            mm.then_inc(sems["pe_mod"], 1)
            up("pe_mod", ("free", u["raw"]))
            marks[("mod_ps", u["mod"])] = marks[("free", u["raw"])]

        def pe_bias(k):
            pe.wait_ge(sems["bias_in"], at("bias_in"))
            pe.wait_ge(sems["vec_setup"], at("relb"))
            pe.wait_ge(sems["act_setup"], at("cols", 0))
            for i in range(3):
                mm = pe.matmul(PB[0:8, i, 0:LINE], o_set["relb"][:, 8 * i:8 * i + 8], o_set["onehot"][:, i, :],
                               start=True, stop=True)
            mm.then_inc(sems["pe_setup"], 1)
            up("pe_setup", ("lines_ps",))

        def pe_stat(k):
            stat_free(k["s"])
            pe.wait_ge(sems["vec_setup"], at("ones"))
            for f in range(NF):
                pe.wait_ge(sems["act_norm"], at("sq", k["key"], f // 2))
                mm = pe.matmul(STAT[:, 0:T], ONES[:], SQ[:, f, :], start=f == 0, stop=f == NF - 1)
            mm.then_inc(sems["pe_norm"], 1)
            up("pe_norm", ("stat", k["s"]))

        def pe_ystat(k):
            if k["c"] == 0:
                stat_free(k["s"])
            pe.wait_ge(sems["act_drain"], at("sqy", k["s"], k["c"]))
            for f in (2 * k["c"], 2 * k["c"] + 1):
                mm = pe.matmul(STAT[:, 0:T], ONES[:], SQ[:, f, :], start=f == 0, stop=f == NF - 1)
            mm.then_inc(sems["pe_norm"], 1)
            up("pe_norm", ("stat", k["s"]) if k["c"] == 3 else None)

        def pe_rstd_cols(k):
            stat_free(k["s"])
            pe.wait_ge(sems["act_norm"], at("rstd", k["key"]))
            for t in range(TT):
                mm = pe.transpose(STAT[:, t * P:(t + 1) * P], RX[:, t * P:(t + 1) * P], IDENT[:])
            mm.then_inc(sems["pe_norm"], 1)
            up("pe_norm", ("rt_ps", k["s"]))

        def pe_qk_norm(k):
            stat_free(k["s"])
            pe.wait_ge(sems["act_drain"], at("asq", k["dst"], k["ft"]))
            pe.wait_ge(sems["consts_in"], at("consts"))
            mm = pe.matmul(STAT[:, :], HEADS[:], ASQ[:, k["b"]].rearrange("p a t -> p (a t)"), start=True, stop=True)
            mm.then_inc(sems["pe_norm"], 1)
            up("pe_norm", ("stat", k["s"]))

        def pe_scores(k):
            c = att(k["cfg"], k["i"])
            if state["att"] is not None:
                pe.wait_ge(sems["vec_attn"], at("o_raw", *state["att"]))
                if state["att"][0][:4] == "diff":
                    pe.wait_ge(sems["act_attn"], at("o_sq", *state["att"]))
            else:
                pe.wait_ge(sems["act_setup"], at("lines_read"))
            if c["hname"] is not None:
                pe.wait_ge(sems["hankel_in"], at(*c["hname"]))
            if k["cfg"] in ("swa", "moba"):
                pe.wait_ge(sems["vec_norm"], at("qk", "qa" if k["cfg"] == "swa" else "qc", k["i"] // 2 * 2))
                pe.wait_ge(sems["vec_norm"], at("qk", "ka", 0))
            elif k["cfg"][:4] == "diff":
                pe.wait_ge(sems["vec_drain"], at("fm", "q", int(k["cfg"][-1]), 6))
            else:
                pe.wait_ge(sems["vec_drain"], at("fm", "xq", int(k["cfg"][-1]), 6))
                pe.wait_ge(sems["vec_drain"], at("fm", "xk", int(k["cfg"][-1]), 6))
            for qt in range(2):
                nk = P * (qt + 1) if c["causal"] else T
                for m in range(c["maps"]):
                    ps = scores_at(c, qt, m, nk)
                    if c["pack"] == "cross":
                        for f in (0, 1):
                            mm = pe.matmul(ps, c["q"][0][f][:, qt * P:(qt + 1) * P], c["k"][0][f], start=f == 0,
                                           stop=f == 1)
                    else:
                        pe.matmul(ps, c["q"][m][:, qt * P:(qt + 1) * P], c["k"][m][:, 0:nk], start=True, stop=False)
                        mm = pe.matmul(ps, FLIP[:], c["hank"][:, c["head"][m], T - nk:T], start=False, stop=True)
            mm.then_inc(sems["pe_attn"], 1)
            up("pe_attn", ("scores", k["cfg"], k["i"]))

        def pe_turn(k):
            c = att(k["cfg"], k["i"])
            pe.wait_ge(sems["vec_attn"], at("probs", k["cfg"], k["i"]))
            for m in range(2 if c["pack"] == "pair" else 1):
                for kb in (0, 1):
                    for qt in ((0, 1) if kb == 0 or c["pack"] == "cross" else (1,)):
                        at_ = m * 384 + (qt * P if kb == 0 else 2 * P + (qt * P if c["pack"] == "cross" else 0))
                        mm = pe.transpose(TURN[:, at_:at_ + P], c["E"][:, qt, m, kb * P:(kb + 1) * P], IDENT[:])
            mm.then_inc(sems["pe_attn"], 1)
            up("pe_attn", ("turned", k["cfg"], k["i"]))

        def pe_pv(k):
            c = att(k["cfg"], k["i"])
            pe.wait_ge(sems["act_attn"], at("pt", k["cfg"], k["i"]))
            if k["cfg"][:4] != "diff":
                pe.wait_ge(*done(("tm", {"swa": "va", "moba": "vc"}.get(k["cfg"], "xv"), 0 if k["cfg"] in ("swa", "moba") else int(k["cfg"][-1]))))
            PT = c["PT"]
            if c["pack"] == "cross":
                for f in (0, 1):
                    for kb in (0, 1):
                        mm = pe.matmul(PB[:, 0, f * T:(f + 1) * T], c["v"][f][kb], PT[:, kb * T:(kb + 1) * T],
                                       start=kb == 0, stop=kb == 1)
            else:
                for m in range(2 if c["pack"] == "pair" else 1):
                    o = PB[64 * m:64 * m + 64, 0, :] if c["pack"] == "pair" else PB[:, 0, :]
                    pe.matmul(o[:, 0:T], c["v"][m][0], PT[:, m * 384:m * 384 + T], start=True, stop=False)
                    mm = pe.matmul(o[:, P:T], c["v"][m][1], PT[:, m * 384 + T:m * 384 + T + P], start=False, stop=True)
            mm.then_inc(sems["pe_attn"], 1)
            up("pe_attn", ("o_ps", k["cfg"], k["i"]))
            state["att"] = (k["cfg"], k["i"])

        def pe_subln(k):
            stat_free(k["s"])
            pe.wait_ge(sems["act_attn"], at("o_sq", k["cfg"], k["i"]))
            mm = pe.matmul(STAT[:, 0:T], ONES[:], ASQ[:, k["i"] % 2, 0, :], start=True, stop=True)
            mm.then_inc(sems["pe_attn"], 1)
            up("pe_attn", ("stat", k["s"]))

        def pe_rnn_gate(k):
            stat_free(k["s"])
            pe.wait_ge(sems["vec_rnn"], at("xc", k["f"]))
            pe.wait_ge(sems["blocks_in"], at("blocks"))
            pe.wait_ge(sems["pool_setup"], at("bd_zero"))
            for g in range(2):
                mm = pe.matmul(STAT[:, g * T:(g + 1) * T], o_b1["bd"][:, k["f"], g, :], o_b1["xc"][:, k["f"], :],
                               start=True, stop=True)
            mm.then_inc(sems["pe_rnn"], 1)
            up("pe_rnn", ("gates", k["f"]))

        def pe_cln_mean(k):
            stat_free(k["s"])
            pe.wait_ge(sems["vec_conv"], at("conv", k["l"]))
            for f in range(NF):
                mm = pe.matmul(STAT[:, 0:T], ONES[:], Y[:, f, :], start=f == 0, stop=f == NF - 1)
            mm.then_inc(sems["pe_norm"], 1)
            up("pe_norm", ("stat", k["s"]))

        def pe_cln_var(k):
            stat_free(k["s"])
            pe.wait_ge(sems["act_conv"], at("cln_sq", k["l"]))
            for f in range(NF):
                mm = pe.matmul(STAT[:, 0:T], ONES[:], SQ[:, f, :], start=f == 0, stop=f == NF - 1)
            mm.then_inc(sems["pe_norm"], 1)
            up("pe_norm", ("stat", k["s"]))

        def pe_mem_turn(k):
            pe.wait_ge(sems["mem_in"], at("memt", k["l"]))
            if state["att"] is not None:
                pe.wait_ge(sems["vec_attn"], at("o_raw", *state["att"]))
                if state["att"][0][:4] == "diff":
                    pe.wait_ge(sems["act_attn"], at("o_sq", *state["att"]))
            for half in range(2):
                if half:
                    pe.wait_ge(sems["vec_norm"], at("memf", f"l{k['l']}", 0))
                for f in range(4):
                    for t in range(TT):
                        ff = 4 * half + f
                        mm = pe.transpose(PBF[:, f * T + t * P:f * T + (t + 1) * P],
                                          o_c["memt"][:, t, ff * P:(ff + 1) * P], IDENT[:])
                mm.then_inc(sems["pe_norm"], 1)
                up("pe_norm", ("mem_ps", k["l"], half))

        def pe_finish(k):
            pe.wait_ge(sems["vec_norm"], at("x", last_x, 3))
            for p in last_pairs:
                pe.wait_ge(sems["act_drain"], at("evac", p))
            for t in range(TT):
                for f in range(NF):
                    mm = pe.transpose(GPF[:, t * D + f * P:t * D + (f + 1) * P], X[:, f, t * P:(t + 1) * P], IDENT[:])
            mm.then_inc(sems["pe_setup"], 1)
            up("pe_setup", ("out_ps",))

        parts = dict(unit=pe_unit, params=pe_params, turn_x=pe_turn_x, mod=pe_mod, bias=pe_bias, stat=pe_stat, ystat=pe_ystat,
                     rstd_cols=pe_rstd_cols, qk_norm=pe_qk_norm, scores=pe_scores, turn=pe_turn, pv=pe_pv,
                     subln=pe_subln, rnn_gate=pe_rnn_gate, cln_mean=pe_cln_mean, cln_var=pe_cln_var,
                     mem_turn=pe_mem_turn, finish=pe_finish)
        for kind, k in steps:
            if kind in parts:
                parts[kind](k)

    @block.scalar
    def _(act):
        state = dict(rq=None)

        def hi(m):
            if m >= len(splits):
                return
            u = splits[m]
            act.wait_ge(*done(("landed", u["raw"])))
            if m >= SPLIT:
                act.wait_ge(sems["gemm_done"], at("unit", splits[m - SPLIT]["n"]))
            s = (slice(None), m % SPLIT, slice(0, u["nkt"]), slice(0, u["cols"]))
            act.copy(WH[s], RAWB[:, u["raw"] % RAW, 0:u["nkt"], 0:u["cols"]]).then_inc(sems["weights_rounded"], 1)
            act.wait_ge(sems["weights_rounded"], up("weights_rounded", ("rounded", m)))

        def rstd(dst, src, scale, eps, sem, name, s):
            act.activation(dst, src, ACT.Ln, bias=EPS[:, eps:eps + 1], scale=scale).then_inc(sems[sem], 1)
            act.wait_ge(sems[sem], up(sem, ("stat_read", s)))
            act.activation(dst, dst, ACT.Exp, scale=-0.5).then_inc(sems[sem], 1)
            act.wait_ge(sems[sem], up(sem, name))

        def act_setup(k):
            act.wait_ge(sems["c_in"], at("c_in"))
            act.activation(o_set["sgc"][:], o_set["c_cols"][:], ACT.Tanh, scale=0.5).then_inc(sems["act_setup"], 1)
            act.wait_ge(sems["act_setup"], up("act_setup", ("c_tanh",)))

        def act_params(k):
            act.wait_ge(sems["pe_setup"], at("rows_T", k["part"]))
            for i in ((0,) if k["part"] == 0 else range(1, len(ROW_TILES))):
                n, at_ = ROW_TILES[i][0], sum(m for m, _ in ROW_TILES[:i])
                act.copy(CT[:, at_:at_ + n], PBF[:, i * P:i * P + n]).then_inc(sems["act_setup"], 1)
                act.wait_ge(sems["act_setup"], up("act_setup", ("cols", k["part"])))
            if k["part"] == 0:
                act.activation(o_set["spt"][:, 0, :], col("lambda", 0, 8), ACT.Abs).then_inc(sems["act_setup"], 1)
                act.wait_ge(sems["act_setup"], up("act_setup"))
                act.activation(o_set["spt"][:, 0, :], o_set["spt"][:, 0, :], ACT.Exp, scale=-1.0).then_inc(sems["act_setup"], 1)
                act.wait_ge(sems["act_setup"], up("act_setup", ("sp_exp",)))
                act.mul(HALFB[:, 0:8], col("gate_a_b", 0, 8), 0.5).then_inc(sems["act_setup"], 1)
                act.wait_ge(sems["act_setup"], up("act_setup"))
                act.mul(HALFB[:, 8:16], col("gate_x_b", 0, 8), 0.5).then_inc(sems["act_setup"], 1)
                act.wait_ge(sems["act_setup"], up("act_setup", ("half_bias",)))
                act.wait_ge(sems["vec_setup"], at("lam_sum"))
                act.activation(o_set["lams"][:], o_set["lams"][:], ACT.Exp).then_inc(sems["act_setup"], 1)
                act.wait_ge(sems["act_setup"], up("act_setup", ("lam_exp",)))

        def act_bias(k):
            act.wait_ge(sems["pe_setup"], at("lines_ps"))
            for i in range(3):
                act.copy(o_set["lines"][:, i, :], PB[0:8, i, 0:LINE]).then_inc(sems["act_setup"], 1)
                act.wait_ge(sems["act_setup"], up("act_setup", ("lines_read",)))

        def act_square(k):
            src = BUF[k["src"]]
            for p in range(4):
                act.wait_ge(*done(("x", k["v"], p) if k["src"] == "x" else ("memf", k["key"][:2], p // 2)))
                act.activation(SQ[:, 2 * p:2 * p + 2, :], src[:, 2 * p:2 * p + 2, :], ACT.Square).then_inc(sems["act_norm"], 1)
                act.wait_ge(sems["act_norm"], up("act_norm", ("sq", k["key"], p)))

        def act_rstd(k):
            act.wait_ge(sems["pe_norm"], at("stat", k["s"]))
            rstd((RX if k["out"] == "RX" else RY)[:], STAT[:, 0:T], k["scale"], 0, "act_norm", ("rstd", k["key"]),
                 k["s"])

        def act_adapt(k):
            for f in range(NF):
                act.wait_ge(sems["vec_norm"], at("adapted", k["key"], f))
                if k["after"] is not None:
                    act.wait_ge(sems["gemm_done"], at("unit", k["after"]))
                act.activation(HH[:, f, :], Y[:, f, :], ACT.Identity, bias=MODC[:, 8 * k["shift"] + f:8 * k["shift"] + f + 1]).then_inc(sems["act_split"], 1)
                act.wait_ge(sems["act_split"], up("act_split", ("split_hi", "H", k["key"], f)))

        def act_split(k):
            h = xbuf(k["buf"], k["gen"])[0]
            f = k["f"]
            act.wait_ge(*done(ready_of(k)))
            if k["after"] is not None:
                act.wait_ge(sems["gemm_done"], at("unit", k["after"]))
            src = source(k)
            c = k.get("col")
            scale = 0.5 if k.get("half") else 1.0
            act.activation(h[:, k["ft0"] + f, :], src, ACT.Copy, scale=col(c[0], c[1] + f) if c else scale).then_inc(sems["act_split"], 1)
            act.wait_ge(sems["act_split"], up("act_split", ("split_hi", k["buf"], k["gen"], k["ft0"] + f)))

        def act_evac_y(k):
            act.wait_ge(sems["gemm_done"], at("unit", k["last_unit"]))
            ft = k["ft"]
            act.copy(Y[:, ft:ft + 2, :], slot(k["id"])).then_inc(sems["act_drain"], 1)
            act.wait_ge(sems["act_drain"], up("act_drain", ("evac", k["id"]) if k["sq"] is None else None))
            mark(("y", k["yk"], ft // 2), "act_drain")
            if k["sq"] is not None:
                act.activation(SQ[:, ft:ft + 2, :], slot(k["id"]), ACT.Square).then_inc(sems["act_drain"], 1)
                act.wait_ge(sems["act_drain"], up("act_drain", ("evac", k["id"])))
                mark(("sqy", k["sq"], ft // 2), "act_drain")

        def act_evac_qk(k):
            act.wait_ge(sems["gemm_done"], at("unit", k["last_unit"]))
            b = k["b"]
            if k["before"] is not None:
                act.wait_ge(sems["pe_norm"], at("stat", k["before"]))
            act.activation(ASQ[:, b], slot(k["id"]), ACT.Square).then_inc(sems["act_drain"], 1)
            act.wait_ge(sems["act_drain"], up("act_drain"))
            mark(("asq", k["dst"], k["ft"]), "act_drain")

        def act_qk_norm(k):
            act.wait_ge(sems["pe_norm"], at("stat", k["s"]))
            if state["rq"] is not None:
                act.wait_ge(*done(state["rq"]))
            rstd(RQ[:].rearrange("p a t -> p (a t)"), STAT[:, :], 1.0 / HD, 0, "act_norm", ("rstd_q", k["s"]), k["s"])
            state["rq"] = ("rq_read", k["s"])

        def act_evac_v1(k):
            act.wait_ge(sems["gemm_done"], at("unit", k["last_unit"]))
            act.copy(BUF[k["dst"]][:, :, k["c0"]:k["c0"] + k["cols"]], GP[:, k["id"] % 2, :, 0:k["cols"]]).then_inc(sems["act_drain"], 1)
            act.wait_ge(sems["act_drain"], up("act_drain", ("evac", k["id"])))
            mark(("tm", k["dst"], 0), "act_drain")

        def act_softmax(k):
            c = att(k["cfg"], k["i"])
            act.wait_ge(sems["vec_attn"], at("max", k["cfg"], k["i"]))
            for qt in range(2):
                nk = P * (qt + 1) if c["causal"] else T
                for m in range(c["maps"]):
                    j = 2 * qt + m
                    act.activation(c["E"][:, qt, m, 0:nk], scores_at(c, qt, m, nk), ACT.Exp, bias=NM[:, j:j + 1], accum_out=DEN[:, j:j + 1]).then_inc(sems["act_attn"], 1)
                    act.wait_ge(sems["act_attn"], up("act_attn", ("exps", k["cfg"], k["i"])))
            if k["cfg"] == "swa":
                act.activation(ES[:], ES[:], ACT.Exp).then_inc(sems["act_attn"], 1)
                act.wait_ge(sems["act_attn"], up("act_attn", ("sink_exp", k["cfg"], k["i"])))

        def act_turn(k):
            c = att(k["cfg"], k["i"])
            act.wait_ge(sems["pe_attn"], at("turned", k["cfg"], k["i"]))
            n = {"pair": 768, "diff": 384, "cross": 512}[c["pack"]]
            act.copy(c["PT"][:, 0:n], TURN[:, 0:n]).then_inc(sems["act_attn"], 1)
            act.wait_ge(sems["act_attn"], up("act_attn", ("pt", k["cfg"], k["i"])))

        def act_pv(k):
            if k["cfg"][:4] == "diff":
                act.wait_ge(sems["pe_attn"], at("o_ps", k["cfg"], k["i"]))
                act.activation(ASQ[:, k["i"] % 2, 0, :], PB[:, 0, 0:T], ACT.Square).then_inc(sems["act_attn"], 1)
                act.wait_ge(sems["act_attn"], up("act_attn", ("o_sq", k["cfg"], k["i"])))

        def act_subln(k):
            act.wait_ge(sems["pe_attn"], at("stat", k["s"]))
            if state["rq"] is not None:
                act.wait_ge(*done(state["rq"]))
            rstd(RQ[:, 0, :], STAT[:, 0:T], 1.0 / (2 * HD), 0, "act_attn", ("rstd_q", k["s"]), k["s"])
            state["rq"] = ("rq_read", k["s"])

        def act_evac_xr(k):
            act.wait_ge(sems["gemm_done"], at("unit", k["last_unit"]))
            act.wait_ge(sems["vec_rnn"], at("pads1"))
            act.copy(o_b1["xr"][:, k["ft"]:k["ft"] + 2, RNN_K - 1:], slot(k["id"])).then_inc(sems["act_drain"], 1)
            act.wait_ge(sems["act_drain"], up("act_drain", ("evac", k["id"])))
            mark(("xr", k["ft"]), "act_drain")

        def act_evac_yr(k):
            act.wait_ge(sems["gemm_done"], at("unit", k["last_unit"]))
            s = slice(k["ft"], k["ft"] + 2)
            act.copy(Y[:, s, :], slot(k["id"])).then_inc(sems["act_drain"], 1)
            act.wait_ge(sems["act_drain"], up("act_drain"))
            act.activation(SQ[:, s, :], slot(k["id"]), ACT.Square).then_inc(sems["act_drain"], 1)
            act.wait_ge(sems["act_drain"], up("act_drain", ("evac", k["id"])))
            act.wait_ge(sems["vec_gelu"], at("gelu_in", k["ft"]))
            act.activation(SQ[:, s, :], SQ[:, s, :], ACT.Tanh).then_inc(sems["act_gelu"], 1)
            act.wait_ge(sems["act_gelu"], up("act_gelu", ("gelu_tanh", k["ft"])))

        def act_rnn_gate(k):
            f = k["f"]
            act.wait_ge(sems["pe_rnn"], at("gates", f))
            act.wait_ge(sems["act_setup"], at("half_bias"))
            if f:
                act.wait_ge(sems["vec_rnn"], at("rnn_in", f - 1))
            for g in range(2):
                act.activation(o_b1["rg"][:, g, :], STAT[:, g * T:(g + 1) * T], ACT.Tanh, scale=0.5, bias=HALFB[:, 8 * g + f:8 * g + f + 1]).then_inc(sems["act_rnn"], 1)
                act.wait_ge(sems["act_rnn"], up("act_rnn", ("stat_read", k["s"])))
            mark(("gate_tanh", "rnn", f), "act_rnn")

        def act_rnn_in(k):
            f = k["f"]
            act.wait_ge(sems["vec_rnn"], at("s", f))
            act.activation(o_b1["xr"][:, f, 0:T], o_b1["s_all"][:, f, :], ACT.Exp, scale=-1.0).then_inc(sems["act_rnn"], 1)
            act.wait_ge(sems["act_rnn"], up("act_rnn"))
            act.activation(o_b1["tmp1"][:, f, :], o_b1["s_all"][:, f, :], ACT.Tanh).then_inc(sems["act_rnn"], 1)
            act.wait_ge(sems["act_rnn"], up("act_rnn", ("a", f)))

        def act_rnn_scan(k):
            for h in range(2):
                s = slice(4 * h, 4 * h + 4)
                act.wait_ge(sems["vec_rnn"], at("m2", 4 * h + 3))
                act.activation(o_b1["tmp1"][:, s, :], o_b1["tmp1"][:, s, :], ACT.Sqrt, scale=0.25).then_inc(sems["act_rnn"], 1)
                act.wait_ge(sems["act_rnn"], up("act_rnn", ("mult", h)))

        def act_evac_gate(k):
            gt = (o_b1["gt1"] if not k["scaled"] else o_m["gt2"])[:, (k["id"] // 2) % 2]
            if k["scaled"]:
                act.wait_ge(sems["vec_drain"], at("evac", k["id"]))
                act.activation(gt, gt, ACT.Tanh, scale=0.5).then_inc(sems["act_drain"], 1)
                act.wait_ge(sems["act_drain"], up("act_drain", ("gate_tanh", k["id"])))
            else:
                act.wait_ge(sems["gemm_done"], at("unit", k["last_unit"]))
                act.wait_ge(*done(("evac", k["id"] - 3)))
                act.activation(gt, slot(k["id"]), ACT.Tanh, scale=0.5).then_inc(sems["act_drain"], 1)
                act.wait_ge(sems["act_drain"], up("act_drain", ("evac", k["id"])))
                marks[("gate_tanh", k["id"])] = marks[("evac", k["id"])]

        def act_ffn_gate(k):
            b = k["j"] % 2
            act.wait_ge(sems["vec_ffn"], at("evac", k["id"]))
            act.activation(o_f2["fe"][:, b], o_f2["fa"][:, b], ACT.Tanh, scale=0.5).then_inc(sems["act_ffn"], 1)
            act.wait_ge(sems["act_ffn"], up("act_ffn", ("ffn_tanh", k["x"][1], k["j"])))

        def act_up1(k):
            act.wait_ge(sems["gemm_done"], at("unit", k["last_unit"]))
            act.wait_ge(sems["vec_ffn"], at("pads_f1"))
            act.copy(o_f1["up"][:, k["val"], :, FFN_K - 1:], slot(k["id"])).then_inc(sems["act_drain"], 1)
            act.wait_ge(sems["act_drain"], up("act_drain", ("evac", k["id"])))
            if k["val"] == 0:
                act.wait_ge(sems["vec_ffn"], at("conv_gate", k["j"]))
                act.activation(o_f1["fe1"][:], o_f1["uc"][:, 0], ACT.Tanh, scale=0.5).then_inc(sems["act_ffn"], 1)
                act.wait_ge(sems["act_ffn"], up("act_ffn", ("ffn_tanh", "b1u", k["j"])))

        def act_hid_split(k):
            h = xbuf("HID", k["gen"])[0]
            src = o_f1["hf1"] if k["gen"] == "b1u" else o_f2["hf"]
            act.wait_ge(sems["vec_ffn"], at("hidden", k["gen"], k["j"]))
            act.copy(h[:, 2 * k["j"]:2 * k["j"] + 2, :], src[:, k["j"] % 2]).then_inc(sems["act_ffn"], 1)
            act.wait_ge(sems["act_ffn"], up("act_ffn", ("hid_hi", k["gen"], k["j"])))

        def act_conv31(k):
            f = k["f"]
            act.wait_ge(sems["vec_conv"], at("glu", k["l"], 6))
            if k["part"] == 0:
                act.activation(Y[:, f, :], o_m["zp"][:, f, 0:T], ACT.Identity, scale=col(f"dw{k['l']}", f), bias=col(f"dw_b{k['l']}", f)).then_inc(sems["act_conv"], 1)
                act.wait_ge(sems["act_conv"], up("act_conv", ("conv0", k["l"], f)))

        def act_cln_mean(k):
            act.wait_ge(sems["pe_norm"], at("stat", k["s"]))
            act.activation(RY[:], STAT[:, 0:T], ACT.Copy, scale=1.0 / D).then_inc(sems["act_conv"], 1)
            act.wait_ge(sems["act_conv"], up("act_conv", ("stat_read", k["s"])))
            mark(("mu", k["l"]), "act_conv")
            act.wait_ge(sems["vec_conv"], at("centred", k["l"]))
            act.activation(SQ[:], Y[:], ACT.Square).then_inc(sems["act_conv"], 1)
            act.wait_ge(sems["act_conv"], up("act_conv", ("cln_sq", k["l"])))

        def act_cln_var(k):
            act.wait_ge(sems["pe_norm"], at("stat", k["s"]))
            rstd(RY[:], STAT[:, 0:T], 1.0 / D, 1, "act_conv", ("cln_rstd", k["l"]), k["s"])

        def act_cln_out(k):
            for h in range(4):
                s = slice(2 * h, 2 * h + 2)
                act.wait_ge(sems["vec_conv"], at("cln_v", k["l"], h))
                act.activation(Y[:, s, :], o_m["tmp2"][:, s, :], ACT.Tanh, scale=0.5).then_inc(sems["act_conv"], 1)
                act.wait_ge(sems["act_conv"], up("act_conv", ("cln_tanh", k["l"], h)))

        def act_evac_pool_w(k):
            l, g = k["l"], k["g"]
            act.wait_ge(sems["gemm_done"], at("unit", k["last_unit"]))
            for i in range(2):
                f = 2 * g + i
                act.activation(o_m["gh2"][:, f, :], slot(k["id"])[:, i, :], ACT.Copy, scale=col(f"pscale{l}", f)).then_inc(sems["act_split"], 1)
                act.wait_ge(sems["act_split"], up("act_split", ("split_hi", "G", f"l{l}mq", f)))

        def act_finish(k):
            act.wait_ge(sems["pe_setup"], at("out_ps"))
            act.copy(o_o["otok"][:].rearrange("p t d -> p (t d)"), GPF).then_inc(sems["act_setup"], 1)
            act.wait_ge(sems["act_setup"], up("act_setup", ("otok",)))

        parts = dict(setup=act_setup, params=act_params, bias=act_bias, square=act_square, rstd=act_rstd, adapt=act_adapt,
                     split=act_split, evac_y=act_evac_y, evac_qk=act_evac_qk, qk_norm=act_qk_norm,
                     evac_v1=act_evac_v1, softmax=act_softmax, turn=act_turn, pv=act_pv, subln=act_subln,
                     evac_xr=act_evac_xr, evac_yr=act_evac_yr, rnn_gate=act_rnn_gate, rnn_in=act_rnn_in,
                     rnn_scan=act_rnn_scan, evac_gate=act_evac_gate, evac_ffn_gate=act_ffn_gate, evac_up1=act_up1,
                     hid_split=act_hid_split, conv31=act_conv31, cln_mean=act_cln_mean, cln_var=act_cln_var,
                     cln_out=act_cln_out, evac_pool_w=act_evac_pool_w, finish=act_finish)
        for kind, k in steps:
            if kind == "presplit":
                hi(k["m"])
            if kind == "unit":
                hi(k["m"] + AHEAD)
            if kind in parts:
                parts[kind](k)

    @block.vector
    def _(dve):
        def lo(m):
            if m >= len(splits):
                return
            u = splits[m]
            dve.wait_ge(sems["weights_rounded"], at("rounded", m))
            s = (slice(None), m % SPLIT, slice(0, u["nkt"]), slice(0, u["cols"]))
            dve.tensor_tensor(WL[s], RAWB[:, u["raw"] % RAW, 0:u["nkt"], 0:u["cols"]], WH[s], ALU.subtract).then_inc(sems["weights_rest"], 1)
            dve.wait_ge(sems["weights_rest"], up("weights_rest", ("rest", m)))
            mark(("free", u["raw"]), "weights_rest")

        def vec_setup(k):
            V = "vec_setup"
            dve.wait_ge(sems["act_setup"], at("c_tanh"))
            sg = o_set["sgc"][:]
            dve.scalar_tensor_tensor(out=sg, in0=sg, scalar=1.0, in1=o_set["c_cols"][:], op0=ALU.add, op1=ALU.mult).then_inc(sems["vec_setup"], 1)
            dve.wait_ge(sems["vec_setup"], up("vec_setup"))
            dve.tensor_scalar(CC[:], sg, 0.5, None, ALU.mult).then_inc(sems["vec_setup"], 1)
            dve.wait_ge(sems["vec_setup"], up("vec_setup", ("cc",)))
            dve.memset(ONES[:], 1.0).then_inc(sems["vec_setup"], 1)
            dve.wait_ge(sems["vec_setup"], up("vec_setup", ("ones",)))
            dve.memset(EPS[:, 0:1], RMS_EPS).then_inc(sems["vec_setup"], 1)
            dve.wait_ge(sems["vec_setup"], up("vec_setup"))
            dve.memset(EPS[:, 1:2], LN_EPS).then_inc(sems["vec_setup"], 1)
            dve.wait_ge(sems["vec_setup"], up("vec_setup", ("eps",)))
            dve.memset(o_set["relb"][32:33, :], 1.0).then_inc(sems["vec_setup"], 1)
            dve.wait_ge(sems["vec_setup"], up("vec_setup", ("relb",)))
            dve.wait_ge(sems["small_in"], at("small"))
            dve.tensor_scalar(SINK[:], o_set["sinks_in"][:], -1.0, None, ALU.mult).then_inc(sems["vec_setup"], 1)
            dve.wait_ge(sems["vec_setup"], up("vec_setup"))
            lam = o_set["lamb"][:].rearrange("p (a two d) -> p a two d", two=2, d=HD)
            dve.tensor_tensor(o_set["lamp"][:], lam[:, :, 0, :], lam[:, :, 1, :], ALU.mult).then_inc(sems["vec_setup"], 1)
            dve.wait_ge(sems["vec_setup"], up("vec_setup"))
            dve.tensor_reduce(o_set["lams"][:], o_set["lamp"][:], AX_X, ALU.add).then_inc(sems["vec_setup"], 1)
            dve.wait_ge(sems["vec_setup"], up("vec_setup", ("lam_sum",)))

        def vec_turn_x(k):
            V = "vec_setup"
            dve.wait_ge(sems["pe_setup"], at("x_T"))
            for p in range(4):
                dve.tensor_copy(X[:, 2 * p:2 * p + 2, :].rearrange("p f t -> p (f t)"), GPF[:, 2 * p * T:(2 * p + 2) * T]).then_inc(sems["vec_setup"], 1)
                dve.wait_ge(sems["vec_setup"], up("vec_setup", ("x", 0, p)))
            dve.wait_ge(sems["act_setup"], at("sp_exp"))
            e, y, y2, s, t = (o_set["spt"][:, i, :] for i in range(5))
            dve.tensor_scalar(y, e, 2.0, None, ALU.add).then_inc(sems["vec_setup"], 1)
            dve.wait_ge(sems["vec_setup"], up("vec_setup"))
            dve.reciprocal(y, y).then_inc(sems["vec_setup"], 1)
            dve.wait_ge(sems["vec_setup"], up("vec_setup"))
            dve.tensor_tensor(y, y, e, ALU.mult).then_inc(sems["vec_setup"], 1)
            dve.wait_ge(sems["vec_setup"], up("vec_setup"))
            dve.tensor_tensor(y2, y, y, ALU.mult).then_inc(sems["vec_setup"], 1)
            dve.wait_ge(sems["vec_setup"], up("vec_setup"))
            dve.memset(s, 1.0 / 21).then_inc(sems["vec_setup"], 1)
            dve.wait_ge(sems["vec_setup"], up("vec_setup"))
            for n in range(19, 0, -2):
                dve.tensor_tensor(s, s, y2, ALU.mult).then_inc(sems["vec_setup"], 1)
                dve.wait_ge(sems["vec_setup"], up("vec_setup"))
                dve.tensor_scalar(s, s, 1.0 / n, None, ALU.add).then_inc(sems["vec_setup"], 1)
                dve.wait_ge(sems["vec_setup"], up("vec_setup"))
            dve.tensor_tensor(s, s, y, ALU.mult).then_inc(sems["vec_setup"], 1)
            dve.wait_ge(sems["vec_setup"], up("vec_setup"))
            dve.tensor_scalar(t, col("lambda", 0, 8), -1.0, 0.0, ALU.mult, ALU.max).then_inc(sems["vec_setup"], 1)
            dve.wait_ge(sems["vec_setup"], up("vec_setup"))
            dve.scalar_tensor_tensor(out=s, in0=s, scalar=2.0, in1=t, op0=ALU.mult, op1=ALU.add).then_inc(sems["vec_setup"], 1)
            dve.wait_ge(sems["vec_setup"], up("vec_setup"))
            dve.tensor_scalar(SP4[:], s, RGLRU_C / 2, None, ALU.mult).then_inc(sems["vec_setup"], 1)
            dve.wait_ge(sems["vec_setup"], up("vec_setup"))
            dve.wait_ge(sems["act_setup"], at("lam_exp"))
            e_ = o_set["lams"]
            for l in range(LAYERS):
                dve.tensor_tensor(LAM[:, l:l + 1], e_[:, 2 * l + 1:2 * l + 2], e_[:, 2 * l:2 * l + 1], ALU.subtract).then_inc(sems["vec_setup"], 1)
                dve.wait_ge(sems["vec_setup"], up("vec_setup"))
                dve.tensor_scalar(LAM[:, l:l + 1], LAM[:, l:l + 1], -lam_init(l), None, ALU.add).then_inc(sems["vec_setup"], 1)
                dve.wait_ge(sems["vec_setup"], up("vec_setup", ("setup_end",)))

        def vec_params(k):
            if k["part"] == 0:
                return
            V = "vec_setup"
            dve.wait_ge(sems["act_setup"], at("cols", 1))
            g = col("qk_gain", 0, 4)
            for i, by in enumerate((HD ** -0.5, 1.0, HD ** -0.5, 1.0)):
                dve.tensor_scalar(QG[:, i:i + 1], g[:, i:i + 1], by, None, ALU.mult).then_inc(sems["vec_setup"], 1)
                dve.wait_ge(sems["vec_setup"], up("vec_setup"))
            for l in range(LAYERS):
                dve.tensor_scalar(col(f"subln{l}"), col(f"subln{l}"), 1.0 - lam_init(l), None, ALU.mult).then_inc(sems["vec_setup"], 1)
                dve.wait_ge(sems["vec_setup"], up("vec_setup"))

        def vec_mod_sum(k):
            s = slice(k["first"], k["first"] + k["count"])
            dve.wait_ge(sems["pe_mod"], at("mod_ps", s.stop - 1))
            dve.wait_ge(sems["act_setup"], at("cols", 0))
            dve.tensor_tensor(MODC[:, s], STAT[:, 0:k["count"]], col("b_mod", k["first"], k["count"]), ALU.add).then_inc(sems["vec_mod"], 1)
            dve.wait_ge(sems["vec_mod"], up("vec_mod", ("stat_read", k["s"])))

        def vec_adapt(k):
            V = "vec_norm"
            a8 = RT8[:]
            dve.tensor_scalar(a8, MODC[:, 8 * k["scale"]:8 * k["scale"] + 8], 1.0, None, ALU.add).then_inc(sems["vec_norm"], 1)
            dve.wait_ge(sems["vec_norm"], up("vec_norm"))
            dve.tensor_tensor(a8, a8, col(k["norm"], 0, 8), ALU.mult).then_inc(sems["vec_norm"], 1)
            dve.wait_ge(sems["vec_norm"], up("vec_norm"))
            dve.wait_ge(sems["act_norm"], at("rstd", k["rstd"]))
            dve.wait_ge(sems["line_out"], at("lines_out"))
            for f in range(NF):
                dve.scalar_tensor_tensor(out=Y[:, f, :], in0=X[:, f, :], scalar=a8[:, f:f + 1], in1=RX[:], op0=ALU.mult, op1=ALU.mult).then_inc(sems["vec_norm"], 1)
                dve.wait_ge(sems["vec_norm"], up("vec_norm", ("adapted", k["key"], f)))
            for f in range(NF):
                dve.wait_ge(sems["act_split"], at("split_hi", "H", k["key"], f))
                c = 8 * k["shift"] + f
                dve.scalar_tensor_tensor(out=HL[:, f, :], in0=Y[:, f, :], scalar=MODC[:, c:c + 1], in1=HH[:, f, :], op0=ALU.add, op1=ALU.subtract).then_inc(sems["vec_norm"], 1)
                dve.wait_ge(sems["vec_norm"], up("vec_norm", ("split", "H", k["key"], f)))

        def vec_split(k):
            h, l_ = xbuf(k["buf"], k["gen"])
            f, d = k["f"], k["ft0"] + k["f"]
            src = source(k)
            c = k.get("col")
            dve.wait_ge(sems["act_split"], at("split_hi", k["buf"], k["gen"], d))
            if c or k.get("half"):
                ins = dve.scalar_tensor_tensor(out=l_[:, d, :], in0=src, scalar=col(c[0], c[1] + f) if c else 0.5,
                                               in1=h[:, d, :], op0=ALU.mult, op1=ALU.subtract)
            else:
                ins = dve.tensor_tensor(l_[:, d, :], src, h[:, d, :], ALU.subtract)
            ins.then_inc(sems["vec_split"], 1)
            dve.wait_ge(sems["vec_split"], up("vec_split", ("split", k["buf"], k["gen"], d)))

        def vec_residual(k):
            for p in range(4):
                dve.wait_ge(sems["act_drain"], at("y", k["key"], p))
                if k["form"] == "gate_mod":
                    for f in (2 * p, 2 * p + 1):
                        c = 8 * k["chunk"] + f
                        dve.scalar_tensor_tensor(out=X[:, f, :], in0=Y[:, f, :], scalar=MODC[:, c:c + 1], in1=X[:, f, :], op0=ALU.mult, op1=ALU.add).then_inc(sems["vec_norm"], 1)
                        dve.wait_ge(sems["vec_norm"], up("vec_norm", ("x", k["v"], p)))
                else:
                    dve.wait_ge(sems["act_norm"], at("rstd", k["key"] + "y"))
                    for f in (2 * p, 2 * p + 1):
                        dve.scalar_tensor_tensor(out=Y[:, f, :], in0=Y[:, f, :], scalar=col(k["col"][0], k["col"][1] + f), in1=RY[:], op0=ALU.mult, op1=ALU.mult).then_inc(sems["vec_norm"], 1)
                        dve.wait_ge(sems["vec_norm"], up("vec_norm"))
                    s = slice(2 * p, 2 * p + 2)
                    dve.scalar_tensor_tensor(out=X[:, s, :], in0=Y[:, s, :], scalar=0.5 if k["half"] else 1.0, in1=X[:, s, :], op0=ALU.mult, op1=ALU.add).then_inc(sems["vec_norm"], 1)
                    dve.wait_ge(sems["vec_norm"], up("vec_norm", ("x", k["v"], p)))

        def vec_rstd_cols(k):
            dve.wait_ge(sems["pe_norm"], at("rt_ps", k["s"]))
            dve.tensor_copy(RT[:], STAT.rearrange("p (t q) -> p t q", q=P)[:, 0:TT, 0]).then_inc(sems["vec_norm"], 1)
            dve.wait_ge(sems["vec_norm"], up("vec_norm", ("stat_read", k["s"])))

        def vec_evac_qk(k):
            dve.wait_ge(sems["act_drain"], at("asq", k["dst"], k["ft"]))
            dve.tensor_copy(BUF[k["dst"]][:, k["ft"]:k["ft"] + 2, :], slot(k["id"])).then_inc(sems["vec_drain"], 1)
            dve.wait_ge(sems["vec_drain"], up("vec_drain", ("evac", k["id"])))

        def vec_qk_norm(k):
            d = BUF[k["dst"]][:, k["ft"]:k["ft"] + 2, :]
            dve.wait_ge(sems["act_norm"], at("rstd_q", k["s"]))
            dve.scalar_tensor_tensor(out=d, in0=d, scalar=QG[:, k["gain"]:k["gain"] + 1], in1=RQ[:], op0=ALU.mult, op1=ALU.mult).then_inc(sems["vec_norm"], 1)
            dve.wait_ge(sems["vec_norm"], up("vec_norm", ("rq_read", k["s"])))
            mark(("qk", k["dst"], k["ft"]), "vec_norm")

        def vec_scaled(k):
            dve.wait_ge(sems["gemm_done"], at("unit", k["last_unit"]))
            dve.wait_ge(sems["act_norm"], at("rstd", k["x"][1]))
            dve.scalar_tensor_tensor(out=BUF[k["dst"]][:, k["ft"]:k["ft"] + 2, :], in0=slot(k["id"]), scalar=k["by"], in1=bc(RX[:]), op0=ALU.mult, op1=ALU.mult).then_inc(sems["vec_drain"], 1)
            dve.wait_ge(sems["vec_drain"], up("vec_drain", ("evac", k["id"])))
            mark(("fm", k["dst"], k["l"], k["ft"]), "vec_drain")

        def vec_v2(k):
            dve.wait_ge(sems["gemm_done"], at("unit", k["last_unit"]))
            for t in range(TT):
                dve.tensor_scalar(BUF[k["dst"]][:, t, k["c0"]:k["c0"] + COLS], slot(k["id"])[:, t, :], RT[:, t:t + 1], None, ALU.mult).then_inc(sems["vec_drain"], 1)
                dve.wait_ge(sems["vec_drain"], up("vec_drain", ("evac", k["id"])))
            mark(("tm", k["dst"], k["l"]), "vec_drain")

        def vec_softmax(k):
            V, c = "vec_attn", att(k["cfg"], k["i"])
            M = c["maps"]
            dve.wait_ge(sems["pe_attn"], at("scores", k["cfg"], k["i"]))
            for qt in range(2):
                nk = P * (qt + 1) if c["causal"] else T
                dve.tensor_reduce(NM[:, 2 * qt:2 * qt + M], PB[:, 0:2, P * qt:P * qt + nk] if M == 2 else PB[:, qt, 0:nk], AX_X, ALU.max, negate=True).then_inc(sems["vec_attn"], 1)
                dve.wait_ge(sems["vec_attn"], up("vec_attn", ("max", k["cfg"], k["i"])))
            sink = k["cfg"] == "swa"
            if sink:
                i = k["i"]
                for qt in range(2):
                    j = slice(2 * qt, 2 * qt + 2)
                    dve.tensor_tensor(NM[:, j], NM[:, j], SINK[:, 2 * i:2 * i + 2], ALU.min).then_inc(sems["vec_attn"], 1)
                    dve.wait_ge(sems["vec_attn"], up("vec_attn"))
                for qt in range(2):
                    j = slice(2 * qt, 2 * qt + 2)
                    dve.tensor_tensor(ES[:, j], NM[:, j], SINK[:, 2 * i:2 * i + 2], ALU.subtract).then_inc(sems["vec_attn"], 1)
                    dve.wait_ge(sems["vec_attn"], up("vec_attn", ("max", k["cfg"], k["i"])))
                dve.wait_ge(sems["act_attn"], at("sink_exp", k["cfg"], k["i"]))
            dve.wait_ge(sems["act_attn"], at("exps", k["cfg"], k["i"]))
            js = slice(0, 4) if M == 2 else slice(0, 3, 2)
            if sink:
                dve.tensor_tensor(DEN[:], DEN[:], ES[:], ALU.add).then_inc(sems["vec_attn"], 1)
                dve.wait_ge(sems["vec_attn"], up("vec_attn"))
            dve.reciprocal(RD[:, js], DEN[:, js]).then_inc(sems["vec_attn"], 1)
            dve.wait_ge(sems["vec_attn"], up("vec_attn"))
            E = c["E"]
            if c["pack"] == "diff":
                l = int(k["cfg"][-1])
                dve.tensor_scalar(RD[:, 1:4:2], RD[:, 1:4:2], LAM[:, l:l + 1], None, ALU.mult).then_inc(sems["vec_attn"], 1)
                dve.wait_ge(sems["vec_attn"], up("vec_attn"))
                for qt in range(2):
                    nk = P * (qt + 1)
                    dve.tensor_scalar(E[:, qt, 1, 0:nk], E[:, qt, 1, 0:nk], RD[:, 2 * qt + 1:2 * qt + 2], None, ALU.mult).then_inc(sems["vec_attn"], 1)
                    dve.wait_ge(sems["vec_attn"], up("vec_attn"))
                    dve.scalar_tensor_tensor(out=E[:, qt, 0, 0:nk], in0=E[:, qt, 0, 0:nk], scalar=RD[:, 2 * qt:2 * qt + 1], in1=E[:, qt, 1, 0:nk], op0=ALU.mult, op1=ALU.add).then_inc(sems["vec_attn"], 1)
                    dve.wait_ge(sems["vec_attn"], up("vec_attn", ("probs", k["cfg"], k["i"])))
            else:
                for qt in range(2):
                    nk = P * (qt + 1) if c["causal"] else T
                    for m in range(M):
                        j = 2 * qt + m
                        dve.tensor_scalar(E[:, qt, m, 0:nk], E[:, qt, m, 0:nk], RD[:, j:j + 1], None, ALU.mult).then_inc(sems["vec_attn"], 1)
                        dve.wait_ge(sems["vec_attn"], up("vec_attn", ("probs", k["cfg"], k["i"])))

        def vec_pv(k):
            c = att(k["cfg"], k["i"])
            dve.wait_ge(sems["pe_attn"], at("o_ps", k["cfg"], k["i"]))
            if c["pack"] == "diff":
                dve.wait_ge(sems["act_attn"], at("o_sq", k["cfg"], k["i"]))
            src = PB[:, 0, 0:T] if c["pack"] != "cross" else PB[:, 0, :].rearrange("p (f t) -> p f t", f=2)
            dve.tensor_copy(c["o"], src).then_inc(sems["vec_attn"], 1)
            dve.wait_ge(sems["vec_attn"], up("vec_attn", ("o_raw", k["cfg"], k["i"])))
            if c["pack"] != "diff":
                mark(("o", k["cfg"], k["i"]), "vec_attn")

        def vec_subln(k):
            o = att(k["cfg"], k["i"])["o"]
            dve.wait_ge(sems["act_attn"], at("rstd_q", k["s"]))
            dve.scalar_tensor_tensor(out=o, in0=o, scalar=col("subln" + k["cfg"][-1]), in1=RQ[:, 0, :], op0=ALU.mult, op1=ALU.mult).then_inc(sems["vec_attn"], 1)
            dve.wait_ge(sems["vec_attn"], up("vec_attn", ("rq_read", k["s"])))
            mark(("o", k["cfg"], k["i"]), "vec_attn")

        def vec_pads1(k):
            dve.wait_ge(sems["vec_norm"], at("split", "H", "b1h", 7))
            dve.memset(o_b1["xr"][:, :, 0:RNN_K - 1], 0.0).then_inc(sems["vec_rnn"], 1)
            dve.wait_ge(sems["vec_rnn"], up("vec_rnn", ("pads1",)))

        def vec_pads_f1(k):
            dve.memset(o_f1["up"][:, :, :, 0:FFN_K - 1], 0.0).then_inc(sems["vec_ffn"], 1)
            dve.wait_ge(sems["vec_ffn"], up("vec_ffn", ("pads_f1",)))

        def vec_rnn_conv(k):
            f, V = k["f"], "vec_rnn"
            dve.wait_ge(sems["act_drain"], at("xr", f // 2 * 2))
            xr, xc = o_b1["xr"], o_b1["xc"]
            dve.tensor_scalar(xc[:, f, :], xr[:, f, 0:T], col("rnn_conv_w", f), col("rnn_conv_b", f), ALU.mult, ALU.add).then_inc(sems["vec_rnn"], 1)
            dve.wait_ge(sems["vec_rnn"], up("vec_rnn"))
            for j in range(1, RNN_K):
                dve.scalar_tensor_tensor(out=xc[:, f, :], in0=xr[:, f, j:j + T], scalar=col("rnn_conv_w", 8 * j + f), in1=xc[:, f, :], op0=ALU.mult, op1=ALU.add).then_inc(sems["vec_rnn"], 1)
                dve.wait_ge(sems["vec_rnn"], up("vec_rnn", ("xc", f)))

        def vec_rnn_in(k):
            f, V = k["f"], "vec_rnn"
            dve.wait_ge(sems["act_rnn"], at("gate_tanh", "rnn", f))
            rg, t, s, xc = o_b1["rg"], o_b1["tmp1"][:, f, :], o_b1["s_all"][:, f, :], o_b1["xc"][:, f, :]
            dve.tensor_scalar(s, rg[:, 0, :], 1.0, SP4[:, f:f + 1], ALU.add, ALU.mult).then_inc(sems["vec_rnn"], 1)
            dve.wait_ge(sems["vec_rnn"], up("vec_rnn", ("s", f)))
            dve.scalar_tensor_tensor(out=xc, in0=rg[:, 1, :], scalar=1.0, in1=xc, op0=ALU.add, op1=ALU.mult).then_inc(sems["vec_rnn"], 1)
            dve.wait_ge(sems["vec_rnn"], up("vec_rnn", ("rnn_in", f)))

        def vec_rnn_mult(k):
            f, V = k["f"], "vec_rnn"
            t, s, av = o_b1["tmp1"][:, f, :], o_b1["s_all"][:, f, :], o_b1["xr"][:, f, 0:T]
            dve.wait_ge(sems["act_rnn"], at("a", f))
            dve.tensor_tensor(s, av, av, ALU.mult).then_inc(sems["vec_rnn"], 1)
            dve.wait_ge(sems["vec_rnn"], up("vec_rnn"))
            dve.scalar_tensor_tensor(out=t, in0=s, scalar=1.0, in1=t, op0=ALU.add, op1=ALU.mult).then_inc(sems["vec_rnn"], 1)
            dve.wait_ge(sems["vec_rnn"], up("vec_rnn"))
            dve.tensor_scalar(t, t, 1e-34, None, ALU.max).then_inc(sems["vec_rnn"], 1)
            dve.wait_ge(sems["vec_rnn"], up("vec_rnn", ("m2", f)))

        def vec_rnn_scan(k):
            V = "vec_rnn"
            t, s, xc = o_b1["tmp1"], o_b1["s_all"], o_b1["xc"]
            for h in range(2):
                dve.wait_ge(sems["act_rnn"], at("mult", h))
                dve.wait_ge(sems["act_gelu"], at("gelu_tanh", 6))
                dve.memset(t[:, 4 * h:4 * h + 4, 0:1], 0.5).then_inc(sems["vec_rnn"], 1)
                dve.wait_ge(sems["vec_rnn"], up("vec_rnn"))
                for f in range(4 * h, 4 * h + 4):
                    dve.tensor_tensor(xc[:, f, :], xc[:, f, :], t[:, f, :], ALU.mult).then_inc(sems["vec_rnn"], 1)
                    dve.wait_ge(sems["vec_rnn"], up("vec_rnn"))
                    dve.tensor_tensor_scan(s[:, f, :], o_b1["xr"][:, f, 0:T], xc[:, f, :], 0.0, ALU.mult, ALU.add).then_inc(sems["vec_rnn"], 1)
                    dve.wait_ge(sems["vec_rnn"], up("vec_rnn"))
                    dve.tensor_tensor(xc[:, f, :], s[:, f, :], Y[:, f, :], ALU.mult).then_inc(sems["vec_rnn"], 1)
                    dve.wait_ge(sems["vec_rnn"], up("vec_rnn", ("ob", f)))

        def vec_evac_yr(k):
            s = slice(k["ft"], k["ft"] + 2)
            c = math.sqrt(2.0 / math.pi)
            dve.wait_ge(sems["act_drain"], at("evac", k["id"]))
            dve.tensor_scalar(SQ[:, s, :], SQ[:, s, :], 0.044715 * c, c, ALU.mult, ALU.add).then_inc(sems["vec_gelu"], 1)
            dve.wait_ge(sems["vec_gelu"], up("vec_gelu"))
            dve.tensor_tensor(SQ[:, s, :], SQ[:, s, :], Y[:, s, :], ALU.mult).then_inc(sems["vec_gelu"], 1)
            dve.wait_ge(sems["vec_gelu"], up("vec_gelu", ("gelu_in", k["ft"])))
            dve.wait_ge(sems["act_gelu"], at("gelu_tanh", k["ft"]))
            dve.scalar_tensor_tensor(out=Y[:, s, :], in0=SQ[:, s, :], scalar=1.0, in1=Y[:, s, :], op0=ALU.add, op1=ALU.mult).then_inc(sems["vec_gelu"], 1)
            dve.wait_ge(sems["vec_gelu"], up("vec_gelu"))

        def vec_evac_gate(k):
            if k["scaled"]:
                dve.wait_ge(sems["gemm_done"], at("unit", k["last_unit"]))
                dve.wait_ge(sems["act_norm"], at("rstd", k["x"][1]))
                dve.tensor_tensor(o_m["gt2"][:, (k["id"] // 2) % 2], slot(k["id"]), bc(RX[:]), ALU.mult).then_inc(sems["vec_drain"], 1)
                dve.wait_ge(sems["vec_drain"], up("vec_drain", ("evac", k["id"])))

        def vec_evac_branch(k):
            b1 = k["mg"][0] == "b1"
            gt = (o_b1["gt1"] if b1 else o_m["gt2"])[:, ((k["id"] - 1) // 2) % 2]
            bt = o_b1["bt1"] if b1 else o_m["bt2"]
            mg = MGS["b1" if b1 else "m"][:, k["ft"]:k["ft"] + 2, :]
            dve.wait_ge(sems["gemm_done"], at("unit", k["last_unit"]))
            dve.wait_ge(sems["act_drain"], at("gate_tanh", k["id"] - 1))
            name = ("mg", *k["mg"], k["ft"] // 2)
            out_ = mg if k["first_branch"] else bt[:]
            dve.scalar_tensor_tensor(out=out_, in0=gt, scalar=1.0, in1=slot(k["id"]), op0=ALU.add, op1=ALU.mult).then_inc(sems["vec_drain"], 1)
            dve.wait_ge(sems["vec_drain"], up("vec_drain", ("evac", k["id"])))
            if not k["first_branch"]:
                dve.tensor_tensor(mg, mg, bt[:], ALU.add).then_inc(sems["vec_drain"], 1)
                dve.wait_ge(sems["vec_drain"], up("vec_drain", name))

        def vec_ffn_gate(k):
            b = k["j"] % 2
            dve.wait_ge(sems["gemm_done"], at("unit", k["last_unit"]))
            dve.wait_ge(sems["act_norm"], at("rstd", k["x"][1]))
            dve.tensor_tensor(o_f2["fa"][:, b], slot(k["id"]), bc(RX[:]), ALU.mult).then_inc(sems["vec_ffn"], 1)
            dve.wait_ge(sems["vec_ffn"], up("vec_ffn", ("evac", k["id"])))

        def vec_ffn_val(k):
            b, V, key = k["j"] % 2, "vec_ffn", k["x"][1]
            fa, fe, fb = o_f2["fa"][:, b], o_f2["fe"][:, b], o_f2["fb"]
            dve.wait_ge(sems["act_ffn"], at("ffn_tanh", key, k["j"]))
            dve.scalar_tensor_tensor(out=fa, in0=fe, scalar=1.0, in1=fa, op0=ALU.add, op1=ALU.mult).then_inc(sems["vec_ffn"], 1)
            dve.wait_ge(sems["vec_ffn"], up("vec_ffn"))
            dve.wait_ge(sems["gemm_done"], at("unit", k["last_unit"]))
            dve.scalar_tensor_tensor(out=fb[:], in0=slot(k["id"]), scalar=0.5, in1=bc(RX[:]), op0=ALU.mult, op1=ALU.mult).then_inc(sems["vec_ffn"], 1)
            dve.wait_ge(sems["vec_ffn"], up("vec_ffn", ("evac", k["id"])))
            dve.tensor_tensor(o_f2["hf"][:, b], fa, fb[:], ALU.mult).then_inc(sems["vec_ffn"], 1)
            dve.wait_ge(sems["vec_ffn"], up("vec_ffn", ("hidden", key, k["j"])))

        def vec_up1(k):
            V, v, j = "vec_ffn", k["val"], k["j"]
            raw_up, uc = o_f1["up"], o_f1["uc"]
            dve.wait_ge(sems["act_drain"], at("evac", k["id"]))
            for i in range(2):
                f = 22 * v + 2 * j + i
                dve.tensor_scalar(uc[:, v, i, :], raw_up[:, v, i, 0:T], col("ffn_conv_w", f), col("ffn_conv_b", f), ALU.mult, ALU.add).then_inc(sems["vec_ffn"], 1)
                dve.wait_ge(sems["vec_ffn"], up("vec_ffn"))
                for n in range(1, FFN_K):
                    dve.scalar_tensor_tensor(out=uc[:, v, i, :], in0=raw_up[:, v, i, n:n + T], scalar=col("ffn_conv_w", 44 * n + f), in1=uc[:, v, i, :], op0=ALU.mult, op1=ALU.add).then_inc(sems["vec_ffn"], 1)
                    dve.wait_ge(sems["vec_ffn"], up("vec_ffn", ("conv_gate", j) if v == 0 else ("conv_val", j)))
            if v == 1:
                dve.wait_ge(sems["act_ffn"], at("ffn_tanh", "b1u", j))
                dve.scalar_tensor_tensor(out=uc[:, 0], in0=o_f1["fe1"][:], scalar=1.0, in1=uc[:, 0], op0=ALU.add, op1=ALU.mult).then_inc(sems["vec_ffn"], 1)
                dve.wait_ge(sems["vec_ffn"], up("vec_ffn"))
                dve.scalar_tensor_tensor(out=o_f1["hf1"][:, j % 2], in0=uc[:, 0], scalar=0.5, in1=uc[:, 1], op0=ALU.mult, op1=ALU.mult).then_inc(sems["vec_ffn"], 1)
                dve.wait_ge(sems["vec_ffn"], up("vec_ffn", ("hidden", "b1u", j)))

        def vec_hid_split(k):
            h, l_ = xbuf("HID", k["gen"])
            src = (o_f1["hf1"] if k["gen"] == "b1u" else o_f2["hf"])[:, k["j"] % 2]
            s = slice(2 * k["j"], 2 * k["j"] + 2)
            dve.wait_ge(sems["act_ffn"], at("hid_hi", k["gen"], k["j"]))
            dve.tensor_tensor(l_[:, s, :], src, h[:, s, :], ALU.subtract).then_inc(sems["vec_ffn"], 1)
            dve.wait_ge(sems["vec_ffn"], up("vec_ffn", ("split", "HID", k["gen"], 2 * k["j"])))
            mark(("split", "HID", k["gen"], 2 * k["j"] + 1), "vec_ffn")

        def vec_pads2(k):
            V = "vec_conv"
            dve.wait_ge(sems["gemm_done"], at("unit", k["hid_unit"]))
            dve.memset(o_m["zp"][:, :, 0:CONV_K - 1], 0.0).then_inc(sems["vec_conv"], 1)
            dve.wait_ge(sems["vec_conv"], up("vec_conv"))
            dve.memset(o_m["pu"][:, :, 0:POOL_PAD], 0.0).then_inc(sems["vec_conv"], 1)
            dve.wait_ge(sems["vec_conv"], up("vec_conv", ("pads2", k["l"])))

        def vec_glu(k):
            gt, bt = o_m["gt2"][:, ((k["id"] - 1) // 2) % 2], o_m["bt2"]
            dve.wait_ge(sems["gemm_done"], at("unit", k["last_unit"]))
            dve.wait_ge(sems["act_drain"], at("gate_tanh", k["id"] - 1))
            dve.scalar_tensor_tensor(out=bt[:], in0=slot(k["id"]), scalar=0.5, in1=bc(RX[:]), op0=ALU.mult, op1=ALU.mult).then_inc(sems["vec_conv"], 1)
            dve.wait_ge(sems["vec_conv"], up("vec_conv", ("evac", k["id"])))
            dve.scalar_tensor_tensor(out=o_m["zp"][:, k["ft"]:k["ft"] + 2, CONV_K - 1:], in0=gt, scalar=1.0, in1=bt[:], op0=ALU.add, op1=ALU.mult).then_inc(sems["vec_conv"], 1)
            dve.wait_ge(sems["vec_conv"], up("vec_conv", ("glu", k["l"], k["ft"])))

        def vec_conv31(k):
            l, f = k["l"], k["f"]
            taps = (CONV_K - 1) // CONV_PARTS
            dve.wait_ge(sems["act_conv"], at("conv0", l, f))
            for j in range(1 + k["part"] * taps, 1 + (k["part"] + 1) * taps):
                dve.scalar_tensor_tensor(out=Y[:, f, :], in0=o_m["zp"][:, f, j:j + T], scalar=col(f"dw{l}", 8 * j + f), in1=Y[:, f, :], op0=ALU.mult, op1=ALU.add).then_inc(sems["vec_conv"], 1)
                dve.wait_ge(sems["vec_conv"], up("vec_conv", ("conv", l)))

        def vec_pool(k):
            dve.wait_ge(sems["gemm_done"], at("unit", k["last_unit"]))
            dve.tensor_tensor(o_m["pu"][:, k["ft"]:k["ft"] + 2, POOL_PAD:], slot(k["id"]), bc(RX[:]), ALU.mult).then_inc(sems["vec_conv"], 1)
            dve.wait_ge(sems["vec_conv"], up("vec_conv", ("evac", k["id"])))

        def vec_window(k):
            g, V = k["g"], "vec_conv"
            u = o_m["pu"][:, 2 * g:2 * g + 2, :]
            bufs = WIN
            src, base = u, 0
            for lev in range(g + 1):
                sh = 1 << lev
                dst = bufs[lev % 2]
                base += sh
                dve.tensor_tensor(dst[:, :, base:], src[:, :, base:], src[:, :, base - sh:-sh], ALU.add).then_inc(sems["vec_conv"], 1)
                dve.wait_ge(sems["vec_conv"], up("vec_conv"))
                src = dst
            p = o_m["tmp2"][:, 2 * g:2 * g + 2, :]
            dve.wait_ge(sems["count_in"], at("cnt", k["l"]))
            dve.tensor_tensor(p, src[:, :, POOL_PAD:], bc(o_m["cnt"][:, g, :]), ALU.mult).then_inc(sems["vec_conv"], 1)
            dve.wait_ge(sems["vec_conv"], up("vec_conv"))
            dve.tensor_tensor(p, p, u[:, :, POOL_PAD:], ALU.subtract).then_inc(sems["vec_conv"], 1)
            dve.wait_ge(sems["vec_conv"], up("vec_conv", ("pooled", f"l{k['l']}", g)))

        def vec_pool_w(k):
            l, g = k["l"], k["g"]
            dve.wait_ge(sems["gemm_done"], at("unit", k["last_unit"]))
            for i in range(2):
                f = 2 * g + i
                dve.wait_ge(sems["act_split"], at("split_hi", "G", f"l{l}mq", f))
                dve.scalar_tensor_tensor(out=o_m["gl2"][:, f, :], in0=slot(k["id"])[:, i, :], scalar=col(f"pscale{l}", f), in1=o_m["gh2"][:, f, :], op0=ALU.mult, op1=ALU.subtract).then_inc(sems["vec_split"], 1)
                dve.wait_ge(sems["vec_split"], up("vec_split", ("split", "G", f"l{l}mq", f)))
            mark(("evac", k["id"]), "vec_split")

        def vec_cln_mean(k):
            dve.wait_ge(sems["act_conv"], at("mu", k["l"]))
            dve.wait_ge(sems["vec_conv"], at("conv", k["l"]))
            dve.tensor_tensor(Y[:], Y[:], bc(RY[:], NF), ALU.subtract).then_inc(sems["vec_conv"], 1)
            dve.wait_ge(sems["vec_conv"], up("vec_conv", ("centred", k["l"])))

        def vec_cln_out(k):
            l, V = k["l"], "vec_conv"
            dve.wait_ge(sems["act_conv"], at("cln_rstd", l))
            dve.tensor_tensor(Y[:], Y[:], bc(RY[:], NF), ALU.mult).then_inc(sems["vec_conv"], 1)
            dve.wait_ge(sems["vec_conv"], up("vec_conv"))
            t = o_m["tmp2"]
            for f in range(NF):
                dve.tensor_scalar(t[:, f, :], Y[:, f, :], col(f"ln_g{l}", f), col(f"ln_b{l}", f), ALU.mult, ALU.add).then_inc(sems["vec_conv"], 1)
                dve.wait_ge(sems["vec_conv"], up("vec_conv", ("cln_v", l, f // 2)))
            for h in range(4):
                s = slice(2 * h, 2 * h + 2)
                dve.wait_ge(sems["act_conv"], at("cln_tanh", l, h))
                dve.scalar_tensor_tensor(out=t[:, s, :], in0=Y[:, s, :], scalar=1.0, in1=t[:, s, :], op0=ALU.add, op1=ALU.mult).then_inc(sems["vec_conv"], 1)
                dve.wait_ge(sems["vec_conv"], up("vec_conv", ("cln", f"l{l}", 2 * h)))
                marks[("cln", f"l{l}", 2 * h + 1)] = marks[("cln", f"l{l}", 2 * h)]

        def vec_mem_turn(k):
            for half in range(2):
                dve.wait_ge(sems["pe_norm"], at("mem_ps", k["l"], half))
                dve.tensor_copy(o_c["memf"][:, 4 * half:4 * half + 4, :].rearrange("p f t -> p (f t)"), PBF[:, 0:1024]).then_inc(sems["vec_norm"], 1)
                dve.wait_ge(sems["vec_norm"], up("vec_norm", ("memf", f"l{k['l']}", half)))

        parts = dict(setup=vec_setup, params=vec_params, turn_x=vec_turn_x, mod_sum=vec_mod_sum, adapt=vec_adapt, split=vec_split,
                     residual=vec_residual, rstd_cols=vec_rstd_cols, evac_qk=vec_evac_qk, qk_norm=vec_qk_norm,
                     evac_scaled=vec_scaled, evac_v2=vec_v2, softmax=vec_softmax, pv=vec_pv, subln=vec_subln,
                     pads1=vec_pads1, pads_f1=vec_pads_f1, rnn_conv=vec_rnn_conv, rnn_in=vec_rnn_in, rnn_mult=vec_rnn_mult, evac_yr=vec_evac_yr, conv31=vec_conv31, rnn_scan=vec_rnn_scan,
                     evac_gate=vec_evac_gate, evac_branch=vec_evac_branch, evac_ffn_gate=vec_ffn_gate,
                     evac_ffn_val=vec_ffn_val, evac_up1=vec_up1, hid_split=vec_hid_split, pads2=vec_pads2,
                     evac_glu=vec_glu, evac_pool=vec_pool, window=vec_window, evac_pool_w=vec_pool_w,
                     cln_mean=vec_cln_mean, cln_out=vec_cln_out, mem_turn=vec_mem_turn)
        for kind, k in steps:
            if kind == "presplit":
                lo(k["m"])
            if kind == "unit":
                lo(k["m"] + AHEAD)
            if kind in parts:
                parts[kind](k)

    @block.gpsimd
    def _(pool):
        def pool_setup(k):
            pool.dma_start(o_set["sinks_in"][:], bass.AP(tensor=a["sinks"].tensor, offset=0, ap=[[0, P], [1, 8]])).then_inc(sems["small_in"], 16)
            up("small_in", by=16)
            pool.dma_start(o_set["lamb"][:], bass.AP(tensor=a["attn_lam_2"].tensor, offset=0, ap=[[0, P], [1, LAYERS * 4 * HD]])).then_inc(sems["small_in"], 16)
            up("small_in", ("small",), by=16)
            pool.dma_start(o_set["onehot"][:], a["onehot"]).then_inc(sems["bias_in"], 16)
            up("bias_in", by=16)
            pool.dma_start(o_set["relb"][0:32, 0:16], a["rel_bias"]).then_inc(sems["bias_in"], 16)
            up("bias_in", by=16)
            pool.dma_start(o_set["relb"][0:32, 16:24], a["rel_bias_2"]).then_inc(sems["bias_in"], 16)
            up("bias_in", ("bias_in",), by=16)

        def pool_bias(k):
            pool.wait_ge(sems["act_setup"], at("lines_read"))
            pool.dma_start(scratch.rearrange("i h j -> h i j"), o_set["lines"][:]).then_inc(sems["line_out"], 16)
            up("line_out", ("lines_out",), by=16)

        def pool_hankel(k):
            pool.wait_ge(sems["line_out"], at("lines_out"))
            pool.wait_ge(sems["vec_setup"], at("setup_end"))
            if k["after"] is not None:
                pool.wait_ge(*done(k["after"]))
            dst = o_m["hank2"] if k["which"] == 2 else o_b1["hank1"]
            src = bass.AP(tensor=scratch.tensor, offset=k["which"] * 8 * LINE, ap=[[1, P], [LINE, 8], [1, T]])
            pool.dma_start(dst[:], src).then_inc(sems["hankel_in"], 16)
            up("hankel_in", ("hank", k["which"], k["l"]), by=16)
            if k["which"] == 2:
                pool.dma_start(o_m["cnt"][:], bass.AP(tensor=a["inv_count"].tensor, offset=0, ap=[[0, P], [1, 4 * T]])).then_inc(sems["count_in"], 16)
                up("count_in", ("cnt", k["l"]), by=16)

        def pool_blocks(k):
            pool.wait_ge(sems["line_out"], at("lines_out"))
            pool.wait_ge(sems["vec_setup"], at("setup_end"))
            pool.memset(o_b1["bd"][:], 0.0).then_inc(sems["pool_setup"], 1)
            pool.wait_ge(sems["pool_setup"], up("pool_setup", ("bd_zero",)))
            for g, n in enumerate(("rnn_gate_a_w", "rnn_gate_x_w")):
                w = a[n][0].rearrange("(f two) k n -> two k f n", two=2)
                for h in range(2):
                    pool.dma_start(o_b1["bd"][h * HD:(h + 1) * HD, :, g, h * HD:(h + 1) * HD], w[h]).then_inc(sems["blocks_in"], 16)
                    up("blocks_in", ("blocks",), by=16)

        def pool_mem_load(k):
            pool.wait_ge(sems["vec_norm"], at("x", k["v"], 3))
            pool.dma_start(o_c["memt"][:], a["mem_2"][0].rearrange("(t p) d -> p t d", p=P)).then_inc(sems["mem_in"], 16)
            up("mem_in", ("memt", k["l"]), by=16)

        parts = dict(setup=pool_setup, bias=pool_bias, hankel=pool_hankel, mem_load=pool_mem_load, pads1=pool_blocks)
        for kind, k in steps:
            if kind in parts:
                parts[kind](k)

    ctx.close()



OUT_SHAPE = (1, T, D)


def shape_constants():
    import numpy as np

    def one_hot(max_distance, masked):
        d = 255 - np.arange(LINE)
        dist = np.maximum(d, 0)
        ratio = np.log(np.maximum(dist, 1).astype(np.float32) / np.float32(16)) / np.float32(math.log(max_distance / 16))
        large = np.minimum(16 + (ratio * np.float32(16)).astype(np.int32), 31)
        bucket = np.where(dist < 16, dist, large)
        o = np.zeros((33, LINE), np.float32)
        o[bucket, np.arange(LINE)] = 1.0
        o[32] = np.where(masked(d), NEG, 0.0)
        return o

    onehot = np.stack([one_hot(2048, lambda d: (d < 0) | (d >= 128)), one_hot(2048, lambda d: d < 0),
                       one_hot(128, lambda d: d < 0)], axis=1)
    heads = np.zeros((P, P), np.float32)
    heads[:HD, :HD] = heads[HD:, HD:] = 1.0
    t = np.arange(T)
    inv = np.stack([(1.0 / np.minimum(t + 1, w)).astype(np.float32) for w in (2, 4, 8, 16)])
    return {"ident": np.eye(P, dtype=np.float32), "flip": np.ascontiguousarray(np.eye(P, dtype=np.float32)[::-1]),
            "headsum": heads, "onehot": np.ascontiguousarray(onehot), "inv_count": inv}


def declare(nc, arrays):
    aps = {n: nc.dram_tensor(f"in_{n}_dram", v.shape, mybir.dt.from_np(v.dtype), kind="ExternalInput").ap()
           for n, v in arrays.items()}
    out = nc.dram_tensor("out_0_dram", OUT_SHAPE, F32, kind="ExternalOutput").ap()
    return aps, out, nc.dram_tensor("bias_lines", (3, 8, LINE), F32, kind="Internal").ap()


def kernel(**inputs):
    import numpy as np
    import concourse.bacc as bacc
    from concourse.bass_utils import run_bass_kernel_spmd

    arrays = {n: np.ascontiguousarray(v) for n, v in inputs.items()} | shape_constants()
    marks = {}
    for final in (False, True):
        nc = bacc.Bacc("TRN2", target_bir_lowering=False, num_devices=1)
        build(nc, *declare(nc, arrays), marks, final)
    r = run_bass_kernel_spmd(nc, [{f"in_{n}_dram": v for n, v in arrays.items()}], core_ids=[0])
    return r.results[0]["out_0_dram"]
```

```python
import math
from contextlib import ExitStack

import concourse.bass as bass
from concourse import mybir

F32 = mybir.dt.float32
F32R = mybir.dt.float32r
ALU = mybir.AluOpType
ACT = mybir.ActivationFunctionType
AX_X = mybir.AxisListType.X

P = 128
T = 256
TT = T // P
D = 1024
NF = D // P
DFF = 2816
HD = 64
LINE = 384
RMS_EPS = 1e-6
LN_EPS = 1e-5
RGLRU_C = 8.0
CONV_K = 31
RNN_K = 4
FFN_K = 3
POOL_PAD = 15
LAYERS = 2
UNIT_KT = 4
COLS = 256
RAW = 6
SPLIT = 4
AHEAD = SPLIT - 1
CONV_PARTS = 10
CONV_TAPS = (CONV_K - 1) // CONV_PARTS
NEG = -1e30

W_IN_1 = dict(qa=(0, 512), ka=(512, 128), va=(640, 128), xr=(768, 1024), yr=(1792, 1024), qc=(2816, 512),
              kc=(3328, 512), vc=(3840, 512), g=(4352, 3072))
W_IN_2 = dict(a=0, gt=1024, q=2048, k=3072, v=4096, pool=5120, gates=6144)

COL = {}
ROW_TILES = []


def _layout():
    def tile(parts):
        base = sum(n for n, _ in ROW_TILES)
        at = 0
        where = []
        for name, n in parts:
            COL[name] = COL.get(name, (base + at, 0))[0], COL.get(name, (0, 0))[1] + n
            where.append((name, at, n))
            at += n
        ROW_TILES.append((at, where))
    tile([("norm_mix", 8), ("norm_ffn", 8), ("b_mod", 48), ("rnn_conv_w", 32), ("rnn_conv_b", 8),
          ("gate_a_b", 8), ("gate_x_b", 8), ("lambda", 8)])
    tile([("ffn_conv_w", 128)])
    tile([("ffn_conv_w", 4), ("ffn_conv_b", 44), ("qk_gain", 4)])
    for l in range(LAYERS):
        tile([(f"norm{l}", 64), (f"dw_b{l}", 8), (f"ln_g{l}", 8), (f"ln_b{l}", 8), (f"pscale{l}", 8),
              (f"memn{l}", 8), (f"subln{l}", 1)])
        tile([(f"dw{l}", 128)])
        tile([(f"dw{l}", 120)])


_layout()
NCOLS = sum(n for n, _ in ROW_TILES)


def lam_init(layer):
    return 0.8 - 0.6 * math.exp(-0.3 * layer)


def plan(stop=None):
    S = []
    units = []
    readers = {}
    stat = [0]
    xv = [0]
    pairs = []
    pending = []
    held = []

    def add(kind, **k):
        S.append((kind, k))

    def gemm(w, col, kts, x, evac, ft0=0, form="F", cols=COLS, side=(), src=None, **k):
        p = dict(k, id=len(pairs), x=x, last_unit=len(units) + -(-kts // UNIT_KT) - 1, cols=cols)
        pairs.append(p)
        n = -(-kts // UNIT_KT)
        for j in range(n):
            nk = min(UNIT_KT, kts - j * UNIT_KT)
            u = dict(k, n=len(units), w=w, col=col, kt0=j * UNIT_KT, nkt=nk, x=x, ft0=ft0, form=form, cols=cols,
                     pair=p["id"], first=j == 0, last=j == n - 1, src=src)
            units.append(u)
            readers[x[0]] = u["n"]
            add("unit", **u)
        S.extend(held)
        held.clear()
        add(evac, **p)
        return p

    def new_stat():
        stat[0] += 1
        return stat[0]

    def order():
        seen, last, splits, raw = {}, None, [], []
        for kind, k in S:
            if k.get("s") is not None and k["s"] not in seen:
                seen[k["s"]] = last
                last = k["s"]
        for kind, k in S:
            if kind == "unit":
                k["m"] = len(splits)
                splits.append(k)
        for kind, k in S:
            if kind == "mod":
                k["raw"] = len(raw)
                raw.append(k)
            elif kind == "presplit" or (kind == "unit" and k["m"] + AHEAD < len(splits)):
                u = splits[k["m"] if kind == "presplit" else k["m"] + AHEAD]
                u["raw"] = len(raw)
                raw.append(u)
        return S, splits, raw, seen

    def split(buf, gen, src, fts=NF, ft0=0, **k):
        for f in range(fts):
            add("split", buf=buf, gen=gen, src=src, f=f, ft0=ft0, after=readers.get(buf), v=xv[0], **k)

    def spread(main, slots):
        n = sum(kind == "unit" for kind, _ in main)
        out, seen, put = [], 0, 0
        for step in main:
            out.append(step)
            if step[0] == "unit":
                seen += 1
                while put < len(slots) * seen // n:
                    out += slots[put]
                    put += 1
        return out

    def collect(fn):
        mark = len(S)
        fn()
        got = S[mark:]
        del S[mark:]
        return got

    def flush_residual():
        for k in pending:
            for p in range(4):
                add("residual", p=p, **k)
        pending.clear()

    def x_stats(key):
        flush_residual()
        s = new_stat()
        for p in range(4):
            add("square", key=key, src="x", p=p, v=xv[0])
        add("stat", key=key, s=s)
        add("rstd", key=key, s=s, out="RX")

    def enter(key, name, at_):
        res = pending.pop() if pending else None
        for p in range(4):
            if res:
                add("residual", p=p, **res)
            for f in (2 * p, 2 * p + 1):
                add("split", buf="H", gen=key, src="x", f=f, ft0=0, after=readers.get("H"), v=xv[0], col=(name, at_))
            add("square", key=key, src="x", p=p, v=xv[0])
        s = new_stat()
        held.extend([("stat", dict(key=key, s=s)), ("rstd", dict(key=key, s=s, out="RX"))])

    def attention(cfg, n):
        slots, subln = [], []
        if cfg in ("swa", "moba"):
            for i in range(n + 1):
                here, before = dict(cfg=cfg, i=i), dict(cfg=cfg, i=i - 1)
                slots += [([("scores", here)] if i < n else []) + ([("turn", dict(before, m=0))] if i else []),
                          ([("softmax", here)] if i < n else []) + ([("turn", dict(before, m=1))] if i else []),
                          [("pv", before)] if i else []]
            return slots
        for i in range(n + 1):
            here, before = dict(cfg=cfg, i=i), dict(cfg=cfg, i=i - 1)
            if i < n:
                slots.append([("scores", here)])
            if i:
                slots += [[("turn", dict(before, m=m))] for m in range(2 if cfg in ("swa", "moba") else 1)]
                slots[-1] += subln
            slots.append(([("softmax", here)] if i < n else []) + ([("pv", before)] if i else []))
            if i and cfg[:4] == "diff":
                subln = [("subln", dict(before, s=new_stat()))] if i % 2 == 0 else []
                slots.append([] if i < n else subln)
        return slots

    def done(tag):
        return stop == tag

    def residual(key, form, **k):
        xv[0] += 1
        pending.append(dict(key=key, form=form, v=xv[0], **k))

    add("setup")

    def mod_tensor(n, s):
        u = dict(n=len(units), w="w_mod", col=n * P, at=n, s=s, by="tensor", src="mod")
        units.append(u)
        return "mod", u

    def mod_vector(n, s, at_):
        steps_ = []
        for half in range(2):
            u = dict(n=len(units), w="w_mod", col=n * COLS, kt0=UNIT_KT * half, nkt=UNIT_KT, cols=COLS, half=half,
                     turn=turns[0], by="vector", src=None)
            units.append(u)
            steps_.append(("mod", u))
        steps_.append(("mod_col", dict(turn=turns[0], at=at_, s=s)))
        turns[0] += 1
        return steps_

    turns = [0]
    initial = new_stat()
    on_pe = [mod_tensor(n, initial) for n in range(6)]
    first_mods, behind = [], []
    for n in range(3, NF):
        first, second, sums = mod_vector(n, initial, 2 * n)
        first_mods += [first, on_pe.pop(0), second] + behind
        behind = [sums]
    first_mods += on_pe + behind + [("mod_sum", dict(first=0, count=2 * NF, s=initial))]
    S += first_mods[:8]
    add("params", part=0)
    add("turn_x")
    S += first_mods[8:16]
    add("bias")
    S += first_mods[16:]
    for m in range(AHEAD):
        add("presplit", m=m)
    x_stats("b1x")
    add("adapt", key="b1h", rstd="b1x", shift=0, scale=1, norm="norm_mix", after=None, v=0)

    def z1(name, j, evac, form="F", cols=COLS, **k):
        gemm("w_in", W_IN_1[name][0] + j * COLS, NF, ("H", "b1h"), evac, form=form, cols=cols, **k)

    waiting, normed = [], []

    def qk_units(name, n, dst, gain):
        for j in range(n):
            s = new_stat()
            normed.append(s)
            b = len(normed) % 2
            k = dict(dst=dst, ft=2 * j, b=b, before=normed[-3] if len(normed) > 2 else None)
            if name == "qa" and j == 1:
                add("params", part=1)
            if name == "ka":
                gemm("w_in", W_IN_1["ka"][0], NF, ("H", "b1h"), "evac_qk", src="dup", **k)
            else:
                z1(name, j, "evac_qk", **k)
            waiting.append(dict(dst=dst, ft=2 * j, gain=gain, s=s, b=b))
            if len(waiting) > 1:
                add("qk_norm", **waiting.pop(0))
    def rnn_slots():
        slots = []
        for f in range(NF + 3):
            if f < NF:
                slots.append([("rnn_conv", dict(f=f))])
            here = []
            if 2 <= f < NF + 2:
                here.append(("rnn_in", dict(f=f - 2)))
            if 1 <= f <= NF:
                here.append(("rnn_gate", dict(f=f - 1, s=new_stat())))
            if f >= 3:
                slots.append([("rnn_mult", dict(f=f - 3))])
            if here:
                slots.append(here)
        return slots + [[("rnn_sqrt", {})]] + [[("rnn_scan", dict(p=p))] for p in range(4)]

    def branch(b, gens):
        row, kts, ft0, gate = {"oa": (0, 4, 0, 0), "ob": (512, 8, 0, 1), "oc": (1536, 4, 4, 2)}[gens]
        for c in range(4):
            gemm("w_in", W_IN_1["g"][0] + gate * D + c * COLS, NF, ("H", "b1h"), "evac_gate", scaled=False, ft=2 * c)
            gemm("w_branch", c * COLS, kts, ("G", gens), "evac_branch", ft0=ft0, row0=row, ft=2 * c,
                 first_branch=b == 0, mg=("b1", b))

    def inputs_xy():
        add("pads1")
        for j in range(4):
            z1("xr", j, "evac_xr", ft=2 * j)
        for j in range(4):
            z1("yr", j, "evac_yr", ft=2 * j)
            if j:
                add("gelu", ft=2 * j - 2)
        add("gelu", ft=6)

    def inputs_swa():
        qk_units("qa", 2, "qa", 0)
        qk_units("ka", 1, "ka", 1)
        gemm("w_in", W_IN_1["va"][0], NF, ("H", "b1h"), "evac_v1", form="T", cols=128, dst="va", c0=0)
        add("qk_norm", **waiting.pop(0))

    def inputs_moba():
        qk_units("qc", 2, "qc", 2)
        qk_units("kc", 2, "kc", 3)
        for j in range(2):
            z1("vc", j, "evac_v1", form="T", dst="vc", c0=j * COLS)
        add("qk_norm", **waiting.pop(0))

    def merge_ab():
        branch(0, "oa")

    def merge_b():
        split("G", "ob", "XC", half=True)
        branch(1, "ob")

    def mod_slots(chunks):
        slots, behind = [], []
        for n in chunks:
            s = new_stat()
            first, second, sums = mod_vector(n, s, 0)
            slots += [[first], [second] + behind]
            behind = [sums, ("mod_sum", dict(first=2 * n, count=2, s=s))]
        return slots + [behind]

    add("hankel", which=0, l=0, after=None)
    xy, swa_in, moba_in = collect(inputs_xy), collect(inputs_swa), collect(inputs_moba)
    moba_in = spread(moba_in, attention("swa", 4))
    moba_in.append(("hankel", dict(which=1, l=0, after=("scores", "swa", 3))))
    xr_units = 1 + max(i for i, (kind, _) in enumerate(xy) if kind == "evac_xr")
    S += xy[:xr_units]

    def oa_part():
        split("G", "oa", "qa", fts=4)
        merge_ab()
    oa = collect(oa_part)
    moba = attention("moba", 4)
    first = len(moba) * 3 // 7
    rest = xy[xr_units:] + swa_in + moba_in + spread(oa, moba[:first])
    rest = spread(rest, rnn_slots())
    rest += spread(collect(merge_b), moba[first:])

    def merge_c():
        split("G", "oc", "qc", fts=4, ft0=4)
        branch(2, "oc")
    rest += collect(merge_c)
    begin = [i for i, (kind, _) in enumerate(rest) if kind == "unit"][20]
    S += rest[:begin] + spread(rest[begin:], mod_slots(range(NF, 20)))
    split("H", "b1m", "MG", mg=("b1", 2), half=True)
    for c in range(4):
        gemm("w_out", c * COLS, NF, ("H", "b1m"), "evac_y", ft=2 * c, sq=None, yk="b1r")
    residual("b1r", "gate_mod", chunk=2)
    flush_residual()
    x_stats("b1f")
    add("adapt", key="b1g", rstd="b1f", shift=3, scale=4, norm="norm_ffn", after=readers["H"], v=xv[0])
    add("pads_f1")
    for j in range(11):
        gemm("w_up", j * COLS, NF, ("H", "b1g"), "evac_up1", j=j, val=0)
        gemm("w_up", DFF + j * COLS, NF, ("H", "b1g"), "evac_up1", j=j, val=1)
        if j:
            add("hid_split", gen="b1u", j=j - 1)
    add("hid_split", gen="b1u", j=10)

    def down():
        for c in range(4):
            gemm("w_down", c * COLS, 22, ("HID", "b1u"), "evac_y", ft=2 * c, sq=None, yk="b1s")
    S += spread(collect(down), mod_slots(range(20, 24)))
    residual("b1s", "gate_mod", chunk=5)
    if stop == "block1":
        flush_residual()
        add("finish")
        return order()

    def ffn(l, i):
        key = f"l{l}f{i}"
        enter(key, f"norm{l}", (0, 6)[i] * 8)
        for j in range(11):
            gemm("w1", j * COLS, NF, ("H", key), "evac_ffn_gate", l=l, i=i, j=j)
            gemm("w3", j * COLS, NF, ("H", key), "evac_ffn_val", l=l, i=i, j=j)
            if j:
                add("hid_split", gen=key, j=j - 1)
        add("hid_split", gen=key, j=10)
        s = new_stat()
        for c in range(4):
            gemm("w2", c * COLS, 22, ("HID", key), "evac_y", ft=2 * c, sq=s, yk=key, l=l, i=i,
                 gain=(f"norm{l}", (1, 7)[i] * 8))
            if c:
                add("ystat", s=s, c=c - 1)
        add("ystat", s=s, c=3)
        add("rstd", key=key + "y", s=s, out="RY")
        residual(key, "normed", half=True)

    def z2(l, name, j, evac, form="F", **k):
        gemm("w_in_2", W_IN_2[name] + j * COLS, NF, ("H", f"l{l}m"), evac, form=form, l=l, **k)

    def mixer(l):
        key = f"l{l}m"
        enter(key, f"norm{l}", 16)
        add("pads2", l=l, hid_unit=readers["HID"])

        def glu(js):
            for j in js:
                z2(l, "gt", j, "evac_gate", scaled=True, ft=2 * j)
                z2(l, "a", j, "evac_glu", ft=2 * j)

        def keys_values():
            add("rstd_cols", key=key, s=new_stat())
            for j in range(4):
                z2(l, "k", j, "evac_scaled", dst="k", ft=2 * j, by=1.0)
            add("hankel", which=2, l=l, after=("unit", readers["HID"]))
            for j in range(4):
                z2(l, "v", j, "evac_v2", form="T", dst="v", c0=j * COLS)
            z2(l, "q", 0, "evac_scaled", dst="q", ft=0, by=HD ** -0.5)

        def queries_pool():
            for name, j in (("pool", 3), ("pool", 2), ("q", 1), ("pool", 1), ("pool", 0), ("q", 2), ("q", 3)):
                if name == "q":
                    z2(l, "q", j, "evac_scaled", dst="q", ft=2 * j, by=HD ** -0.5)
                else:
                    z2(l, "pool", j, "evac_pool", ft=2 * j)
                    add("window", g=j, l=l)
            for g in (3, 2, 1, 0):
                for f in (2 * g, 2 * g + 1):
                    add("split", buf="G", gen=key + "p", src="pooled", f=f, ft0=0, after=readers.get("G"), v=0)
            for g in (3, 2, 1, 0):
                gemm("pool_w", 0, 2, ("G", key + "p"), "evac_pool_w", ft0=2 * g, l=l, g=g)
            merge(0, 8, "pool_o", "q", True)

        def merge(b, gate, w, gen, first):
            for c in range(4):
                z2(l, "gates", gate + c, "evac_gate", scaled=True, ft=2 * c)
                gemm(w, c * COLS, NF, ("G", key + gen), "evac_branch", l=l, ft=2 * c, first_branch=first, mg=(key, b))

        def merge_attention():
            split("G", key + "a", "q")
            merge(1, 4, "attn_o", "a", False)

        def conv(features, by):
            return [[("conv31", dict(l=l, f=f, part=part, by=by))] for f in features for part in range(CONV_PARTS)]

        glu((0,))
        by_pool, by_vector = conv(range(1, NF, 2), "pool"), conv(range(0, NF, 2), "vector")
        early = len(by_pool) * 20 // 40
        main = spread(collect(lambda: (glu((1, 2, 3)), keys_values())), by_pool[:early])
        middle = spread(collect(queries_pool), attention(f"diff{l}", 8))
        windows = 1 + max(i for i, (kind, _) in enumerate(middle) if kind == "window")
        last = collect(merge_attention)
        half = 1 + [i for i, (kind, _) in enumerate(last) if kind == "evac_branch"][0]
        main += middle[:windows] + spread(middle[windows:] + last[:half], by_pool[early:])
        S.extend(spread(main, by_vector))
        norm = [[("cln_mean", dict(l=l, s=new_stat()))], [("cln_var", dict(l=l, s=new_stat()))]]
        norm += [[("cln_out", dict(l=l, p=p))] for p in range(4)]
        S.extend(spread(last[half:], norm))
        split("G", key + "c", "TMP", half=True)
        merge(2, 0, "conv_pw", "c", False)
        split("H", key + "o", "MG", mg=(key, 2), half=True)
        s = new_stat()
        mem = f"l{l}cm"
        add("mem_load", l=l, after=("split", "H", key + "o", 7))
        for c in range(4):
            gemm("w_out_2", c * COLS, NF, ("H", key + "o"), "evac_y", ft=2 * c, sq=s, yk=key, l=l, gain=(f"norm{l}", 24))
            if c:
                add("ystat", s=s, c=c - 1)
            if c == 1:
                add("mem_turn", l=l)
            if c == 2:
                split("M", mem, "memf", col=(f"memn{l}", 0))
                for p in range(4):
                    add("square", key=mem, src="memf", p=p, v=0)
        add("ystat", s=s, c=3)
        add("rstd", key=key + "y", s=s, out="RY")
        s = new_stat()
        add("stat", key=mem, s=s)
        add("rstd", key=mem, s=s, out="RM")
        residual(key, "normed", half=False)

    def cross(l):
        key, mem = f"l{l}c", f"l{l}cm"
        enter(key, f"norm{l}", 32)
        for j in range(4):
            gemm("xattn_kv", j * COLS, NF, ("M", mem), "evac_scaled", l=l, dst="xk", ft=2 * j, by=1.0)
        add("rstd_cols", key=mem, s=new_stat())

        def values(j):
            gemm("xattn_kv", D + j * COLS, NF, ("M", mem), "evac_v2", form="T", l=l, dst="xv", c0=j * COLS)

        def queries(j):
            gemm("xattn_q", j * COLS, NF, ("H", key), "evac_scaled", l=l, dst="xq", ft=2 * j, by=(D // 4) ** -0.5)

        queries(0)
        heads = attention(f"cross{l}", 4)
        main = collect(lambda: [(values(i), queries(i + 1)) for i in range(3)])
        S.extend(spread(main, heads[:7]))
        S.extend(heads[7] + heads[8] + heads[9] + heads[10])
        values(3)
        for steps_ in heads[11:]:
            S.extend(steps_)
        split("H", key + "o", "xq")
        s = new_stat()
        for c in range(4):
            gemm("xattn_o", c * COLS, NF, ("H", key + "o"), "evac_y", ft=2 * c, sq=s, yk=key, l=l, gain=(f"norm{l}", 40))
            if c:
                add("ystat", s=s, c=c - 1)
        add("ystat", s=s, c=3)
        add("rstd", key=key + "y", s=s, out="RY")
        residual(key, "normed", half=False)

    for l in range(LAYERS):
        ffn(l, 0)
        if done(f"f{l}0"):
            break
        mixer(l)
        if done(f"m{l}"):
            break
        cross(l)
        if done(f"c{l}"):
            break
        ffn(l, 1)
        if done(f"f{l}1"):
            break
    flush_residual()
    add("finish")
    return order()


def build(nc, a, out, scratch, marks, final, stop=None):
    steps, splits, raws, stat_before = plan(stop)

    ctx = ExitStack()
    sb = lambda name, shape, dt=F32: ctx.enter_context(nc.sbuf_tensor(name, shape, dt))

    RAWB = sb("raw_weights", [P, RAW, UNIT_KT, COLS])
    WH, WL = sb("weights_hi", [P, SPLIT, UNIT_KT, COLS], F32R), sb("weights_lo", [P, SPLIT, UNIT_KT, COLS], F32R)
    X, Y = sb("x_res", [P, NF, T]), sb("y", [P, NF, T])
    HH, HL = sb("h_hi", [P, NF, T], F32R), sb("h_lo", [P, NF, T], F32R)
    SQ = sb("squares", [P, NF, T])
    RX, RY, RQ = sb("rstd_x", [P, T]), sb("rstd_y", [P, T]), sb("rstd_q", [P, 2, T])
    RT = sb("rstd_tok", [P, TT])
    ASQ = sb("small_squares", [P, 2, 2, T])
    CT = sb("param_cols", [P, NCOLS])
    HALFB = sb("half_gate_bias", [P, 2 * NF])
    MODC = sb("mod_cols", [P, 48])
    ACC = sb("mod_partial", [P, 2, COLS])
    CC, SP4, QG = sb("silu_c", [P, NF]), sb("softplus4", [P, NF]), sb("qk_gains", [P, 4])
    ONES, IDENT, FLIP, HEADS = (sb(n, [P, P]) for n in ("ones", "ident", "flip", "headsum"))
    EPS = sb("eps", [P, 4])
    LAM, SINK = sb("neg_lam", [P, LAYERS]), sb("neg_sinks", [P, 8])
    NM, DEN, RD, ES = sb("neg_max", [P, 4]), sb("den", [P, 4]), sb("rden", [P, 4]), sb("sink_exp", [P, 4])

    def overlay(**shapes):
        with ExitStack() as c:
            return {n: c.enter_context(nc.sbuf_tensor(n, *(s if isinstance(s, tuple) else (s,)), F32)
                                       if not isinstance(s, tuple) else nc.sbuf_tensor(n, s[0], s[1]))
                    for n, s in shapes.items()}
    R = F32R
    o_set = overlay(rows=[P, len(ROW_TILES), P], xtok=[P, TT, D], onehot=[33, 3, LINE], relb=[33, 24],
                    lines=[8, 3, LINE], lamb=[P, LAYERS * 4 * HD], lamp=[P, LAYERS * 2, HD], lams=[P, LAYERS * 2],
                    spt=[P, 6, NF], sgc=[P, NF], sinks_in=[P, 8], c_cols=[P, NF])
    o_b1 = overlay(gh=([P, NF, T], R), gl=([P, NF, T], R), qa=[P, 4, T], ka=[P, 2, T], va=[P, TT, 128],
                   qc=[P, 4, T], kc=[P, 4, T], vc=[P, TT, 512], hank1=[P, 8, T], e1=[P, 2, 2, 2, T], pt1=[P, 768],
                   xr=[P, NF, RNN_K - 1 + T], xc=[P, NF, T], s_all=[P, NF, T], rg=[P, 2, 2, T],
                   gt1=[P, 2, 2, T], bd=[P, NF, 2, P])
    o_f1 = overlay(hidh=([P, 22, T], R), hidl=([P, 22, T], R), up=[P, 2, 2, T + FFN_K - 1], uc=[P, 2, 2, 2, T],
                   fe1=[P, 2, T], hf1=[P, 2, 2, T])
    o_f2 = overlay(hidh2=([P, 22, T], R), hidl2=([P, 22, T], R), fa=[P, 2, 2, T], fe=[P, 2, 2, T], fb=[P, 2, T],
                   hf=[P, 2, 2, T])
    o_m = overlay(gh2=([P, NF, T], R), gl2=([P, NF, T], R), q=[P, NF, T], k=[P, NF, T], v=[P, TT, D],
                  hank2=[P, 8, T], e2=[P, 2, 2, T], pt2=[P, 384], zp=[P, NF, CONV_K - 1 + T],
                  pu=[P, NF, POOL_PAD + T], tmp2=[P, NF, T], gt2=[P, 2, 2, T], bt2=[P, 2, T],
                  cnt=[P, 4, T], prod=[P, 2, CONV_TAPS, T])
    o_c = overlay(mh=([P, NF, T], R), ml=([P, NF, T], R), xq=[P, NF, T], xk=[P, NF, T], xv=[P, TT, D],
                  e3=[P, 2, 2, T], pt3=[P, 2 * 512], memt=[P, TT, D], memf=[P, NF, T],
                  msq=[P, NF, T], rm=[P, T])
    o_o = overlay(otok=[P, TT, D])

    o_b1["bt1"] = o_b1["rg"][:, 0]
    wide = POOL_PAD + T
    WIN = [SQ[:].rearrange("p f t -> p (f t)")[:, i * 2 * wide:(i + 1) * 2 * wide].rearrange("p (a t) -> p a t", a=2)
           for i in range(2)]
    RT8 = sb("adapt_gain", [P, NF])
    MGS = {"b1": SQ[:], "m": o_m["pu"][:, :, POOL_PAD:]}
    last_x = max([k["v"] for kind, k in steps if kind == "residual"], default=0)
    n_pairs = 1 + max([k["id"] for kind, k in steps if kind.startswith("evac")], default=-1)
    last_pairs = [p for p in (n_pairs - 2, n_pairs - 1) if p >= 0]

    GP = ctx.enter_context(nc.psum_tensor("gemm_ps", [P, 2, 2, 512], F32))
    PB = ctx.enter_context(nc.psum_tensor("misc_ps", [P, 4, 512], F32))
    GPF = GP[:].rearrange("p a b c -> p (a b c)")
    PBF = PB[:].rearrange("p a b -> p (a b)")
    STAT = PB[:, 3, :]
    TURN = PB[:, 2, :]
    PV = PB[:, 2, :]

    names = [f"raw_landed{i}" for i in range(RAW)] + [
        "consts_in", "ident_in", "x_in", "bias_in", "small_in", "count_in", "hankel_in", "line_out", "mem_in", "rows_in", "blocks_in", "y_out",
        "weights_rounded", "weights_rest", "gemm_done", "act_drain", "vec_drain", "act_norm", "vec_norm", "pe_norm",
        "act_attn", "vec_attn", "pe_attn", "act_rnn", "vec_rnn", "pe_rnn", "act_ffn", "vec_ffn", "act_split",
        "vec_split", "act_conv", "vec_conv", "pool_conv", "pool_window", "act_products", "hidden_rest", "vec_mod", "c_in", "rows_in2", "act_gelu", "vec_gelu", "pe_mod", "act_setup", "vec_setup",
        "pe_setup", "pool_setup"]
    sems = {n: ctx.enter_context(nc.semaphore(n)) for n in names}

    count = {}

    def up(name, reached=None, by=1):
        count[name] = count.get(name, 0) + by
        if reached is not None:
            marks[reached] = (name, count[name])
        return count[name]

    def mark(reached, name):
        marks[reached] = (name, count[name])

    def at(*reached):
        assert reached in marks or not final, reached
        return marks.get(reached, (None, 1))[1]

    def done(reached):
        assert reached in marks or not final, reached
        name, value = marks.get(reached, (names[0], 1))
        return sems[name], value

    XBUF = {"H": (HH, HL), "M": (o_c["mh"], o_c["ml"])}

    def xbuf(buf, gen):
        if buf == "G":
            return (o_b1["gh"], o_b1["gl"]) if gen in ("oa", "ob", "oc") else (o_m["gh2"], o_m["gl2"])
        if buf == "HID":
            return (o_f1["hidh"], o_f1["hidl"]) if gen == "b1u" else (o_f2["hidh2"], o_f2["hidl2"])
        return XBUF[buf]

    BUF = {"x": X, "y": Y, "qa": o_b1["qa"], "ka": o_b1["ka"], "qc": o_b1["qc"], "kc": o_b1["kc"], "va": o_b1["va"],
           "vc": o_b1["vc"], "XC": o_b1["xc"], "q": o_m["q"], "k": o_m["k"], "v": o_m["v"], "xq": o_c["xq"],
           "xk": o_c["xk"], "xv": o_c["xv"], "memf": o_c["memf"], "pooled": o_m["tmp2"], "TMP": o_m["tmp2"],
           }

    def col(name, i=0, n=1):
        return CT[:, COL[name][0] + i:COL[name][0] + i + n]

    def bc(ap, n=2):
        return ap.unsqueeze(1).to_broadcast([P, n, T])

    def slot(pid):
        return GP[:, pid % 2, :, 0:T]

    def att(cfg, i):
        if cfg in ("swa", "moba"):
            q, k, v = (o_b1["qa"], o_b1["ka"], o_b1["va"]) if cfg == "swa" else (o_b1["qc"], o_b1["kc"], o_b1["vc"])
            kt = i // 2 if cfg == "swa" else i
            vcol = (lambda m: (i // 2) * HD) if cfg == "swa" else (lambda m: (2 * i + m) * HD)
            return dict(maps=2, q=[q[64 * m:64 * m + 64, i, :] for m in (0, 1)],
                        k=[k[64 * m:64 * m + 64, kt, :] for m in (0, 1)],
                        v=[[v[:, b, vcol(m):vcol(m) + HD] for b in (0, 1)] for m in (0, 1)],
                        hank=o_b1["hank1"], head=[2 * i, 2 * i + 1], E=o_b1["e1"][:, i % 2], PT=o_b1["pt1"], o=q[:, i, :],
                        causal=True, pack="pair", hname=("hank", 0 if cfg == "swa" else 1, 0))
        l = int(cfg[-1])
        if cfg[:4] == "diff":
            q, k, v = o_m["q"], o_m["k"], o_m["v"]
            return dict(maps=2, q=[q[64 * m:64 * m + 64, i, :] for m in (0, 1)],
                        k=[k[64 * m:64 * m + 64, i, :] for m in (0, 1)],
                        v=[[v[:, b, i * P:(i + 1) * P] for b in (0, 1)]], hank=o_m["hank2"], head=[i, i],
                        E=o_m["e2"], PT=o_m["pt2"], o=q[:, i, :], causal=True, pack="diff", hname=("hank", 2, l))
        q, k, v = o_c["xq"], o_c["xk"], o_c["xv"]
        return dict(maps=1, q=[[q[:, 2 * i + f, :] for f in (0, 1)]], k=[[k[:, 2 * i + f, :] for f in (0, 1)]],
                    v=[[v[:, b, (2 * i + f) * P:(2 * i + f + 1) * P] for b in (0, 1)] for f in (0, 1)],
                    hank=None, E=o_c["e3"], PT=o_c["pt3"], o=q[:, 2 * i:2 * i + 2, :], causal=False, pack="cross",
                    hname=None)

    def scores_at(c, qt, m, nk):
        return PB[:, qt, 0:nk] if c["maps"] == 1 else PB[:, m, P * qt:P * qt + nk]

    def source(k):
        if k["src"] == "MG":
            return MGS["b1" if k["mg"][0] == "b1" else "m"][:, k["f"], :]
        return BUF[k["src"]][:, k["f"], :]

    def ready_of(k):
        src, f, gen = k["src"], k["f"], k["gen"]
        return {"x": ("x", k["v"], f // 2), "qa": ("o", "swa", f), "qc": ("o", "moba", f), "XC": ("ob", f),
                "MG": ("mg",) + (k.get("mg") or ()) + (f // 2,), "q": ("o", "diff" + gen[1], f),
                "xq": ("o", "cross" + gen[1], f // 2), "pooled": ("pooled", gen[:2], f // 2),
                "TMP": ("cln", gen[:2], f), "memf": ("memf", gen[:2], f // 4)}[src]

    W_DRAM = {
        "w_mod": lambda u: a["w_mod"][0], "w_in": lambda u: a["w_in"][0],
        "w_branch": lambda u: a["w_branch"][0, u["row0"]:u["row0"] + (512 if u["ft0"] or u["row0"] == 0 else 1024), :],
        "w_out": lambda u: a["w_out"][0], "w_up": lambda u: a["w_up"][0], "w_down": lambda u: a["w_down"][0],
        "w1": lambda u: a["ffn_w1_2"][u["l"], u["i"]], "w3": lambda u: a["ffn_w3_2"][u["l"], u["i"]],
        "w2": lambda u: a["ffn_w2_2"][u["l"], u["i"]], "w_in_2": lambda u: a["w_in_2"][u["l"]],
        "pool_w": lambda u: a["pool_w_2"][u["l"], u["g"]], "pool_o": lambda u: a["pool_o_2"][u["l"]],
        "conv_pw": lambda u: a["conv_pw_2"][u["l"]], "attn_o": lambda u: a["attn_o_2"][u["l"]],
        "w_out_2": lambda u: a["w_out_2"][u["l"]], "xattn_q": lambda u: a["xattn_q_2"][u["l"]],
        "xattn_kv": lambda u: a["xattn_kv_2"][u["l"]], "xattn_o": lambda u: a["xattn_o_2"][u["l"]],
    }

    def mod_raw(r):
        return RAWB[:, r % RAW].rearrange("p k n -> p (k n)").rearrange("p (k n) -> p k n", n=P)

    block = ctx.enter_context(nc.Block())

    @block.sync
    def _(sp):
        c_cols = bass.AP(tensor=a["c"].tensor, offset=a["c"].offset, ap=[[1, P], [P, NF]])
        sp.dma_start(o_set["c_cols"][:], c_cols, allow_slow_non_contiguous=True).then_inc(sems["c_in"], 16)
        up("c_in", ("c_in",), by=16)
        src = {"norm_mix": a["norm_mix"], "norm_ffn": a["norm_ffn"], "b_mod": a["b_mod"],
               "rnn_conv_w": a["rnn_conv_w"], "rnn_conv_b": a["rnn_conv_b"], "gate_a_b": a["rnn_gate_a_b"],
               "gate_x_b": a["rnn_gate_x_b"], "lambda": a["rnn_lambda"], "ffn_conv_w": a["ffn_conv_w"],
               "ffn_conv_b": a["ffn_conv_b"]}
        for l in range(LAYERS):
            src |= {f"norm{l}": a["norm_g_2"][l], f"dw_b{l}": a["conv_dw_b_2"][l], f"ln_g{l}": a["conv_ln_g_2"][l],
                    f"ln_b{l}": a["conv_ln_b_2"][l], f"pscale{l}": a["pool_scale_2"][l],
                    f"memn{l}": a["mem_norm_2"][l], f"subln{l}": a["attn_subln_2"][l], f"dw{l}": a["conv_dw_2"][l]}
        used = {}

        def load_rows(tiles, sem, mark):
            for i in tiles:
                for name, at_, n in ROW_TILES[i][1]:
                    if name == "qk_gain":
                        for j, g in enumerate(("qnorm_a", "knorm_a", "qnorm_c", "knorm_c")):
                            for h in range(2):
                                sp.dma_start(o_set["rows"][at_ + j:at_ + j + 1, i, h * HD:(h + 1) * HD], a[g]).then_inc(sems["rows_in2"], 16)
                                up("rows_in2", by=16)
                        continue
                    ap = src[name]
                    first = used.get(name, 0)
                    used[name] = first + n
                    flat = bass.AP(tensor=ap.tensor, offset=ap.offset + first * P, ap=[[P, n], [1, P]])
                    sp.dma_start(o_set["rows"][at_:at_ + n, i, :], flat).then_inc(sems[sem], 16)
                    up(sem, mark, by=16)

        for u in raws:
            r = u["raw"]
            if r == RAW:
                sp.dma_start(IDENT[:], a["ident"]).then_inc(sems["ident_in"], 16)
                up("ident_in", ("ident",), by=16)
                load_rows((0,), "rows_in", ("rows",))
                sp.dma_start(o_set["xtok"][:], a["x"][0].rearrange("(t p) d -> p t d", p=P)).then_inc(sems["x_in"], 16)
                up("x_in", ("xtok",), by=16)
                sp.dma_start(FLIP[:], a["flip"]).then_inc(sems["consts_in"], 16)
                up("consts_in", by=16)
                sp.dma_start(HEADS[:], a["headsum"]).then_inc(sems["consts_in"], 16)
                up("consts_in", ("consts",), by=16)
            if r == 2 * NF + 3:
                load_rows(range(1, len(ROW_TILES)), "rows_in2", ("rows2",))
            if r >= RAW:
                sp.wait_ge(*done(("free", r - RAW)))
            w = W_DRAM[u["w"]](u).rearrange("(k p) n -> p k n", p=P)
            if u["src"] == "mod":
                sp.dma_start(mod_raw(r), w[:, :, u["col"]:u["col"] + P]).then_inc(sems[f"raw_landed{r % RAW}"], 16)
                up(f"raw_landed{r % RAW}", ("landed", r), by=16)
                continue
            w = w[:, u["kt0"]:u["kt0"] + u["nkt"], :]
            dst = RAWB[:, r % RAW, 0:u["nkt"], :]
            sem = f"raw_landed{r % RAW}"
            if u["src"] == "dup":
                for g in range(4):
                    c = u["col"] + (g // 2) * HD
                    sp.dma_start(dst[:, :, g * HD:(g + 1) * HD], w[:, :, c:c + HD]).then_inc(sems[sem], 16)
                    up(sem, ("landed", r), by=16)
            else:
                sp.dma_start(dst[:, :, 0:u["cols"]], w[:, :, u["col"]:u["col"] + u["cols"]]).then_inc(sems[sem], 16)
                up(sem, ("landed", r), by=16)
        sp.wait_ge(sems["act_setup"], at("otok"))
        sp.dma_start(out[0].rearrange("(t p) d -> p t d", p=P), o_o["otok"][:]).then_inc(sems["y_out"], 16)
        sp.wait_ge(sems["y_out"], up("y_out", by=16))

    @block.tensor
    def _(pe):
        state = dict(att=None, scores=None)

        def stat_free(s):
            if stat_before.get(s) is not None:
                pe.wait_ge(*done(("stat_read", stat_before[s])))

        def pe_unit(u):
            xh, xl = xbuf(*u["x"])
            m = u["m"] % SPLIT
            pe.wait_ge(sems["weights_rest"], at("rest", u["m"]))
            if u["first"]:
                if u["pair"] >= 2:
                    pe.wait_ge(*done(("evac", u["pair"] - 2)))
                else:
                    pe.wait_ge(sems["vec_setup"], at("x", 0, 3))
            ps = GP[:, u["pair"] % 2, :, :]
            tiles = u["cols"] // P if u["form"] == "F" else TT
            for c in range(tiles):
                for kt in range(u["nkt"]):
                    f = u["ft0"] + u["kt0"] + kt
                    if c == 0:
                        pe.wait_ge(*done(("split", *u["x"], f)))
                    for n, (w, x) in enumerate(((WH, xh), (WH, xl), (WL, xh))):
                        start = u["first"] and kt == 0 and n == 0
                        stop_ = u["last"] and kt == u["nkt"] - 1 and n == 2
                        if u["form"] == "F":
                            mm = pe.matmul(ps[:, c, 0:T], w[:, m, kt, c * P:(c + 1) * P], x[:, f, :],
                                           start=start, stop=stop_)
                        else:
                            mm = pe.matmul(ps[:, c, 0:u["cols"]], x[:, f, c * P:(c + 1) * P],
                                           w[:, m, kt, 0:u["cols"]], start=start, stop=stop_)
            mm.then_inc(sems["gemm_done"], 1)
            up("gemm_done", ("unit", u["n"]))

        def pe_params(k):
            if k["part"] == 0:
                pe.wait_ge(sems["ident_in"], at("ident"))
                pe.wait_ge(sems["rows_in"], at("rows"))
            else:
                pe.wait_ge(sems["rows_in2"], at("rows2"))
                pe.wait_ge(sems["act_setup"], at("lines_read"))
            for i in ((0,) if k["part"] == 0 else range(1, len(ROW_TILES))):
                n = ROW_TILES[i][0]
                t = pe.transpose(PBF[:, i * P:i * P + n], o_set["rows"][0:n, i, :], IDENT[0:n, 0:n])
            t.then_inc(sems["pe_setup"], 1)
            up("pe_setup", ("rows_T", k["part"]))

        def pe_turn_x(k):
            pe.wait_ge(sems["x_in"], at("xtok"))
            for f in range(NF):
                for t in range(TT):
                    mm = pe.transpose(GPF[:, f * T + t * P:f * T + (t + 1) * P], o_set["xtok"][:, t, f * P:(f + 1) * P],
                                      IDENT[:])
            mm.then_inc(sems["pe_setup"], 1)
            up("pe_setup", ("x_T",))

        def pe_mod(u):
            if u["by"] == "vector":
                return
            pe.wait_ge(*done(("landed", u["raw"])))
            pe.wait_ge(sems["vec_setup"], at("cc"))
            stat_free(u["s"])
            for kt in range(NF):
                mm = pe.matmul(STAT[:, u["at"]:u["at"] + 1], mod_raw(u["raw"])[:, kt, :], CC[:, kt:kt + 1],
                               start=kt == 0, stop=kt == NF - 1)
            mm.then_inc(sems["pe_mod"], 1)
            up("pe_mod", ("free", u["raw"]))
            mark(("mod_cols", u["s"]), "pe_mod")

        def pe_mod_col(k):
            stat_free(k["s"])
            pe.wait_ge(sems["vec_mod"], at("mod_partial", k["turn"]))
            for i in range(2):
                mm = pe.matmul(STAT[:, k["at"] + i:k["at"] + i + 1], ACC[:, k["turn"] % 2, i * P:(i + 1) * P],
                               ONES[:, 0:1], start=True, stop=True)
            mm.then_inc(sems["pe_mod"], 1)
            up("pe_mod", ("mod_added", k["turn"]))
            mark(("mod_cols", k["s"]), "pe_mod")

        def pe_bias(k):
            pe.wait_ge(sems["bias_in"], at("bias_in"))
            pe.wait_ge(sems["vec_setup"], at("relb"))
            pe.wait_ge(sems["act_setup"], at("cols", 0))
            for i in range(3):
                mm = pe.matmul(PB[0:8, i, 0:LINE], o_set["relb"][:, 8 * i:8 * i + 8], o_set["onehot"][:, i, :],
                               start=True, stop=True)
            mm.then_inc(sems["pe_setup"], 1)
            up("pe_setup", ("lines_ps",))

        def pe_stat(k):
            squares = o_c["msq"] if k["key"].endswith("cm") else SQ
            stat_free(k["s"])
            pe.wait_ge(sems["vec_setup"], at("ones"))
            for f in range(NF):
                pe.wait_ge(sems["act_norm"], at("sq", k["key"], f // 2))
                mm = pe.matmul(STAT[:, 0:T], ONES[:], squares[:, f, :], start=f == 0, stop=f == NF - 1)
            mm.then_inc(sems["pe_norm"], 1)
            up("pe_norm", ("stat", k["s"]))

        def pe_ystat(k):
            if k["c"] == 0:
                stat_free(k["s"])
            pe.wait_ge(sems["act_drain"], at("sqy", k["s"], k["c"]))
            for f in (2 * k["c"], 2 * k["c"] + 1):
                mm = pe.matmul(STAT[:, 0:T], ONES[:], SQ[:, f, :], start=f == 0, stop=f == NF - 1)
            mm.then_inc(sems["pe_norm"], 1)
            up("pe_norm", ("stat", k["s"]) if k["c"] == 3 else None)

        def pe_rstd_cols(k):
            stat_free(k["s"])
            src = o_c["rm"] if k["key"].endswith("cm") else RX
            pe.wait_ge(sems["act_norm"], at("rstd", k["key"]))
            for t in range(TT):
                mm = pe.transpose(STAT[:, t * P:(t + 1) * P], src[:, t * P:(t + 1) * P], IDENT[:])
            mm.then_inc(sems["pe_norm"], 1)
            up("pe_norm", ("rt_ps", k["s"]))

        def pe_qk_norm(k):
            stat_free(k["s"])
            pe.wait_ge(sems["act_drain"], at("asq", k["dst"], k["ft"]))
            pe.wait_ge(sems["consts_in"], at("consts"))
            mm = pe.matmul(STAT[:, :], HEADS[:], ASQ[:, k["b"]].rearrange("p a t -> p (a t)"), start=True, stop=True)
            mm.then_inc(sems["pe_norm"], 1)
            up("pe_norm", ("stat", k["s"]))

        def pe_scores(k):
            c = att(k["cfg"], k["i"])
            if state["scores"] is not None:
                pe.wait_ge(sems["act_attn"], at("exps", *state["scores"]))
            else:
                pe.wait_ge(sems["act_setup"], at("lines_read"))
            state["scores"] = (k["cfg"], k["i"])
            if c["hname"] is not None:
                pe.wait_ge(sems["hankel_in"], at(*c["hname"]))
            if k["cfg"] in ("swa", "moba"):
                pe.wait_ge(sems["vec_norm"], at("qk", "qa" if k["cfg"] == "swa" else "qc", k["i"] // 2 * 2))
                pe.wait_ge(sems["vec_norm"], at("qk", "ka", 0))
            elif k["cfg"][:4] == "diff":
                pe.wait_ge(sems["vec_drain"], at("fm", "q", int(k["cfg"][-1]), k["i"] // 2 * 2))
            else:
                pe.wait_ge(sems["vec_drain"], at("fm", "xq", int(k["cfg"][-1]), 2 * k["i"]))
                pe.wait_ge(sems["vec_drain"], at("fm", "xk", int(k["cfg"][-1]), 6))
            for qt in range(2):
                nk = P * (qt + 1) if c["causal"] else T
                for m in range(c["maps"]):
                    ps = scores_at(c, qt, m, nk)
                    if c["pack"] == "cross":
                        for f in (0, 1):
                            mm = pe.matmul(ps, c["q"][0][f][:, qt * P:(qt + 1) * P], c["k"][0][f], start=f == 0,
                                           stop=f == 1)
                    else:
                        pe.matmul(ps, c["q"][m][:, qt * P:(qt + 1) * P], c["k"][m][:, 0:nk], start=True, stop=False)
                        mm = pe.matmul(ps, FLIP[:], c["hank"][:, c["head"][m], T - nk:T], start=False, stop=True)
            mm.then_inc(sems["pe_attn"], 1)
            up("pe_attn", ("scores", k["cfg"], k["i"]))

        def pe_turn(k):
            c, m = att(k["cfg"], k["i"]), k["m"]
            pe.wait_ge(sems["vec_attn"], at("probs", k["cfg"], k["i"]))
            if m:
                pe.wait_ge(sems["act_attn"], at("pt", k["cfg"], k["i"], 0))
            elif state["att"] is not None:
                pe.wait_ge(sems["vec_attn"], at("o_raw", *state["att"]))
                if state["att"][0][:4] == "diff":
                    pe.wait_ge(sems["act_attn"], at("o_sq", *state["att"]))
            for kb in (0, 1):
                for qt in ((0, 1) if kb == 0 or c["pack"] == "cross" else (1,)):
                    at_ = qt * P if kb == 0 else 2 * P + (qt * P if c["pack"] == "cross" else 0)
                    mm = pe.transpose(TURN[:, at_:at_ + P], c["E"][:, qt, m, kb * P:(kb + 1) * P], IDENT[:])
            mm.then_inc(sems["pe_attn"], 1)
            up("pe_attn", ("turned", k["cfg"], k["i"], m))

        def pe_pv(k):
            c = att(k["cfg"], k["i"])
            pe.wait_ge(sems["act_attn"], at("pt", k["cfg"], k["i"], 1 if c["pack"] == "pair" else 0))
            if c["pack"] == "cross":
                pe.wait_ge(*done(("tm", "xv", int(k["cfg"][-1]), k["i"] * COLS)))
            elif k["cfg"][:4] != "diff":
                pe.wait_ge(*done(("tm", {"swa": "va", "moba": "vc"}[k["cfg"]], 0)))
            PT = c["PT"]
            if c["pack"] == "cross":
                for f in (0, 1):
                    for kb in (0, 1):
                        mm = pe.matmul(PV[:, f * T:(f + 1) * T], c["v"][f][kb], PT[:, kb * T:(kb + 1) * T],
                                       start=kb == 0, stop=kb == 1)
            else:
                for m in range(2 if c["pack"] == "pair" else 1):
                    o = PV[64 * m:64 * m + 64, :] if c["pack"] == "pair" else PV
                    pe.matmul(o[:, 0:T], c["v"][m][0], PT[:, m * 384:m * 384 + T], start=True, stop=False)
                    mm = pe.matmul(o[:, P:T], c["v"][m][1], PT[:, m * 384 + T:m * 384 + T + P], start=False, stop=True)
            mm.then_inc(sems["pe_attn"], 1)
            up("pe_attn", ("o_ps", k["cfg"], k["i"]))
            state["att"] = (k["cfg"], k["i"])

        def pe_subln(k):
            stat_free(k["s"])
            pe.wait_ge(sems["act_attn"], at("o_sq", k["cfg"], k["i"]))
            mm = pe.matmul(STAT[:, :], ONES[:], ASQ[:, k["i"] // 2 % 2].rearrange("p a t -> p (a t)"), start=True,
                           stop=True)
            mm.then_inc(sems["pe_attn"], 1)
            up("pe_attn", ("stat", k["s"]))

        def pe_rnn_gate(k):
            stat_free(k["s"])
            pe.wait_ge(sems["vec_rnn"], at("xc", k["f"]))
            pe.wait_ge(sems["blocks_in"], at("blocks"))
            pe.wait_ge(sems["pool_setup"], at("bd_zero"))
            for g in range(2):
                mm = pe.matmul(STAT[:, g * T:(g + 1) * T], o_b1["bd"][:, k["f"], g, :], o_b1["xc"][:, k["f"], :],
                               start=True, stop=True)
            mm.then_inc(sems["pe_rnn"], 1)
            up("pe_rnn", ("gates", k["f"]))

        def pe_cln_mean(k):
            stat_free(k["s"])
            pe.wait_ge(sems["vec_conv"], at("conv", k["l"]))
            pe.wait_ge(sems["pool_conv"], at("conv_by_pool", k["l"]))
            for f in range(NF):
                mm = pe.matmul(STAT[:, 0:T], ONES[:], Y[:, f, :], start=f == 0, stop=f == NF - 1)
            mm.then_inc(sems["pe_norm"], 1)
            up("pe_norm", ("stat", k["s"]))

        def pe_cln_var(k):
            stat_free(k["s"])
            pe.wait_ge(sems["act_conv"], at("cln_sq", k["l"]))
            for f in range(NF):
                mm = pe.matmul(STAT[:, 0:T], ONES[:], SQ[:, f, :], start=f == 0, stop=f == NF - 1)
            mm.then_inc(sems["pe_norm"], 1)
            up("pe_norm", ("stat", k["s"]))

        def pe_mem_turn(k):
            pe.wait_ge(sems["mem_in"], at("memt", k["l"]))
            if state["att"] is not None:
                pe.wait_ge(sems["vec_attn"], at("o_raw", *state["att"]))
                if state["att"][0][:4] == "diff":
                    pe.wait_ge(sems["act_attn"], at("o_sq", *state["att"]))
            for half in range(2):
                if half:
                    pe.wait_ge(sems["vec_norm"], at("memf", f"l{k['l']}", 0))
                for f in range(4):
                    for t in range(TT):
                        ff = 4 * half + f
                        mm = pe.transpose(PBF[:, f * T + t * P:f * T + (t + 1) * P],
                                          o_c["memt"][:, t, ff * P:(ff + 1) * P], IDENT[:])
                mm.then_inc(sems["pe_norm"], 1)
                up("pe_norm", ("mem_ps", k["l"], half))

        def pe_finish(k):
            pe.wait_ge(sems["vec_norm"], at("x", last_x, 3))
            for p in last_pairs:
                pe.wait_ge(sems["act_drain"], at("evac", p))
            for t in range(TT):
                for f in range(NF):
                    mm = pe.transpose(GPF[:, t * D + f * P:t * D + (f + 1) * P], X[:, f, t * P:(t + 1) * P], IDENT[:])
            mm.then_inc(sems["pe_setup"], 1)
            up("pe_setup", ("out_ps",))

        parts = dict(unit=pe_unit, params=pe_params, turn_x=pe_turn_x, mod=pe_mod, mod_col=pe_mod_col, bias=pe_bias, stat=pe_stat, ystat=pe_ystat,
                     rstd_cols=pe_rstd_cols, qk_norm=pe_qk_norm, scores=pe_scores, turn=pe_turn, pv=pe_pv,
                     subln=pe_subln, rnn_gate=pe_rnn_gate, cln_mean=pe_cln_mean, cln_var=pe_cln_var,
                     mem_turn=pe_mem_turn, finish=pe_finish)
        for kind, k in steps:
            if kind in parts:
                parts[kind](k)

    @block.scalar
    def _(act):
        state = dict(rq=None)
        products = [0]

        def hi(m):
            if m >= len(splits):
                return
            u = splits[m]
            act.wait_ge(*done(("landed", u["raw"])))
            if m >= SPLIT:
                act.wait_ge(sems["gemm_done"], at("unit", splits[m - SPLIT]["n"]))
            s = (slice(None), m % SPLIT, slice(0, u["nkt"]), slice(0, u["cols"]))
            act.copy(WH[s], RAWB[:, u["raw"] % RAW, 0:u["nkt"], 0:u["cols"]]).then_inc(sems["weights_rounded"], 1)
            act.wait_ge(sems["weights_rounded"], up("weights_rounded", ("rounded", m)))

        def rstd(dst, src, scale, eps, sem, name, s):
            act.activation(dst, src, ACT.Ln, bias=EPS[:, eps:eps + 1], scale=scale).then_inc(sems[sem], 1)
            act.wait_ge(sems[sem], up(sem, ("stat_read", s)))
            act.activation(dst, dst, ACT.Exp, scale=-0.5).then_inc(sems[sem], 1)
            act.wait_ge(sems[sem], up(sem, name))

        def act_setup(k):
            act.wait_ge(sems["c_in"], at("c_in"))
            act.activation(o_set["sgc"][:], o_set["c_cols"][:], ACT.Tanh, scale=0.5).then_inc(sems["act_setup"], 1)
            act.wait_ge(sems["act_setup"], up("act_setup", ("c_tanh",)))

        def act_params(k):
            act.wait_ge(sems["pe_setup"], at("rows_T", k["part"]))
            for i in ((0,) if k["part"] == 0 else range(1, len(ROW_TILES))):
                n, at_ = ROW_TILES[i][0], sum(m for m, _ in ROW_TILES[:i])
                act.copy(CT[:, at_:at_ + n], PBF[:, i * P:i * P + n]).then_inc(sems["act_setup"], 1)
                act.wait_ge(sems["act_setup"], up("act_setup", ("cols", k["part"])))
            if k["part"] == 0:
                act.activation(o_set["spt"][:, 0, :], col("lambda", 0, 8), ACT.Abs).then_inc(sems["act_setup"], 1)
                act.wait_ge(sems["act_setup"], up("act_setup"))
                act.activation(o_set["spt"][:, 0, :], o_set["spt"][:, 0, :], ACT.Exp, scale=-1.0).then_inc(sems["act_setup"], 1)
                act.wait_ge(sems["act_setup"], up("act_setup", ("sp_exp",)))
                act.mul(HALFB[:, 0:8], col("gate_a_b", 0, 8), 0.5).then_inc(sems["act_setup"], 1)
                act.wait_ge(sems["act_setup"], up("act_setup"))
                act.mul(HALFB[:, 8:16], col("gate_x_b", 0, 8), 0.5).then_inc(sems["act_setup"], 1)
                act.wait_ge(sems["act_setup"], up("act_setup", ("half_bias",)))
                act.wait_ge(sems["vec_setup"], at("lam_sum"))
                act.activation(o_set["lams"][:], o_set["lams"][:], ACT.Exp).then_inc(sems["act_setup"], 1)
                act.wait_ge(sems["act_setup"], up("act_setup", ("lam_exp",)))

        def act_bias(k):
            act.wait_ge(sems["pe_setup"], at("lines_ps"))
            for i in range(3):
                act.copy(o_set["lines"][:, i, :], PB[0:8, i, 0:LINE]).then_inc(sems["act_setup"], 1)
                act.wait_ge(sems["act_setup"], up("act_setup", ("lines_read",)))

        def act_square(k):
            p = k["p"]
            of_x = k["src"] == "x"
            squares = SQ if of_x else o_c["msq"]
            act.wait_ge(*done(("x", k["v"], p) if of_x else ("memf", k["key"][:2], p // 2)))
            act.activation(squares[:, 2 * p:2 * p + 2, :], BUF[k["src"]][:, 2 * p:2 * p + 2, :],
                           ACT.Square).then_inc(sems["act_norm"], 1)
            act.wait_ge(sems["act_norm"], up("act_norm", ("sq", k["key"], p)))

        def act_rstd(k):
            act.wait_ge(sems["pe_norm"], at("stat", k["s"]))
            rstd({"RX": RX, "RY": RY, "RM": o_c["rm"]}[k["out"]][:], STAT[:, 0:T], 1.0 / D, 0, "act_norm",
                 ("rstd", k["key"]), k["s"])

        def act_adapt(k):
            for f in range(NF):
                act.wait_ge(sems["vec_norm"], at("adapted", k["key"], f))
                if k["after"] is not None:
                    act.wait_ge(sems["gemm_done"], at("unit", k["after"]))
                act.activation(HH[:, f, :], Y[:, f, :], ACT.Identity, bias=MODC[:, 8 * k["shift"] + f:8 * k["shift"] + f + 1]).then_inc(sems["act_split"], 1)
                act.wait_ge(sems["act_split"], up("act_split", ("split_hi", "H", k["key"], f)))

        def act_split(k):
            h = xbuf(k["buf"], k["gen"])[0]
            f = k["f"]
            act.wait_ge(*done(ready_of(k)))
            if k["after"] is not None:
                act.wait_ge(sems["gemm_done"], at("unit", k["after"]))
            src = source(k)
            c = k.get("col")
            scale = 0.5 if k.get("half") else 1.0
            act.activation(h[:, k["ft0"] + f, :], src, ACT.Copy, scale=col(c[0], c[1] + f) if c else scale).then_inc(sems["act_split"], 1)
            act.wait_ge(sems["act_split"], up("act_split", ("split_hi", k["buf"], k["gen"], k["ft0"] + f)))

        def act_evac_y(k):
            act.wait_ge(sems["gemm_done"], at("unit", k["last_unit"]))
            ft = k["ft"]
            if k["sq"] is None:
                act.copy(Y[:, ft:ft + 2, :], slot(k["id"])).then_inc(sems["act_drain"], 1)
                act.wait_ge(sems["act_drain"], up("act_drain", ("evac", k["id"])))
                mark(("y", k["yk"], ft // 2), "act_drain")
                return
            act.activation(SQ[:, ft:ft + 2, :], slot(k["id"]), ACT.Square).then_inc(sems["act_drain"], 1)
            act.wait_ge(sems["act_drain"], up("act_drain", ("sqy", k["sq"], ft // 2)))
            for i in range(2):
                act.activation(Y[:, ft + i, :], slot(k["id"])[:, i, :], ACT.Copy,
                               scale=col(k["gain"][0], k["gain"][1] + ft + i)).then_inc(sems["act_drain"], 1)
                act.wait_ge(sems["act_drain"], up("act_drain", ("evac", k["id"])))
            mark(("y", k["yk"], ft // 2), "act_drain")

        def act_evac_qk(k):
            act.wait_ge(sems["gemm_done"], at("unit", k["last_unit"]))
            b = k["b"]
            if k["before"] is not None:
                act.wait_ge(sems["pe_norm"], at("stat", k["before"]))
            act.activation(ASQ[:, b], slot(k["id"]), ACT.Square).then_inc(sems["act_drain"], 1)
            act.wait_ge(sems["act_drain"], up("act_drain"))
            mark(("asq", k["dst"], k["ft"]), "act_drain")

        def act_qk_norm(k):
            act.wait_ge(sems["pe_norm"], at("stat", k["s"]))
            if state["rq"] is not None:
                act.wait_ge(*done(state["rq"]))
            rstd(RQ[:].rearrange("p a t -> p (a t)"), STAT[:, :], 1.0 / HD, 0, "act_norm", ("rstd_q", k["s"]), k["s"])
            state["rq"] = ("rq_read", k["s"])

        def act_evac_v1(k):
            act.wait_ge(sems["gemm_done"], at("unit", k["last_unit"]))
            act.copy(BUF[k["dst"]][:, :, k["c0"]:k["c0"] + k["cols"]], GP[:, k["id"] % 2, :, 0:k["cols"]]).then_inc(sems["act_drain"], 1)
            act.wait_ge(sems["act_drain"], up("act_drain", ("evac", k["id"])))
            mark(("tm", k["dst"], 0), "act_drain")

        def act_softmax(k):
            c = att(k["cfg"], k["i"])
            act.wait_ge(sems["vec_attn"], at("max", k["cfg"], k["i"]))
            for qt in range(2):
                nk = P * (qt + 1) if c["causal"] else T
                for m in range(c["maps"]):
                    j = 2 * qt + m
                    act.activation(c["E"][:, qt, m, 0:nk], scores_at(c, qt, m, nk), ACT.Exp, bias=NM[:, j:j + 1], accum_out=DEN[:, j:j + 1]).then_inc(sems["act_attn"], 1)
                    act.wait_ge(sems["act_attn"], up("act_attn", ("exps", k["cfg"], k["i"])))
            if k["cfg"] == "swa":
                act.activation(ES[:], ES[:], ACT.Exp).then_inc(sems["act_attn"], 1)
                act.wait_ge(sems["act_attn"], up("act_attn", ("sink_exp", k["cfg"], k["i"])))

        def act_turn(k):
            c, m = att(k["cfg"], k["i"]), k["m"]
            act.wait_ge(sems["pe_attn"], at("turned", k["cfg"], k["i"], m))
            n = 512 if c["pack"] == "cross" else 384
            act.copy(c["PT"][:, m * n:(m + 1) * n], TURN[:, 0:n]).then_inc(sems["act_attn"], 1)
            act.wait_ge(sems["act_attn"], up("act_attn", ("pt", k["cfg"], k["i"], m)))

        def act_pv(k):
            if k["cfg"][:4] == "diff":
                act.wait_ge(sems["pe_attn"], at("o_ps", k["cfg"], k["i"]))
                act.activation(ASQ[:, k["i"] // 2 % 2, k["i"] % 2, :], PV[:, 0:T], ACT.Square).then_inc(sems["act_attn"], 1)
                act.wait_ge(sems["act_attn"], up("act_attn", ("o_sq", k["cfg"], k["i"])))

        def act_subln(k):
            act.wait_ge(sems["pe_attn"], at("stat", k["s"]))
            if state["rq"] is not None:
                act.wait_ge(*done(state["rq"]))
            rstd(RQ[:].rearrange("p a t -> p (a t)"), STAT[:, :], 1.0 / (2 * HD), 0, "act_attn", ("rstd_q", k["s"]), k["s"])
            state["rq"] = ("rq_read", k["s"])

        def act_evac_xr(k):
            act.wait_ge(sems["gemm_done"], at("unit", k["last_unit"]))
            act.wait_ge(sems["vec_rnn"], at("pads1"))
            act.copy(o_b1["xr"][:, k["ft"]:k["ft"] + 2, RNN_K - 1:], slot(k["id"])).then_inc(sems["act_drain"], 1)
            act.wait_ge(sems["act_drain"], up("act_drain", ("evac", k["id"])))
            mark(("xr", k["ft"]), "act_drain")

        def act_evac_yr(k):
            act.wait_ge(sems["gemm_done"], at("unit", k["last_unit"]))
            s = slice(k["ft"], k["ft"] + 2)
            act.copy(Y[:, s, :], slot(k["id"])).then_inc(sems["act_drain"], 1)
            act.wait_ge(sems["act_drain"], up("act_drain"))
            act.activation(SQ[:, s, :], slot(k["id"]), ACT.Square).then_inc(sems["act_drain"], 1)
            act.wait_ge(sems["act_drain"], up("act_drain", ("evac", k["id"])))

        def act_gelu(k):
            s = slice(k["ft"], k["ft"] + 2)
            act.wait_ge(sems["vec_gelu"], at("gelu_in", k["ft"]))
            act.activation(SQ[:, s, :], SQ[:, s, :], ACT.Tanh).then_inc(sems["act_gelu"], 1)
            act.wait_ge(sems["act_gelu"], up("act_gelu", ("gelu_tanh", k["ft"])))

        def act_rnn_gate(k):
            f = k["f"]
            act.wait_ge(sems["pe_rnn"], at("gates", f))
            act.wait_ge(sems["act_setup"], at("half_bias"))
            if f >= 2:
                act.wait_ge(sems["vec_rnn"], at("m2", f - 2))
            for g in range(2):
                act.activation(o_b1["rg"][:, f % 2, g, :], STAT[:, g * T:(g + 1) * T], ACT.Tanh, scale=0.5,
                               bias=HALFB[:, 8 * g + f:8 * g + f + 1]).then_inc(sems["act_rnn"], 1)
                act.wait_ge(sems["act_rnn"], up("act_rnn", ("stat_read", k["s"])))
            mark(("gate_tanh", "rnn", f), "act_rnn")

        def act_rnn_in(k):
            f = k["f"]
            s = o_b1["rg"][:, f % 2, 0, :]
            act.wait_ge(sems["vec_rnn"], at("s", f))
            act.activation(o_b1["xr"][:, f, 0:T], s, ACT.Exp, scale=-1.0).then_inc(sems["act_rnn"], 1)
            act.wait_ge(sems["act_rnn"], up("act_rnn"))
            act.activation(o_b1["s_all"][:, f, :], s, ACT.Tanh).then_inc(sems["act_rnn"], 1)
            act.wait_ge(sems["act_rnn"], up("act_rnn", ("a", f)))

        def act_rnn_sqrt(k):
            for h in range(2):
                s = slice(4 * h, 4 * h + 4)
                act.wait_ge(sems["vec_rnn"], at("m2", 4 * h + 3))
                act.activation(o_b1["s_all"][:, s, :], o_b1["s_all"][:, s, :], ACT.Sqrt,
                               scale=0.25).then_inc(sems["act_rnn"], 1)
                act.wait_ge(sems["act_rnn"], up("act_rnn", ("mult", h)))

        def act_evac_gate(k):
            gt = (o_b1["gt1"] if not k["scaled"] else o_m["gt2"])[:, (k["id"] // 2) % 2]
            if k["scaled"]:
                return
            act.wait_ge(sems["gemm_done"], at("unit", k["last_unit"]))
            act.wait_ge(*done(("evac", k["id"] - 3)))
            act.activation(gt, slot(k["id"]), ACT.Tanh, scale=0.5).then_inc(sems["act_drain"], 1)
            act.wait_ge(sems["act_drain"], up("act_drain", ("evac", k["id"])))
            marks[("gate_tanh", k["id"])] = marks[("evac", k["id"])]

        def act_gate_tanh(k):
            if k.get("mg", ("",))[0] == "b1":
                return
            gt = o_m["gt2"][:, ((k["id"] - 1) // 2) % 2]
            act.wait_ge(sems["vec_drain"], at("evac", k["id"] - 1))
            act.activation(gt, gt, ACT.Tanh, scale=0.5).then_inc(sems["act_drain"], 1)
            act.wait_ge(sems["act_drain"], up("act_drain", ("gate_tanh", k["id"] - 1)))

        def act_ffn_val(k):
            b = k["j"] % 2
            act.wait_ge(sems["vec_ffn"], at("evac", k["id"] - 1))
            act.activation(o_f2["fe"][:, b], o_f2["fa"][:, b], ACT.Tanh, scale=0.5).then_inc(sems["act_ffn"], 1)
            act.wait_ge(sems["act_ffn"], up("act_ffn", ("ffn_tanh", k["x"][1], k["j"])))

        def act_up1(k):
            v, j = k["val"], k["j"]
            if v == 1:
                act.wait_ge(sems["vec_ffn"], at("conv_gate", j))
                act.activation(o_f1["fe1"][:], o_f1["uc"][:, j % 2, 0], ACT.Tanh, scale=0.5).then_inc(sems["act_ffn"], 1)
                act.wait_ge(sems["act_ffn"], up("act_ffn", ("ffn_tanh", "b1u", j)))
            act.wait_ge(sems["gemm_done"], at("unit", k["last_unit"]))
            act.wait_ge(sems["vec_ffn"], at("pads_f1"))
            act.copy(o_f1["up"][:, v, :, FFN_K - 1:], slot(k["id"])).then_inc(sems["act_drain"], 1)
            act.wait_ge(sems["act_drain"], up("act_drain"))
            if j >= 2:
                act.wait_ge(sems["vec_ffn"], at("hidden", "b1u", j - 2))
            for i in range(2):
                f = 22 * v + 2 * j + i
                act.activation(o_f1["uc"][:, j % 2, v, i, :], slot(k["id"])[:, i, :], ACT.Identity,
                               scale=col("ffn_conv_w", 44 * (FFN_K - 1) + f),
                               bias=col("ffn_conv_b", f)).then_inc(sems["act_drain"], 1)
                act.wait_ge(sems["act_drain"], up("act_drain", ("evac", k["id"])))

        def act_hid_split(k):
            h = xbuf("HID", k["gen"])[0]
            src = o_f1["hf1"] if k["gen"] == "b1u" else o_f2["hf"]
            act.wait_ge(sems["vec_ffn"], at("hidden", k["gen"], k["j"]))
            act.copy(h[:, 2 * k["j"]:2 * k["j"] + 2, :], src[:, k["j"] % 2]).then_inc(sems["act_ffn"], 1)
            act.wait_ge(sems["act_ffn"], up("act_ffn", ("hid_hi", k["gen"], k["j"])))

        def act_conv31(k):
            f = k["f"]
            act.wait_ge(sems["vec_conv"], at("glu", k["l"], f // 2 * 2))
            if k["part"] == 0:
                act.activation(Y[:, f, :], o_m["zp"][:, f, 0:T], ACT.Identity, scale=col(f"dw{k['l']}", f), bias=col(f"dw_b{k['l']}", f)).then_inc(sems["act_conv"], 1)
                act.wait_ge(sems["act_conv"], up("act_conv", ("conv0", k["l"], f)))
            if k["by"] == "pool":
                b = products[0] % 2
                if products[0] >= 2:
                    act.wait_ge(sems["pool_conv"], at("products_used", products[0] - 2))
                for i in range(CONV_TAPS):
                    j = 1 + k["part"] * CONV_TAPS + i
                    act.activation(o_m["prod"][:, b, i, :], o_m["zp"][:, f, j:j + T], ACT.Copy,
                                   scale=col(f"dw{k['l']}", 8 * j + f)).then_inc(sems["act_products"], 1)
                    up("act_products", ("products", products[0]))
                products[0] += 1

        def act_cln_mean(k):
            act.wait_ge(sems["pe_norm"], at("stat", k["s"]))
            act.activation(RY[:], STAT[:, 0:T], ACT.Copy, scale=1.0 / D).then_inc(sems["act_conv"], 1)
            act.wait_ge(sems["act_conv"], up("act_conv", ("stat_read", k["s"])))
            mark(("mu", k["l"]), "act_conv")
            act.wait_ge(sems["vec_conv"], at("centred", k["l"]))
            act.activation(SQ[:], Y[:], ACT.Square).then_inc(sems["act_conv"], 1)
            act.wait_ge(sems["act_conv"], up("act_conv", ("cln_sq", k["l"])))

        def act_cln_var(k):
            act.wait_ge(sems["pe_norm"], at("stat", k["s"]))
            rstd(RY[:], STAT[:, 0:T], 1.0 / D, 1, "act_conv", ("cln_rstd", k["l"]), k["s"])

        def act_cln_out(k):
            l, p = k["l"], k["p"]
            s = slice(2 * p, 2 * p + 2)
            act.wait_ge(sems["vec_conv"], at("cln_v", l, p))
            act.activation(Y[:, s, :], o_m["tmp2"][:, s, :], ACT.Tanh, scale=0.5).then_inc(sems["act_conv"], 1)
            act.wait_ge(sems["act_conv"], up("act_conv", ("cln_tanh", l, p)))

        def act_evac_pool_w(k):
            l, g = k["l"], k["g"]
            act.wait_ge(sems["gemm_done"], at("unit", k["last_unit"]))
            for i in range(2):
                f = 2 * g + i
                act.activation(o_m["gh2"][:, f, :], slot(k["id"])[:, i, :], ACT.Copy, scale=col(f"pscale{l}", f)).then_inc(sems["act_split"], 1)
                act.wait_ge(sems["act_split"], up("act_split", ("split_hi", "G", f"l{l}mq", f)))

        def act_finish(k):
            act.wait_ge(sems["pe_setup"], at("out_ps"))
            act.copy(o_o["otok"][:].rearrange("p t d -> p (t d)"), GPF).then_inc(sems["act_setup"], 1)
            act.wait_ge(sems["act_setup"], up("act_setup", ("otok",)))

        parts = dict(setup=act_setup, params=act_params, bias=act_bias, square=act_square, rstd=act_rstd, adapt=act_adapt,
                     split=act_split, evac_y=act_evac_y, evac_qk=act_evac_qk, qk_norm=act_qk_norm,
                     evac_v1=act_evac_v1, softmax=act_softmax, turn=act_turn, pv=act_pv, subln=act_subln,
                     evac_xr=act_evac_xr, evac_yr=act_evac_yr, gelu=act_gelu, rnn_gate=act_rnn_gate, rnn_in=act_rnn_in,
                     rnn_sqrt=act_rnn_sqrt, evac_gate=act_evac_gate, evac_branch=act_gate_tanh, evac_glu=act_gate_tanh, evac_ffn_val=act_ffn_val, evac_up1=act_up1,
                     hid_split=act_hid_split, conv31=act_conv31, cln_mean=act_cln_mean, cln_var=act_cln_var,
                     cln_out=act_cln_out, evac_pool_w=act_evac_pool_w, finish=act_finish)
        for kind, k in steps:
            if kind == "presplit":
                hi(k["m"])
            if kind == "unit":
                hi(k["m"] + AHEAD)
            if kind in parts:
                parts[kind](k)

    @block.vector
    def _(dve):
        def lo(m):
            if m >= len(splits):
                return
            u = splits[m]
            dve.wait_ge(sems["weights_rounded"], at("rounded", m))
            s = (slice(None), m % SPLIT, slice(0, u["nkt"]), slice(0, u["cols"]))
            dve.tensor_tensor(WL[s], RAWB[:, u["raw"] % RAW, 0:u["nkt"], 0:u["cols"]], WH[s], ALU.subtract).then_inc(sems["weights_rest"], 1)
            dve.wait_ge(sems["weights_rest"], up("weights_rest", ("rest", m)))
            mark(("free", u["raw"]), "weights_rest")

        def vec_setup(k):
            V = "vec_setup"
            dve.wait_ge(sems["act_setup"], at("c_tanh"))
            sg = o_set["sgc"][:]
            dve.scalar_tensor_tensor(out=sg, in0=sg, scalar=1.0, in1=o_set["c_cols"][:], op0=ALU.add, op1=ALU.mult).then_inc(sems["vec_setup"], 1)
            dve.wait_ge(sems["vec_setup"], up("vec_setup"))
            dve.tensor_scalar(CC[:], sg, 0.5, None, ALU.mult).then_inc(sems["vec_setup"], 1)
            dve.wait_ge(sems["vec_setup"], up("vec_setup", ("cc",)))
            dve.memset(ONES[:], 1.0).then_inc(sems["vec_setup"], 1)
            dve.wait_ge(sems["vec_setup"], up("vec_setup", ("ones",)))
            dve.memset(EPS[:, 0:1], RMS_EPS).then_inc(sems["vec_setup"], 1)
            dve.wait_ge(sems["vec_setup"], up("vec_setup"))
            dve.memset(EPS[:, 1:2], LN_EPS).then_inc(sems["vec_setup"], 1)
            dve.wait_ge(sems["vec_setup"], up("vec_setup", ("eps",)))
            dve.memset(o_set["relb"][32:33, :], 1.0).then_inc(sems["vec_setup"], 1)
            dve.wait_ge(sems["vec_setup"], up("vec_setup", ("relb",)))
            dve.wait_ge(sems["small_in"], at("small"))
            dve.tensor_scalar(SINK[:], o_set["sinks_in"][:], -1.0, None, ALU.mult).then_inc(sems["vec_setup"], 1)
            dve.wait_ge(sems["vec_setup"], up("vec_setup"))
            lam = o_set["lamb"][:].rearrange("p (a two d) -> p a two d", two=2, d=HD)
            dve.tensor_tensor(o_set["lamp"][:], lam[:, :, 0, :], lam[:, :, 1, :], ALU.mult).then_inc(sems["vec_setup"], 1)
            dve.wait_ge(sems["vec_setup"], up("vec_setup"))
            dve.tensor_reduce(o_set["lams"][:], o_set["lamp"][:], AX_X, ALU.add).then_inc(sems["vec_setup"], 1)
            dve.wait_ge(sems["vec_setup"], up("vec_setup", ("lam_sum",)))

        def vec_turn_x(k):
            V = "vec_setup"
            dve.wait_ge(sems["pe_setup"], at("x_T"))
            for p in range(4):
                dve.tensor_copy(X[:, 2 * p:2 * p + 2, :].rearrange("p f t -> p (f t)"), GPF[:, 2 * p * T:(2 * p + 2) * T]).then_inc(sems["vec_setup"], 1)
                dve.wait_ge(sems["vec_setup"], up("vec_setup", ("x", 0, p)))
            dve.wait_ge(sems["act_setup"], at("sp_exp"))
            e, y, y2, s, t = (o_set["spt"][:, i, :] for i in range(5))
            dve.tensor_scalar(y, e, 2.0, None, ALU.add).then_inc(sems["vec_setup"], 1)
            dve.wait_ge(sems["vec_setup"], up("vec_setup"))
            dve.reciprocal(y, y).then_inc(sems["vec_setup"], 1)
            dve.wait_ge(sems["vec_setup"], up("vec_setup"))
            dve.tensor_tensor(y, y, e, ALU.mult).then_inc(sems["vec_setup"], 1)
            dve.wait_ge(sems["vec_setup"], up("vec_setup"))
            dve.tensor_tensor(y2, y, y, ALU.mult).then_inc(sems["vec_setup"], 1)
            dve.wait_ge(sems["vec_setup"], up("vec_setup"))
            dve.memset(s, 1.0 / 21).then_inc(sems["vec_setup"], 1)
            dve.wait_ge(sems["vec_setup"], up("vec_setup"))
            for n in range(19, 0, -2):
                dve.tensor_tensor(s, s, y2, ALU.mult).then_inc(sems["vec_setup"], 1)
                dve.wait_ge(sems["vec_setup"], up("vec_setup"))
                dve.tensor_scalar(s, s, 1.0 / n, None, ALU.add).then_inc(sems["vec_setup"], 1)
                dve.wait_ge(sems["vec_setup"], up("vec_setup"))
            dve.tensor_tensor(s, s, y, ALU.mult).then_inc(sems["vec_setup"], 1)
            dve.wait_ge(sems["vec_setup"], up("vec_setup"))
            dve.tensor_scalar(t, col("lambda", 0, 8), -1.0, 0.0, ALU.mult, ALU.max).then_inc(sems["vec_setup"], 1)
            dve.wait_ge(sems["vec_setup"], up("vec_setup"))
            dve.scalar_tensor_tensor(out=s, in0=s, scalar=2.0, in1=t, op0=ALU.mult, op1=ALU.add).then_inc(sems["vec_setup"], 1)
            dve.wait_ge(sems["vec_setup"], up("vec_setup"))
            dve.tensor_scalar(SP4[:], s, RGLRU_C / 2, None, ALU.mult).then_inc(sems["vec_setup"], 1)
            dve.wait_ge(sems["vec_setup"], up("vec_setup"))
            dve.wait_ge(sems["act_setup"], at("lam_exp"))
            e_ = o_set["lams"]
            for l in range(LAYERS):
                dve.tensor_tensor(LAM[:, l:l + 1], e_[:, 2 * l + 1:2 * l + 2], e_[:, 2 * l:2 * l + 1], ALU.subtract).then_inc(sems["vec_setup"], 1)
                dve.wait_ge(sems["vec_setup"], up("vec_setup"))
                dve.tensor_scalar(LAM[:, l:l + 1], LAM[:, l:l + 1], -lam_init(l), None, ALU.add).then_inc(sems["vec_setup"], 1)
                dve.wait_ge(sems["vec_setup"], up("vec_setup", ("setup_end",)))

        def vec_params(k):
            if k["part"] == 0:
                return
            V = "vec_setup"
            dve.wait_ge(sems["act_setup"], at("cols", 1))
            g = col("qk_gain", 0, 4)
            for i, by in enumerate((HD ** -0.5, 1.0, HD ** -0.5, 1.0)):
                dve.tensor_scalar(QG[:, i:i + 1], g[:, i:i + 1], by, None, ALU.mult).then_inc(sems["vec_setup"], 1)
                dve.wait_ge(sems["vec_setup"], up("vec_setup"))
            for l in range(LAYERS):
                dve.tensor_scalar(col(f"subln{l}"), col(f"subln{l}"), 1.0 - lam_init(l), None, ALU.mult).then_inc(sems["vec_setup"], 1)
                dve.wait_ge(sems["vec_setup"], up("vec_setup"))

        def vec_mod(u):
            if u["by"] == "tensor":
                return
            acc, raw = ACC[:, u["turn"] % 2, :], RAWB[:, u["raw"] % RAW]
            dve.wait_ge(*done(("landed", u["raw"])))
            if u["half"] == 0 and u["turn"] >= 2:
                dve.wait_ge(sems["pe_mod"], at("mod_added", u["turn"] - 2))
            for kt in range(UNIT_KT):
                c = CC[:, u["kt0"] + kt:u["kt0"] + kt + 1]
                if kt == 0 and u["half"] == 0:
                    dve.tensor_scalar(acc, raw[:, kt, :], c, None, ALU.mult).then_inc(sems["vec_mod"], 1)
                else:
                    dve.scalar_tensor_tensor(out=acc, in0=raw[:, kt, :], scalar=c, in1=acc, op0=ALU.mult,
                                             op1=ALU.add).then_inc(sems["vec_mod"], 1)
                dve.wait_ge(sems["vec_mod"], up("vec_mod", ("mod_partial", u["turn"])))
            mark(("free", u["raw"]), "vec_mod")

        def vec_mod_sum(k):
            s = slice(k["first"], k["first"] + k["count"])
            dve.wait_ge(sems["pe_mod"], at("mod_cols", k["s"]))
            dve.wait_ge(sems["act_setup"], at("cols", 0))
            dve.tensor_tensor(MODC[:, s], STAT[:, 0:k["count"]], col("b_mod", k["first"], k["count"]), ALU.add).then_inc(sems["vec_mod"], 1)
            dve.wait_ge(sems["vec_mod"], up("vec_mod", ("stat_read", k["s"])))

        def vec_adapt(k):
            V = "vec_norm"
            a8 = RT8[:]
            dve.tensor_scalar(a8, MODC[:, 8 * k["scale"]:8 * k["scale"] + 8], 1.0, None, ALU.add).then_inc(sems["vec_norm"], 1)
            dve.wait_ge(sems["vec_norm"], up("vec_norm"))
            dve.tensor_tensor(a8, a8, col(k["norm"], 0, 8), ALU.mult).then_inc(sems["vec_norm"], 1)
            dve.wait_ge(sems["vec_norm"], up("vec_norm"))
            dve.wait_ge(sems["act_norm"], at("rstd", k["rstd"]))
            dve.wait_ge(sems["line_out"], at("lines_out"))
            for f in range(NF):
                dve.scalar_tensor_tensor(out=Y[:, f, :], in0=X[:, f, :], scalar=a8[:, f:f + 1], in1=RX[:], op0=ALU.mult, op1=ALU.mult).then_inc(sems["vec_norm"], 1)
                dve.wait_ge(sems["vec_norm"], up("vec_norm", ("adapted", k["key"], f)))
            for f in range(NF):
                dve.wait_ge(sems["act_split"], at("split_hi", "H", k["key"], f))
                c = 8 * k["shift"] + f
                dve.scalar_tensor_tensor(out=HL[:, f, :], in0=Y[:, f, :], scalar=MODC[:, c:c + 1], in1=HH[:, f, :], op0=ALU.add, op1=ALU.subtract).then_inc(sems["vec_norm"], 1)
                dve.wait_ge(sems["vec_norm"], up("vec_norm", ("split", "H", k["key"], f)))

        def vec_split(k):
            h, l_ = xbuf(k["buf"], k["gen"])
            f, d = k["f"], k["ft0"] + k["f"]
            src = source(k)
            c = k.get("col")
            dve.wait_ge(sems["act_split"], at("split_hi", k["buf"], k["gen"], d))
            if c or k.get("half"):
                ins = dve.scalar_tensor_tensor(out=l_[:, d, :], in0=src, scalar=col(c[0], c[1] + f) if c else 0.5,
                                               in1=h[:, d, :], op0=ALU.mult, op1=ALU.subtract)
            else:
                ins = dve.tensor_tensor(l_[:, d, :], src, h[:, d, :], ALU.subtract)
            ins.then_inc(sems["vec_split"], 1)
            dve.wait_ge(sems["vec_split"], up("vec_split", ("split", k["buf"], k["gen"], d)))

        def vec_residual(k):
            p = k["p"]
            s = slice(2 * p, 2 * p + 2)
            dve.wait_ge(sems["act_drain"], at("y", k["key"], p))
            if k["form"] == "gate_mod":
                for f in (2 * p, 2 * p + 1):
                    c = 8 * k["chunk"] + f
                    dve.scalar_tensor_tensor(out=X[:, f, :], in0=Y[:, f, :], scalar=MODC[:, c:c + 1], in1=X[:, f, :],
                                             op0=ALU.mult, op1=ALU.add).then_inc(sems["vec_norm"], 1)
                    dve.wait_ge(sems["vec_norm"], up("vec_norm", ("x", k["v"], p)))
                return
            dve.wait_ge(sems["act_norm"], at("rstd", k["key"] + "y"))
            dve.tensor_tensor(Y[:, s, :], Y[:, s, :], bc(RY[:]), ALU.mult).then_inc(sems["vec_norm"], 1)
            dve.wait_ge(sems["vec_norm"], up("vec_norm"))
            dve.scalar_tensor_tensor(out=X[:, s, :], in0=Y[:, s, :], scalar=0.5 if k["half"] else 1.0, in1=X[:, s, :],
                                     op0=ALU.mult, op1=ALU.add).then_inc(sems["vec_norm"], 1)
            dve.wait_ge(sems["vec_norm"], up("vec_norm", ("x", k["v"], p)))

        def vec_rstd_cols(k):
            dve.wait_ge(sems["pe_norm"], at("rt_ps", k["s"]))
            dve.tensor_copy(RT[:], STAT.rearrange("p (t q) -> p t q", q=P)[:, 0:TT, 0]).then_inc(sems["vec_norm"], 1)
            dve.wait_ge(sems["vec_norm"], up("vec_norm", ("stat_read", k["s"])))

        def vec_evac_qk(k):
            dve.wait_ge(sems["act_drain"], at("asq", k["dst"], k["ft"]))
            dve.tensor_copy(BUF[k["dst"]][:, k["ft"]:k["ft"] + 2, :], slot(k["id"])).then_inc(sems["vec_drain"], 1)
            dve.wait_ge(sems["vec_drain"], up("vec_drain", ("evac", k["id"])))

        def vec_qk_norm(k):
            d = BUF[k["dst"]][:, k["ft"]:k["ft"] + 2, :]
            dve.wait_ge(sems["act_norm"], at("rstd_q", k["s"]))
            dve.scalar_tensor_tensor(out=d, in0=d, scalar=QG[:, k["gain"]:k["gain"] + 1], in1=RQ[:], op0=ALU.mult, op1=ALU.mult).then_inc(sems["vec_norm"], 1)
            dve.wait_ge(sems["vec_norm"], up("vec_norm", ("rq_read", k["s"])))
            mark(("qk", k["dst"], k["ft"]), "vec_norm")

        def vec_scaled(k):
            dve.wait_ge(sems["gemm_done"], at("unit", k["last_unit"]))
            dve.wait_ge(sems["act_norm"], at("rstd", k["x"][1]))
            dve.scalar_tensor_tensor(out=BUF[k["dst"]][:, k["ft"]:k["ft"] + 2, :], in0=slot(k["id"]), scalar=k["by"], in1=bc((o_c["rm"] if k["x"][0] == "M" else RX)[:]), op0=ALU.mult, op1=ALU.mult).then_inc(sems["vec_drain"], 1)
            dve.wait_ge(sems["vec_drain"], up("vec_drain", ("evac", k["id"])))
            mark(("fm", k["dst"], k["l"], k["ft"]), "vec_drain")

        def vec_v2(k):
            dve.wait_ge(sems["gemm_done"], at("unit", k["last_unit"]))
            for t in range(TT):
                dve.tensor_scalar(BUF[k["dst"]][:, t, k["c0"]:k["c0"] + COLS], slot(k["id"])[:, t, :], RT[:, t:t + 1], None, ALU.mult).then_inc(sems["vec_drain"], 1)
                dve.wait_ge(sems["vec_drain"], up("vec_drain", ("evac", k["id"])))
            mark(("tm", k["dst"], k["l"]), "vec_drain")
            mark(("tm", k["dst"], k["l"], k["c0"]), "vec_drain")

        def vec_softmax(k):
            V, c = "vec_attn", att(k["cfg"], k["i"])
            M = c["maps"]
            dve.wait_ge(sems["pe_attn"], at("scores", k["cfg"], k["i"]))
            for qt in range(2):
                nk = P * (qt + 1) if c["causal"] else T
                dve.tensor_reduce(NM[:, 2 * qt:2 * qt + M], PB[:, 0:2, P * qt:P * qt + nk] if M == 2 else PB[:, qt, 0:nk], AX_X, ALU.max, negate=True).then_inc(sems["vec_attn"], 1)
                dve.wait_ge(sems["vec_attn"], up("vec_attn", ("max", k["cfg"], k["i"])))
            sink = k["cfg"] == "swa"
            if sink:
                i = k["i"]
                for qt in range(2):
                    j = slice(2 * qt, 2 * qt + 2)
                    dve.tensor_tensor(NM[:, j], NM[:, j], SINK[:, 2 * i:2 * i + 2], ALU.min).then_inc(sems["vec_attn"], 1)
                    dve.wait_ge(sems["vec_attn"], up("vec_attn"))
                for qt in range(2):
                    j = slice(2 * qt, 2 * qt + 2)
                    dve.tensor_tensor(ES[:, j], NM[:, j], SINK[:, 2 * i:2 * i + 2], ALU.subtract).then_inc(sems["vec_attn"], 1)
                    dve.wait_ge(sems["vec_attn"], up("vec_attn", ("max", k["cfg"], k["i"])))
                dve.wait_ge(sems["act_attn"], at("sink_exp", k["cfg"], k["i"]))
            dve.wait_ge(sems["act_attn"], at("exps", k["cfg"], k["i"]))
            js = slice(0, 4) if M == 2 else slice(0, 3, 2)
            if sink:
                dve.tensor_tensor(DEN[:], DEN[:], ES[:], ALU.add).then_inc(sems["vec_attn"], 1)
                dve.wait_ge(sems["vec_attn"], up("vec_attn"))
            dve.reciprocal(RD[:, js], DEN[:, js]).then_inc(sems["vec_attn"], 1)
            dve.wait_ge(sems["vec_attn"], up("vec_attn"))
            E = c["E"]
            if c["pack"] == "diff":
                l = int(k["cfg"][-1])
                dve.tensor_scalar(RD[:, 1:4:2], RD[:, 1:4:2], LAM[:, l:l + 1], None, ALU.mult).then_inc(sems["vec_attn"], 1)
                dve.wait_ge(sems["vec_attn"], up("vec_attn"))
                for qt in range(2):
                    nk = P * (qt + 1)
                    dve.tensor_scalar(E[:, qt, 1, 0:nk], E[:, qt, 1, 0:nk], RD[:, 2 * qt + 1:2 * qt + 2], None, ALU.mult).then_inc(sems["vec_attn"], 1)
                    dve.wait_ge(sems["vec_attn"], up("vec_attn"))
                    dve.scalar_tensor_tensor(out=E[:, qt, 0, 0:nk], in0=E[:, qt, 0, 0:nk], scalar=RD[:, 2 * qt:2 * qt + 1], in1=E[:, qt, 1, 0:nk], op0=ALU.mult, op1=ALU.add).then_inc(sems["vec_attn"], 1)
                    dve.wait_ge(sems["vec_attn"], up("vec_attn", ("probs", k["cfg"], k["i"])))
            else:
                for qt in range(2):
                    nk = P * (qt + 1) if c["causal"] else T
                    for m in range(M):
                        j = 2 * qt + m
                        dve.tensor_scalar(E[:, qt, m, 0:nk], E[:, qt, m, 0:nk], RD[:, j:j + 1], None, ALU.mult).then_inc(sems["vec_attn"], 1)
                        dve.wait_ge(sems["vec_attn"], up("vec_attn", ("probs", k["cfg"], k["i"])))

        def vec_pv(k):
            c = att(k["cfg"], k["i"])
            dve.wait_ge(sems["pe_attn"], at("o_ps", k["cfg"], k["i"]))
            if c["pack"] == "diff":
                dve.wait_ge(sems["act_attn"], at("o_sq", k["cfg"], k["i"]))
            src = PV[:, 0:T] if c["pack"] != "cross" else PV.rearrange("p (f t) -> p f t", f=2)
            dve.tensor_copy(c["o"], src).then_inc(sems["vec_attn"], 1)
            dve.wait_ge(sems["vec_attn"], up("vec_attn", ("o_raw", k["cfg"], k["i"])))
            if c["pack"] != "diff":
                mark(("o", k["cfg"], k["i"]), "vec_attn")

        def vec_subln(k):
            o = o_m["q"][:, k["i"] - 1:k["i"] + 1, :]
            dve.wait_ge(sems["act_attn"], at("rstd_q", k["s"]))
            dve.scalar_tensor_tensor(out=o, in0=o, scalar=col("subln" + k["cfg"][-1]), in1=RQ[:], op0=ALU.mult,
                                     op1=ALU.mult).then_inc(sems["vec_attn"], 1)
            dve.wait_ge(sems["vec_attn"], up("vec_attn", ("rq_read", k["s"])))
            mark(("o", k["cfg"], k["i"] - 1), "vec_attn")
            mark(("o", k["cfg"], k["i"]), "vec_attn")

        def vec_pads1(k):
            dve.wait_ge(sems["vec_norm"], at("split", "H", "b1h", 7))
            dve.memset(o_b1["xr"][:, :, 0:RNN_K - 1], 0.0).then_inc(sems["vec_rnn"], 1)
            dve.wait_ge(sems["vec_rnn"], up("vec_rnn", ("pads1",)))

        def vec_pads_f1(k):
            dve.memset(o_f1["up"][:, :, :, 0:FFN_K - 1], 0.0).then_inc(sems["vec_ffn"], 1)
            dve.wait_ge(sems["vec_ffn"], up("vec_ffn", ("pads_f1",)))

        def vec_rnn_conv(k):
            f, V = k["f"], "vec_rnn"
            dve.wait_ge(sems["act_drain"], at("xr", f // 2 * 2))
            xr, xc = o_b1["xr"], o_b1["xc"]
            dve.tensor_scalar(xc[:, f, :], xr[:, f, 0:T], col("rnn_conv_w", f), col("rnn_conv_b", f), ALU.mult, ALU.add).then_inc(sems["vec_rnn"], 1)
            dve.wait_ge(sems["vec_rnn"], up("vec_rnn"))
            for j in range(1, RNN_K):
                dve.scalar_tensor_tensor(out=xc[:, f, :], in0=xr[:, f, j:j + T], scalar=col("rnn_conv_w", 8 * j + f), in1=xc[:, f, :], op0=ALU.mult, op1=ALU.add).then_inc(sems["vec_rnn"], 1)
                dve.wait_ge(sems["vec_rnn"], up("vec_rnn", ("xc", f)))

        def vec_rnn_in(k):
            f = k["f"]
            dve.wait_ge(sems["act_rnn"], at("gate_tanh", "rnn", f))
            rg, xc = o_b1["rg"][:, f % 2], o_b1["xc"][:, f, :]
            dve.tensor_scalar(rg[:, 0, :], rg[:, 0, :], 1.0, SP4[:, f:f + 1], ALU.add,
                              ALU.mult).then_inc(sems["vec_rnn"], 1)
            dve.wait_ge(sems["vec_rnn"], up("vec_rnn", ("s", f)))
            dve.scalar_tensor_tensor(out=xc, in0=rg[:, 1, :], scalar=1.0, in1=xc, op0=ALU.add,
                                     op1=ALU.mult).then_inc(sems["vec_rnn"], 1)
            dve.wait_ge(sems["vec_rnn"], up("vec_rnn", ("rnn_in", f)))

        def vec_rnn_mult(k):
            f = k["f"]
            t, sq, av = o_b1["s_all"][:, f, :], o_b1["rg"][:, f % 2, 0, :], o_b1["xr"][:, f, 0:T]
            dve.wait_ge(sems["act_rnn"], at("a", f))
            dve.tensor_tensor(sq, av, av, ALU.mult).then_inc(sems["vec_rnn"], 1)
            dve.wait_ge(sems["vec_rnn"], up("vec_rnn"))
            dve.scalar_tensor_tensor(out=t, in0=sq, scalar=1.0, in1=t, op0=ALU.add,
                                     op1=ALU.mult).then_inc(sems["vec_rnn"], 1)
            dve.wait_ge(sems["vec_rnn"], up("vec_rnn"))
            dve.tensor_scalar(t, t, 1e-34, None, ALU.max).then_inc(sems["vec_rnn"], 1)
            dve.wait_ge(sems["vec_rnn"], up("vec_rnn", ("m2", f)))

        def vec_rnn_scan(k):
            s, xc = o_b1["s_all"], o_b1["xc"]
            for f in (2 * k["p"], 2 * k["p"] + 1):
                dve.wait_ge(sems["act_rnn"], at("mult", f // 4))
                dve.memset(s[:, f, 0:1], 0.5).then_inc(sems["vec_rnn"], 1)
                dve.wait_ge(sems["vec_rnn"], up("vec_rnn"))
                dve.tensor_tensor(xc[:, f, :], xc[:, f, :], s[:, f, :], ALU.mult).then_inc(sems["vec_rnn"], 1)
                dve.wait_ge(sems["vec_rnn"], up("vec_rnn"))
                dve.tensor_tensor_scan(s[:, f, :], o_b1["xr"][:, f, 0:T], xc[:, f, :], 0.0, ALU.mult,
                                       ALU.add).then_inc(sems["vec_rnn"], 1)
                dve.wait_ge(sems["vec_rnn"], up("vec_rnn"))
                dve.tensor_tensor(xc[:, f, :], s[:, f, :], Y[:, f, :], ALU.mult).then_inc(sems["vec_rnn"], 1)
                dve.wait_ge(sems["vec_rnn"], up("vec_rnn", ("ob", f)))

        def vec_evac_yr(k):
            s = slice(k["ft"], k["ft"] + 2)
            c = math.sqrt(2.0 / math.pi)
            dve.wait_ge(sems["act_drain"], at("evac", k["id"]))
            dve.tensor_scalar(SQ[:, s, :], SQ[:, s, :], 0.044715 * c, c, ALU.mult, ALU.add).then_inc(sems["vec_gelu"], 1)
            dve.wait_ge(sems["vec_gelu"], up("vec_gelu"))
            dve.tensor_tensor(SQ[:, s, :], SQ[:, s, :], Y[:, s, :], ALU.mult).then_inc(sems["vec_gelu"], 1)
            dve.wait_ge(sems["vec_gelu"], up("vec_gelu", ("gelu_in", k["ft"])))

        def vec_gelu(k):
            s = slice(k["ft"], k["ft"] + 2)
            dve.wait_ge(sems["act_gelu"], at("gelu_tanh", k["ft"]))
            dve.scalar_tensor_tensor(out=Y[:, s, :], in0=SQ[:, s, :], scalar=1.0, in1=Y[:, s, :], op0=ALU.add, op1=ALU.mult).then_inc(sems["vec_gelu"], 1)
            dve.wait_ge(sems["vec_gelu"], up("vec_gelu"))

        def vec_evac_gate(k):
            if k["scaled"]:
                dve.wait_ge(sems["gemm_done"], at("unit", k["last_unit"]))
                dve.wait_ge(sems["act_norm"], at("rstd", k["x"][1]))
                dve.tensor_tensor(o_m["gt2"][:, (k["id"] // 2) % 2], slot(k["id"]), bc(RX[:]), ALU.mult).then_inc(sems["vec_drain"], 1)
                dve.wait_ge(sems["vec_drain"], up("vec_drain", ("evac", k["id"])))

        def vec_evac_branch(k):
            b1 = k["mg"][0] == "b1"
            gt = (o_b1["gt1"] if b1 else o_m["gt2"])[:, ((k["id"] - 1) // 2) % 2]
            bt = o_b1["bt1"] if b1 else o_m["bt2"]
            mg = MGS["b1" if b1 else "m"][:, k["ft"]:k["ft"] + 2, :]
            dve.wait_ge(sems["gemm_done"], at("unit", k["last_unit"]))
            dve.wait_ge(sems["act_drain"], at("gate_tanh", k["id"] - 1))
            name = ("mg", *k["mg"], k["ft"] // 2)
            out_ = mg if k["first_branch"] else bt[:]
            dve.scalar_tensor_tensor(out=out_, in0=gt, scalar=1.0, in1=slot(k["id"]), op0=ALU.add, op1=ALU.mult).then_inc(sems["vec_drain"], 1)
            dve.wait_ge(sems["vec_drain"], up("vec_drain", ("evac", k["id"])))
            if not k["first_branch"]:
                dve.tensor_tensor(mg, mg, bt[:], ALU.add).then_inc(sems["vec_drain"], 1)
                dve.wait_ge(sems["vec_drain"], up("vec_drain", name))

        def vec_ffn_gate(k):
            b = k["j"] % 2
            dve.wait_ge(sems["gemm_done"], at("unit", k["last_unit"]))
            dve.wait_ge(sems["act_norm"], at("rstd", k["x"][1]))
            dve.tensor_tensor(o_f2["fa"][:, b], slot(k["id"]), bc(RX[:]), ALU.mult).then_inc(sems["vec_ffn"], 1)
            dve.wait_ge(sems["vec_ffn"], up("vec_ffn", ("evac", k["id"])))

        def vec_ffn_val(k):
            b, V, key = k["j"] % 2, "vec_ffn", k["x"][1]
            fa, fe, fb = o_f2["fa"][:, b], o_f2["fe"][:, b], o_f2["fb"]
            dve.wait_ge(sems["gemm_done"], at("unit", k["last_unit"]))
            dve.scalar_tensor_tensor(out=fb[:], in0=slot(k["id"]), scalar=0.5, in1=bc(RX[:]), op0=ALU.mult, op1=ALU.mult).then_inc(sems["vec_ffn"], 1)
            dve.wait_ge(sems["vec_ffn"], up("vec_ffn", ("evac", k["id"])))
            dve.wait_ge(sems["act_ffn"], at("ffn_tanh", key, k["j"]))
            dve.scalar_tensor_tensor(out=fa, in0=fe, scalar=1.0, in1=fa, op0=ALU.add,
                                     op1=ALU.mult).then_inc(sems["vec_ffn"], 1)
            dve.wait_ge(sems["vec_ffn"], up("vec_ffn"))
            if k["j"] >= 2:
                dve.wait_ge(sems["hidden_rest"], at("split", "HID", key, 2 * (k["j"] - 2)))
            dve.tensor_tensor(o_f2["hf"][:, b], fa, fb[:], ALU.mult).then_inc(sems["vec_ffn"], 1)
            dve.wait_ge(sems["vec_ffn"], up("vec_ffn", ("hidden", key, k["j"])))

        def vec_up1(k):
            v, j = k["val"], k["j"]
            raw_up, uc = o_f1["up"], o_f1["uc"][:, j % 2]
            dve.wait_ge(sems["act_drain"], at("evac", k["id"]))
            for i in range(2):
                f = 22 * v + 2 * j + i
                for n in range(FFN_K - 1):
                    dve.scalar_tensor_tensor(out=uc[:, v, i, :], in0=raw_up[:, v, i, n:n + T],
                                             scalar=col("ffn_conv_w", 44 * n + f), in1=uc[:, v, i, :], op0=ALU.mult,
                                             op1=ALU.add).then_inc(sems["vec_ffn"], 1)
                    dve.wait_ge(sems["vec_ffn"], up("vec_ffn", ("conv_gate" if v == 0 else "conv_val", j)))
            if v == 1:
                dve.wait_ge(sems["act_ffn"], at("ffn_tanh", "b1u", j))
                dve.scalar_tensor_tensor(out=uc[:, 0], in0=o_f1["fe1"][:], scalar=1.0, in1=uc[:, 0], op0=ALU.add,
                                         op1=ALU.mult).then_inc(sems["vec_ffn"], 1)
                dve.wait_ge(sems["vec_ffn"], up("vec_ffn"))
                if j >= 2:
                    dve.wait_ge(sems["hidden_rest"], at("split", "HID", "b1u", 2 * (j - 2)))
                dve.scalar_tensor_tensor(out=o_f1["hf1"][:, j % 2], in0=uc[:, 0], scalar=0.5, in1=uc[:, 1],
                                         op0=ALU.mult, op1=ALU.mult).then_inc(sems["vec_ffn"], 1)
                dve.wait_ge(sems["vec_ffn"], up("vec_ffn", ("hidden", "b1u", j)))

        def vec_pads2(k):
            V = "vec_conv"
            dve.wait_ge(sems["gemm_done"], at("unit", k["hid_unit"]))
            dve.memset(o_m["zp"][:, :, 0:CONV_K - 1], 0.0).then_inc(sems["vec_conv"], 1)
            dve.wait_ge(sems["vec_conv"], up("vec_conv"))
            dve.memset(o_m["pu"][:, :, 0:POOL_PAD], 0.0).then_inc(sems["vec_conv"], 1)
            dve.wait_ge(sems["vec_conv"], up("vec_conv", ("pads2", k["l"])))

        def vec_glu(k):
            gt, bt = o_m["gt2"][:, ((k["id"] - 1) // 2) % 2], o_m["bt2"]
            dve.wait_ge(sems["gemm_done"], at("unit", k["last_unit"]))
            dve.wait_ge(sems["act_drain"], at("gate_tanh", k["id"] - 1))
            dve.scalar_tensor_tensor(out=bt[:], in0=slot(k["id"]), scalar=0.5, in1=bc(RX[:]), op0=ALU.mult, op1=ALU.mult).then_inc(sems["vec_conv"], 1)
            dve.wait_ge(sems["vec_conv"], up("vec_conv", ("evac", k["id"])))
            dve.scalar_tensor_tensor(out=o_m["zp"][:, k["ft"]:k["ft"] + 2, CONV_K - 1:], in0=gt, scalar=1.0, in1=bt[:], op0=ALU.add, op1=ALU.mult).then_inc(sems["vec_conv"], 1)
            dve.wait_ge(sems["vec_conv"], up("vec_conv", ("glu", k["l"], k["ft"])))

        def vec_conv31(k):
            if k["by"] == "pool":
                return
            l, f = k["l"], k["f"]
            dve.wait_ge(sems["act_conv"], at("conv0", l, f))
            for j in range(1 + k["part"] * CONV_TAPS, 1 + (k["part"] + 1) * CONV_TAPS):
                dve.scalar_tensor_tensor(out=Y[:, f, :], in0=o_m["zp"][:, f, j:j + T], scalar=col(f"dw{l}", 8 * j + f), in1=Y[:, f, :], op0=ALU.mult, op1=ALU.add).then_inc(sems["vec_conv"], 1)
                dve.wait_ge(sems["vec_conv"], up("vec_conv", ("conv", l)))

        def vec_pool_in(k):
            dve.wait_ge(sems["gemm_done"], at("unit", k["last_unit"]))
            dve.tensor_tensor(o_m["pu"][:, k["ft"]:k["ft"] + 2, POOL_PAD:], slot(k["id"]), bc(RX[:]), ALU.mult).then_inc(sems["vec_conv"], 1)
            dve.wait_ge(sems["vec_conv"], up("vec_conv", ("evac", k["id"])))
            mark(("pool_in", k["l"], k["ft"] // 2), "vec_conv")

        def vec_pool_w(k):
            l, g = k["l"], k["g"]
            dve.wait_ge(sems["gemm_done"], at("unit", k["last_unit"]))
            for i in range(2):
                f = 2 * g + i
                dve.wait_ge(sems["act_split"], at("split_hi", "G", f"l{l}mq", f))
                dve.scalar_tensor_tensor(out=o_m["gl2"][:, f, :], in0=slot(k["id"])[:, i, :], scalar=col(f"pscale{l}", f), in1=o_m["gh2"][:, f, :], op0=ALU.mult, op1=ALU.subtract).then_inc(sems["vec_split"], 1)
                dve.wait_ge(sems["vec_split"], up("vec_split", ("split", "G", f"l{l}mq", f)))
            mark(("evac", k["id"]), "vec_split")

        def vec_cln_mean(k):
            dve.wait_ge(sems["act_conv"], at("mu", k["l"]))
            dve.wait_ge(sems["vec_conv"], at("conv", k["l"]))
            dve.wait_ge(sems["pool_conv"], at("conv_by_pool", k["l"]))
            dve.tensor_tensor(Y[:], Y[:], bc(RY[:], NF), ALU.subtract).then_inc(sems["vec_conv"], 1)
            dve.wait_ge(sems["vec_conv"], up("vec_conv", ("centred", k["l"])))

        def vec_cln_out(k):
            l, p, t = k["l"], k["p"], o_m["tmp2"]
            s = slice(2 * p, 2 * p + 2)
            dve.wait_ge(sems["act_conv"], at("cln_rstd", l))
            dve.tensor_tensor(Y[:, s, :], Y[:, s, :], bc(RY[:]), ALU.mult).then_inc(sems["vec_conv"], 1)
            dve.wait_ge(sems["vec_conv"], up("vec_conv"))
            for f in (2 * p, 2 * p + 1):
                dve.tensor_scalar(t[:, f, :], Y[:, f, :], col(f"ln_g{l}", f), col(f"ln_b{l}", f), ALU.mult,
                                  ALU.add).then_inc(sems["vec_conv"], 1)
                dve.wait_ge(sems["vec_conv"], up("vec_conv", ("cln_v", l, p)))
            dve.wait_ge(sems["act_conv"], at("cln_tanh", l, p))
            dve.scalar_tensor_tensor(out=t[:, s, :], in0=Y[:, s, :], scalar=1.0, in1=t[:, s, :], op0=ALU.add,
                                     op1=ALU.mult).then_inc(sems["vec_conv"], 1)
            dve.wait_ge(sems["vec_conv"], up("vec_conv", ("cln", f"l{l}", 2 * p)))
            mark(("cln", f"l{l}", 2 * p + 1), "vec_conv")

        def vec_mem_turn(k):
            for half in range(2):
                dve.wait_ge(sems["pe_norm"], at("mem_ps", k["l"], half))
                dve.tensor_copy(o_c["memf"][:, 4 * half:4 * half + 4, :].rearrange("p f t -> p (f t)"), PBF[:, 0:1024]).then_inc(sems["vec_norm"], 1)
                dve.wait_ge(sems["vec_norm"], up("vec_norm", ("memf", f"l{k['l']}", half)))

        parts = dict(setup=vec_setup, params=vec_params, turn_x=vec_turn_x, mod=vec_mod, mod_sum=vec_mod_sum, adapt=vec_adapt, split=vec_split,
                     residual=vec_residual, rstd_cols=vec_rstd_cols, evac_qk=vec_evac_qk, qk_norm=vec_qk_norm,
                     evac_scaled=vec_scaled, evac_v2=vec_v2, softmax=vec_softmax, pv=vec_pv, subln=vec_subln,
                     pads1=vec_pads1, pads_f1=vec_pads_f1, rnn_conv=vec_rnn_conv, rnn_in=vec_rnn_in, rnn_mult=vec_rnn_mult, evac_yr=vec_evac_yr, gelu=vec_gelu, conv31=vec_conv31, rnn_scan=vec_rnn_scan,
                     evac_gate=vec_evac_gate, evac_branch=vec_evac_branch, evac_ffn_gate=vec_ffn_gate,
                     evac_ffn_val=vec_ffn_val, evac_up1=vec_up1, pads2=vec_pads2,
                     evac_glu=vec_glu, evac_pool=vec_pool_in, evac_pool_w=vec_pool_w,
                     cln_mean=vec_cln_mean, cln_out=vec_cln_out, mem_turn=vec_mem_turn)
        for kind, k in steps:
            if kind == "presplit":
                lo(k["m"])
            if kind == "unit":
                lo(k["m"] + AHEAD)
            if kind in parts:
                parts[kind](k)

    @block.gpsimd
    def _(pool):
        products = [0]
        def pool_setup(k):
            pool.dma_start(o_set["sinks_in"][:], bass.AP(tensor=a["sinks"].tensor, offset=0, ap=[[0, P], [1, 8]])).then_inc(sems["small_in"], 16)
            up("small_in", by=16)
            pool.dma_start(o_set["lamb"][:], bass.AP(tensor=a["attn_lam_2"].tensor, offset=0, ap=[[0, P], [1, LAYERS * 4 * HD]])).then_inc(sems["small_in"], 16)
            up("small_in", ("small",), by=16)
            pool.dma_start(o_set["onehot"][:], a["onehot"]).then_inc(sems["bias_in"], 16)
            up("bias_in", by=16)
            pool.dma_start(o_set["relb"][0:32, 0:16], a["rel_bias"]).then_inc(sems["bias_in"], 16)
            up("bias_in", by=16)
            pool.dma_start(o_set["relb"][0:32, 16:24], a["rel_bias_2"]).then_inc(sems["bias_in"], 16)
            up("bias_in", ("bias_in",), by=16)

        def pool_bias(k):
            pool.wait_ge(sems["act_setup"], at("lines_read"))
            pool.dma_start(scratch.rearrange("i h j -> h i j"), o_set["lines"][:]).then_inc(sems["line_out"], 16)
            up("line_out", ("lines_out",), by=16)

        def pool_hankel(k):
            pool.wait_ge(sems["line_out"], at("lines_out"))
            pool.wait_ge(sems["vec_setup"], at("setup_end"))
            if k["after"] is not None:
                pool.wait_ge(*done(k["after"]))
            dst = o_m["hank2"] if k["which"] == 2 else o_b1["hank1"]
            src = bass.AP(tensor=scratch.tensor, offset=k["which"] * 8 * LINE, ap=[[1, P], [LINE, 8], [1, T]])
            pool.dma_start(dst[:], src).then_inc(sems["hankel_in"], 16)
            up("hankel_in", ("hank", k["which"], k["l"]), by=16)
            if k["which"] == 2:
                pool.dma_start(o_m["cnt"][:], bass.AP(tensor=a["inv_count"].tensor, offset=0, ap=[[0, P], [1, 4 * T]])).then_inc(sems["count_in"], 16)
                up("count_in", ("cnt", k["l"]), by=16)

        def pool_blocks(k):
            pool.wait_ge(sems["line_out"], at("lines_out"))
            pool.wait_ge(sems["vec_setup"], at("setup_end"))
            pool.memset(o_b1["bd"][:], 0.0).then_inc(sems["pool_setup"], 1)
            pool.wait_ge(sems["pool_setup"], up("pool_setup", ("bd_zero",)))
            for g, n in enumerate(("rnn_gate_a_w", "rnn_gate_x_w")):
                w = a[n][0].rearrange("(f two) k n -> two k f n", two=2)
                for h in range(2):
                    pool.dma_start(o_b1["bd"][h * HD:(h + 1) * HD, :, g, h * HD:(h + 1) * HD], w[h]).then_inc(sems["blocks_in"], 16)
                    up("blocks_in", ("blocks",), by=16)

        def pool_hid_split(k):
            h, l_ = xbuf("HID", k["gen"])
            src = (o_f1["hf1"] if k["gen"] == "b1u" else o_f2["hf"])[:, k["j"] % 2]
            s = slice(2 * k["j"], 2 * k["j"] + 2)
            pool.wait_ge(sems["act_ffn"], at("hid_hi", k["gen"], k["j"]))
            pool.tensor_tensor(l_[:, s, :], src, h[:, s, :], ALU.subtract).then_inc(sems["hidden_rest"], 1)
            up("hidden_rest", ("split", "HID", k["gen"], 2 * k["j"]))
            mark(("split", "HID", k["gen"], 2 * k["j"] + 1), "hidden_rest")

        def pool_conv31(k):
            if k["by"] == "vector":
                return
            l, f, b = k["l"], k["f"], products[0] % 2
            pool.wait_ge(sems["act_products"], at("products", products[0]))
            pool.wait_ge(sems["act_conv"], at("conv0", l, f))
            for i in range(CONV_TAPS):
                pool.tensor_tensor(Y[:, f, :], Y[:, f, :], o_m["prod"][:, b, i, :],
                                   ALU.add).then_inc(sems["pool_conv"], 1)
                pool.wait_ge(sems["pool_conv"], up("pool_conv", ("products_used", products[0])))
            mark(("conv_by_pool", l), "pool_conv")
            products[0] += 1

        def pool_window(k):
            g = k["g"]
            u = o_m["pu"][:, 2 * g:2 * g + 2, :]
            pool.wait_ge(sems["vec_conv"], at("pool_in", k["l"], g))
            pool.wait_ge(sems["count_in"], at("cnt", k["l"]))
            src, base = u, 0
            for lev in range(g + 1):
                sh = 1 << lev
                dst = WIN[lev % 2]
                base += sh
                pool.tensor_tensor(dst[:, :, base:], src[:, :, base:], src[:, :, base - sh:-sh],
                                   ALU.add).then_inc(sems["pool_window"], 1)
                pool.wait_ge(sems["pool_window"], up("pool_window"))
                src = dst
            p = o_m["tmp2"][:, 2 * g:2 * g + 2, :]
            pool.tensor_tensor(p, src[:, :, POOL_PAD:], bc(o_m["cnt"][:, g, :]),
                               ALU.mult).then_inc(sems["pool_window"], 1)
            pool.wait_ge(sems["pool_window"], up("pool_window"))
            pool.tensor_tensor(p, p, u[:, :, POOL_PAD:], ALU.subtract).then_inc(sems["pool_window"], 1)
            pool.wait_ge(sems["pool_window"], up("pool_window", ("pooled", f"l{k['l']}", g)))

        def pool_mem_load(k):
            pool.wait_ge(sems["vec_split"], at(*k["after"]))
            pool.dma_start(o_c["memt"][:], a["mem_2"][0].rearrange("(t p) d -> p t d", p=P)).then_inc(sems["mem_in"], 16)
            up("mem_in", ("memt", k["l"]), by=16)

        parts = dict(setup=pool_setup, bias=pool_bias, hankel=pool_hankel, mem_load=pool_mem_load, hid_split=pool_hid_split, conv31=pool_conv31, window=pool_window, pads1=pool_blocks)
        for kind, k in steps:
            if kind in parts:
                parts[kind](k)

    ctx.close()



OUT_SHAPE = (1, T, D)


def shape_constants():
    import numpy as np

    def one_hot(max_distance, masked):
        d = 255 - np.arange(LINE)
        dist = np.maximum(d, 0)
        ratio = np.log(np.maximum(dist, 1).astype(np.float32) / np.float32(16)) / np.float32(math.log(max_distance / 16))
        large = np.minimum(16 + (ratio * np.float32(16)).astype(np.int32), 31)
        bucket = np.where(dist < 16, dist, large)
        o = np.zeros((33, LINE), np.float32)
        o[bucket, np.arange(LINE)] = 1.0
        o[32] = np.where(masked(d), NEG, 0.0)
        return o

    onehot = np.stack([one_hot(2048, lambda d: (d < 0) | (d >= 128)), one_hot(2048, lambda d: d < 0),
                       one_hot(128, lambda d: d < 0)], axis=1)
    heads = np.zeros((P, P), np.float32)
    heads[:HD, :HD] = heads[HD:, HD:] = 1.0
    t = np.arange(T)
    inv = np.stack([(1.0 / np.minimum(t + 1, w)).astype(np.float32) for w in (2, 4, 8, 16)])
    return {"ident": np.eye(P, dtype=np.float32), "flip": np.ascontiguousarray(np.eye(P, dtype=np.float32)[::-1]),
            "headsum": heads, "onehot": np.ascontiguousarray(onehot), "inv_count": inv}


def declare(nc, arrays):
    aps = {n: nc.dram_tensor(f"in_{n}_dram", v.shape, mybir.dt.from_np(v.dtype), kind="ExternalInput").ap()
           for n, v in arrays.items()}
    out = nc.dram_tensor("out_0_dram", OUT_SHAPE, F32, kind="ExternalOutput").ap()
    return aps, out, nc.dram_tensor("bias_lines", (3, 8, LINE), F32, kind="Internal").ap()


def kernel(**inputs):
    import numpy as np
    import concourse.bacc as bacc
    from concourse.bass_utils import run_bass_kernel_spmd

    arrays = {n: np.ascontiguousarray(v) for n, v in inputs.items()} | shape_constants()
    marks = {}
    for final in (False, True):
        nc = bacc.Bacc("TRN2", target_bir_lowering=False, num_devices=1)
        build(nc, *declare(nc, arrays), marks, final)
    r = run_bass_kernel_spmd(nc, [{f"in_{n}_dram": v for n, v in arrays.items()}], core_ids=[0])
    return r.results[0]["out_0_dram"]
```
